# Optimizing a Trainium2 kernel written in Bass

```python
import jax, jax.numpy as jnp
from jax import lax
import numpy as np

D_MODEL = 1024
BATCH = 1
SEQ = 256
DEPTH = 2

N_A_LAYERS = DEPTH // 2
N_B_LAYERS = DEPTH - N_A_LAYERS
CONV_WIDTH = 31
CONV_CH = D_MODEL
N_HEADS = 16
N_KV_GROUPS = 4
HEADS_PER_GROUP = N_HEADS // N_KV_GROUPS
HEAD_DIM = 64
CMP_LEN = 32
CMP_STRIDE = 16
SLC_LEN = 64
SLC_TOP_N = 16
WINDOW = 512
PHI_HIDDEN = 2 * HEAD_DIM
Q_BLOCK = 64
N_BRANCH = 3
N_EXPERTS = 16
N_EXPERT_GROUPS = 4
EXPERTS_PER_GROUP = N_EXPERTS // N_EXPERT_GROUPS
TOP_K = 2
D_EXPERT = 512
EPS = 1e-6
NEG_BIG = -1e30

kernel_name = "conv_nsa_yoco_moe_trunk"

def rmsnorm(x, g):
    xf = x.astype(jnp.float32)
    y = xf * lax.rsqrt(jnp.mean(xf * xf, axis=-1, keepdims=True) + EPS)
    return (y * g.astype(jnp.float32)).astype(x.dtype)

def masked_softmax(s, mask):
    s = jnp.where(mask, s.astype(jnp.float32), NEG_BIG)
    p = jax.nn.softmax(s, axis=-1)
    return jnp.where(jnp.any(mask, axis=-1, keepdims=True), p, 0.0)

def conformer_conv(h, w_in, dw, dw_bias, conv_norm, w_out):
    u = h @ w_in
    a, b = jnp.split(u, 2, axis=-1)
    u = a * jax.nn.sigmoid(b)
    u = lax.conv_general_dilated(
        u, dw[:, None, :], window_strides=(1,), padding=((CONV_WIDTH - 1, 0),),
        dimension_numbers=("NWC", "WIO", "NWC"), feature_group_count=CONV_CH) + dw_bias
    u = jax.nn.silu(rmsnorm(u, conv_norm))
    return u @ w_out

def nsa_shared_kv(x, kv_norm, w_kv, cmp_pe, phi_w1, phi_b1, phi_w2, k_norm):
    bsz, s, _ = x.shape
    g, dh = N_KV_GROUPS, HEAD_DIM
    kv = (rmsnorm(x, kv_norm) @ w_kv).reshape(bsz, s, 6, g, dh)
    k_c, v_c, k_s, v_s, k_w, v_w = [kv[:, :, i] for i in range(6)]
    n_cmp = (s - CMP_LEN) // CMP_STRIDE + 1
    idx = jnp.arange(n_cmp)[:, None] * CMP_STRIDE + jnp.arange(CMP_LEN)[None, :]

    def compress(t, pe, w1, b1, w2):
        blk = t[:, idx] + pe[None, None, :, None, :]
        blk = blk.transpose(0, 1, 3, 2, 4).reshape(bsz, n_cmp, g, CMP_LEN * dh)
        return jax.nn.gelu(blk @ w1 + b1) @ w2

    k_cmp = rmsnorm(compress(k_c, cmp_pe[0], phi_w1[0], phi_b1[0], phi_w2[0]), k_norm[0])
    v_cmp = compress(v_c, cmp_pe[1], phi_w1[1], phi_b1[1], phi_w2[1])
    k_s = rmsnorm(k_s, k_norm[1])
    k_w = rmsnorm(k_w, k_norm[2])
    n_slc = s // SLC_LEN
    k_sb = k_s.reshape(bsz, n_slc, SLC_LEN, g, dh).transpose(0, 3, 1, 2, 4)
    v_sb = v_s.reshape(bsz, n_slc, SLC_LEN, g, dh).transpose(0, 3, 1, 2, 4)
    pad = ((0, 0), (WINDOW, 0), (0, 0), (0, 0))
    k_wp = jnp.pad(k_w, pad)
    v_wp = jnp.pad(v_w, pad)
    return k_cmp, v_cmp, k_sb, v_sb, k_wp, v_wp

def nsa_attention(h, w_in, q_norm, w_out, shared):
    k_cmp, v_cmp, k_sb, v_sb, k_wp, v_wp = shared
    bsz, s, _ = h.shape
    g, r, dh = N_KV_GROUPS, HEADS_PER_GROUP, HEAD_DIM
    proj = h @ w_in
    q = rmsnorm(proj[..., :N_HEADS * dh].reshape(bsz, s, g, r, dh), q_norm) * (HEAD_DIM ** -0.5)
    gates = jax.nn.sigmoid(proj[..., N_HEADS * dh:].astype(jnp.float32))
    gates = gates.reshape(bsz, s, g, r, N_BRANCH).astype(h.dtype)
    n_cmp = k_cmp.shape[1]
    n_slc = k_sb.shape[2]
    top_n = min(SLC_TOP_N, n_slc)
    n_blk = s // Q_BLOCK
    cmp_end = jnp.arange(n_cmp) * CMP_STRIDE + CMP_LEN - 1
    ratio, span = SLC_LEN // CMP_STRIDE, CMP_LEN // CMP_STRIDE
    w_np = np.convolve(np.ones(ratio), np.ones(span)).astype(np.float32)
    offs = np.arange(ratio + span - 1) - (span - 1)
    m_idx = ratio * np.arange(n_slc)[:, None] + offs[None, :]
    m_ok = (m_idx >= 0) & (m_idx < n_cmp)
    map_w = jnp.asarray(np.where(m_ok, w_np[None, :], 0.0).astype(np.float32))
    map_idx = jnp.asarray(np.clip(m_idx, 0, n_cmp - 1).astype(np.int32))
    jb = jnp.arange(n_slc)
    gather = jax.vmap(jax.vmap(lambda kb, i: kb[i]))

    def block_fn(args):
        qb, gb, blk = args
        q0 = blk * Q_BLOCK
        t = q0 + jnp.arange(Q_BLOCK)
        s_c = jnp.einsum("bqgrd,bcgd->bgrqc", qb, k_cmp)
        p_c = masked_softmax(s_c, cmp_end[None, :] <= t[:, None])
        o_c = jnp.einsum("bgrqc,bcgd->bqgrd", p_c.astype(v_cmp.dtype), v_cmp)
        imp = (p_c.sum(axis=2)[..., map_idx] * map_w).sum(-1)
        cur = t // SLC_LEN
        forced = (jb[None, :] == 0) | (jb[None, :] == cur[:, None]) | (jb[None, :] == cur[:, None] - 1)
        imp = jnp.where(forced, jnp.inf, imp)
        imp = jnp.where(jb[None, :] > cur[:, None], -jnp.inf, imp)
        _, sel = lax.top_k(imp, top_n)
        k_sel = gather(k_sb, sel).reshape(bsz, g, Q_BLOCK, top_n * SLC_LEN, dh)
        v_sel = gather(v_sb, sel).reshape(bsz, g, Q_BLOCK, top_n * SLC_LEN, dh)
        pos_sel = (sel[..., None] * SLC_LEN + jnp.arange(SLC_LEN)).reshape(bsz, g, Q_BLOCK, top_n * SLC_LEN)
        s_s = jnp.einsum("bqgrd,bgqkd->bgrqk", qb, k_sel)
        p_s = masked_softmax(s_s, (pos_sel <= t[None, None, :, None])[:, :, None])
        o_s = jnp.einsum("bgrqk,bgqkd->bqgrd", p_s.astype(v_sel.dtype), v_sel)
        k_win = lax.dynamic_slice_in_dim(k_wp, q0, WINDOW + Q_BLOCK, axis=1)
        v_win = lax.dynamic_slice_in_dim(v_wp, q0, WINDOW + Q_BLOCK, axis=1)
        kpos = q0 - WINDOW + jnp.arange(WINDOW + Q_BLOCK)
        m_w = (kpos[None, :] <= t[:, None]) & (kpos[None, :] > t[:, None] - WINDOW) & (kpos[None, :] >= 0)
        s_w = jnp.einsum("bqgrd,bkgd->bgrqk", qb, k_win)
        p_w = masked_softmax(s_w, m_w)
        o_w = jnp.einsum("bgrqk,bkgd->bqgrd", p_w.astype(v_win.dtype), v_win)
        return gb[..., 0:1] * o_c + gb[..., 1:2] * o_s + gb[..., 2:3] * o_w

    qs = q.reshape(bsz, n_blk, Q_BLOCK, g, r, dh).swapaxes(0, 1)
    gs = gates.reshape(bsz, n_blk, Q_BLOCK, g, r, N_BRANCH).swapaxes(0, 1)
    o = lax.map(block_fn, (qs, gs, jnp.arange(n_blk)))
    o = o.swapaxes(0, 1).reshape(bsz, s, N_HEADS * dh)
    return o @ w_out

def moe_ffn(h, router_w, router_bias, w1, w3, w2):
    bsz, s, d = h.shape
    hf = h.reshape(-1, d)
    scores = jax.nn.sigmoid((hf @ router_w).astype(jnp.float32))
    biased = scores + router_bias.astype(jnp.float32)
    grp = biased.reshape(-1, N_EXPERT_GROUPS, EXPERTS_PER_GROUP)
    grp_score = lax.top_k(grp, TOP_K)[0].sum(-1)
    g_sel = jnp.argmax(grp_score, axis=-1)
    in_grp = (jnp.arange(N_EXPERTS) // EXPERTS_PER_GROUP)[None, :] == g_sel[:, None]
    _, top_idx = lax.top_k(jnp.where(in_grp, biased, -jnp.inf), TOP_K)
    top_w = jnp.take_along_axis(scores, top_idx, axis=-1)
    top_w = top_w / top_w.sum(-1, keepdims=True)
    gate = (jax.nn.one_hot(top_idx, N_EXPERTS, dtype=jnp.float32) * top_w[..., None]).sum(1).astype(h.dtype)
    out = jnp.zeros_like(hf)
    for e in range(N_EXPERTS):
        y = (jax.nn.silu(hf @ w1[e]) * (hf @ w3[e])) @ w2[e]
        out = out + gate[:, e:e + 1] * y
    return out.reshape(bsz, s, d)

def setup_inputs(seed: int = 0) -> dict:
    key = jax.random.key(seed)
    ks = jax.random.split(key, 32)
    nrm = jax.random.normal
    f32 = jnp.float32
    res = (2.0 * DEPTH) ** -0.5
    qg = N_HEADS * HEAD_DIM + N_BRANCH * N_HEADS
    return {
        "x": nrm(ks[0], (BATCH, SEQ, D_MODEL), f32),
        "a_norm": 1.0 + 0.01 * nrm(ks[1], (N_A_LAYERS, D_MODEL), f32),
        "a_w_in": nrm(ks[2], (N_A_LAYERS, D_MODEL, 2 * CONV_CH), f32) * D_MODEL ** -0.5,
        "a_dw": nrm(ks[3], (N_A_LAYERS, CONV_WIDTH, CONV_CH), f32) * CONV_WIDTH ** -0.5,
        "a_dw_bias": 0.01 * nrm(ks[4], (N_A_LAYERS, CONV_CH), f32),
        "a_conv_norm": 1.0 + 0.01 * nrm(ks[5], (N_A_LAYERS, CONV_CH), f32),
        "a_w_out": nrm(ks[6], (N_A_LAYERS, CONV_CH, D_MODEL), f32) * CONV_CH ** -0.5 * res,
        "kv_norm": 1.0 + 0.01 * nrm(ks[7], (D_MODEL,), f32),
        "w_kv": nrm(ks[8], (D_MODEL, 6 * N_KV_GROUPS * HEAD_DIM), f32) * D_MODEL ** -0.5,
        "cmp_pe": 0.1 * nrm(ks[9], (2, CMP_LEN, HEAD_DIM), f32),
        "phi_w1": nrm(ks[10], (2, CMP_LEN * HEAD_DIM, PHI_HIDDEN), f32) * (CMP_LEN * HEAD_DIM) ** -0.5,
        "phi_b1": 0.01 * nrm(ks[11], (2, PHI_HIDDEN), f32),
        "phi_w2": nrm(ks[12], (2, PHI_HIDDEN, HEAD_DIM), f32) * PHI_HIDDEN ** -0.5,
        "k_norm": 1.0 + 0.01 * nrm(ks[13], (N_BRANCH, HEAD_DIM), f32),
        "b_norm": 1.0 + 0.01 * nrm(ks[14], (N_B_LAYERS, D_MODEL), f32),
        "b_w_in": nrm(ks[15], (N_B_LAYERS, D_MODEL, qg), f32) * D_MODEL ** -0.5,
        "b_q_norm": 1.0 + 0.01 * nrm(ks[16], (N_B_LAYERS, HEAD_DIM), f32),
        "b_w_out": nrm(ks[17], (N_B_LAYERS, N_HEADS * HEAD_DIM, D_MODEL), f32) * (N_HEADS * HEAD_DIM) ** -0.5 * res,
        "ffn_norm": 1.0 + 0.01 * nrm(ks[18], (DEPTH, D_MODEL), f32),
        "router_w": nrm(ks[19], (D_MODEL, N_EXPERTS), f32) * D_MODEL ** -0.5,
        "router_bias": 0.01 * nrm(ks[20], (N_EXPERTS,), f32),
        "moe_w1": nrm(ks[21], (DEPTH, N_EXPERTS, D_MODEL, D_EXPERT), f32) * D_MODEL ** -0.5,
        "moe_w3": nrm(ks[22], (DEPTH, N_EXPERTS, D_MODEL, D_EXPERT), f32) * D_MODEL ** -0.5,
        "moe_w2": nrm(ks[23], (DEPTH, N_EXPERTS, D_EXPERT, D_MODEL), f32) * D_EXPERT ** -0.5 * res,
    }

def reference(x, a_norm, a_w_in, a_dw, a_dw_bias, a_conv_norm, a_w_out, kv_norm, w_kv, cmp_pe,
              phi_w1, phi_b1, phi_w2, k_norm, b_norm, b_w_in, b_q_norm, b_w_out, ffn_norm,
              router_w, router_bias, moe_w1, moe_w3, moe_w2):
    h = x
    shared = None
    for layer in range(DEPTH):
        if layer < N_A_LAYERS:
            i = layer
            h = h + conformer_conv(rmsnorm(h, a_norm[i]), a_w_in[i], a_dw[i], a_dw_bias[i],
                                   a_conv_norm[i], a_w_out[i])
        else:
            i = layer - N_A_LAYERS
            h = h + nsa_attention(rmsnorm(h, b_norm[i]), b_w_in[i], b_q_norm[i], b_w_out[i], shared)
        h = h + moe_ffn(rmsnorm(h, ffn_norm[layer]), router_w, router_bias,
                        moe_w1[layer], moe_w3[layer], moe_w2[layer])
        if layer == N_A_LAYERS - 1:
            shared = nsa_shared_kv(h, kv_norm, w_kv, cmp_pe, phi_w1, phi_b1, phi_w2, k_norm)
    return h


_drawn_inputs = setup_inputs


def setup_inputs(seed=0):
    import zlib

    import numpy as np

    out = dict(_drawn_inputs(seed))
    spreads = {}
    factors = {'a_norm': 3.574,
     'a_conv_norm': 8.0,
     'kv_norm': 7.67,
     'cmp_pe': 2.828,
     'phi_b1': 34.76,
     'k_norm': 7.781,
     'b_norm': 8.0,
     'b_q_norm': 8.0}
    for name, (base, spread) in spreads.items():
        noise = np.random.default_rng([zlib.crc32(name.encode()), seed]).standard_normal(out[name].shape)
        drawn = base * np.exp(spread * noise) if base else spread * noise
        out[name] = __import__('jax').numpy.asarray(drawn.astype(out[name].dtype))
    for name, factor in factors.items():
        out[name] = (out[name] * factor).astype(out[name].dtype)
    return out
```

```python
from contextlib import ExitStack

import concourse.bass as bass
from concourse import mybir

F32 = mybir.dt.float32
BF16 = mybir.dt.bfloat16
I32 = mybir.dt.int32
ALU = mybir.AluOpType
ACT = mybir.ActivationFunctionType
AX = mybir.AxisListType

P = 128
SEQ = 256
TC = SEQ // P
D = 1024
KC = D // P
TAPS = 31
HEADS, GROUPS, HPG, DH = 16, 4, 4, 64
CMP_LEN, CMP_STRIDE = 32, 16
NCMP = (SEQ - CMP_LEN) // CMP_STRIDE + 1
CPAD = 32
HID = 128
EXPERTS, EGROUPS, EPG = 16, 4, 4
DE = 512
FC = DE // P
EPS = 1e-6
NEG = -1e30
BANK = 512
UNIT = 4096
PRE = 2 * UNIT


class Sems:

    def __init__(self, nc, ctx):
        self.nc, self.ctx, self.taken = nc, ctx, []

    def __call__(self, name):
        s = self.ctx.enter_context(self.nc.semaphore(name))
        self.taken.append(s)
        return s

    def clear(self):
        nums = sorted(s.num for s in self.taken)
        first = [n for n in nums if n - 1 not in nums]
        last = [n for n in nums if n + 1 not in nums]
        with self.nc.Block() as block:
            @block.gpsimd
            def _(pool):
                for a, b in zip(first, last):
                    pool.sem_clear(range(a, b + 1))


class Link:

    def __init__(self, eng, sem):
        self.eng, self.sem, self.n = eng, sem, 0

    def __call__(self, ins):
        self.n += 1
        ins.then_inc(self.sem, 1)
        self.eng.wait_ge(self.sem, self.n)


class Mem:

    def __init__(self, nc, ctx):
        def sb(name, shape, dt=F32):
            return ctx.enter_context(nc.sbuf_tensor(name, shape, dt))

        self.ring = sb("ring", [P, 6, UNIT])
        self.arena = sb("arena", [P, 18944])
        self.h = sb("h", [P, TC, D])
        self.hn = sb("hn", [P, TC, D])
        self.hnT = sb("hnT", [P, KC, SEQ])
        self.gain = sb("gain", [P, D])
        self.ident = sb("ident", [P, P])
        self.ones = sb("ones", [P, P])
        self.before = sb("before", [P, P])
        self.iota = sb("iota", [P, P])
        self.identb = sb("identb", [P, P], BF16)
        self.causal = sb("causal", [P, P], BF16)
        self.cmask = sb("cmask", [P, TC, CPAD])
        self.cvalid = sb("cvalid", [P, TC])
        self.cols = sb("cols", [P, KC, TAPS + 2])
        self.cols2 = sb("cols2", [P, 38])
        self.stat = sb("stat", [P, 8])
        self.rw = sb("rw", [P, KC, EXPERTS])
        self.rb = sb("rb", [P, EXPERTS])
        self.wg = sb("wg", [P, KC, 3 * HEADS])
        self.phi2 = sb("phi2", [P, 2, DH])
        self.jgate = sb("jgate", [P, 5, EPG])
        self.rank = sb("rank", [P, TC])
        self.g4 = sb("g4", [P, TC, EPG])
        self.gates = sb("gates", [P, TC, 3 * HEADS])
        self.ovf = sb("ovf", [P, 2], I32)
        self.ps = ctx.enter_context(nc.psum_tensor("ps", [P, 8, BANK], F32))

    def at(self, start, *shape):
        n = 1
        for s in shape:
            n *= s
        v = self.arena[:, start:start + n]
        if len(shape) == 1:
            return v
        names = "abcd"[:len(shape)]
        return v.rearrange(f"p ({' '.join(names)}) -> p {' '.join(names)}",
                           **{k: s for k, s in zip(names, shape)})

    def unit(self, u):
        return self.ring[:, u, :].rearrange("p (k f) -> p k f", k=KC)


def w13(w, layer, e):
    return w[layer][bass.ds(e, 1)].rearrange("o (k p) f -> p (o k) f", p=P)


def load_w1(sp, M, T, layer, slot, e, s):
    sp.dma_start(M.unit(slot), w13(T["moe_w1"], layer, e)).then_inc(s.w1[slot], 16)


def load_w3(sp, M, T, layer, slot, e, s):
    sp.dma_start(M.unit(2 + slot), w13(T["moe_w3"], layer, e)).then_inc(s.w3[slot], 16)


def load_w2(sp, M, T, layer, slot, e, s):
    sp.dma_start(M.ring[:, 4 + slot, :].rearrange("p (k n) -> p k n", k=FC),
                 w13(T["moe_w2"], layer, e)).then_inc(s.w2[slot], 16)



class NormSems:
    def __init__(self, sem, gain, tag):
        self.sq, self.ms, self.sd, self.rs = (sem(f"{tag}_{n}") for n in ("sumsq", "meansq", "std", "rstd"))
        self.hn, self.tp = sem(f"{tag}_normed"), sem(f"{tag}_turned")
        self.ev = [sem(f"{tag}_hnT_act"), sem(f"{tag}_hnT_dve")]
        self.gain = gain


def norm_act(nc, act, M, s):
    for c in range(TC):
        nc.scalar.activation(M.hnT[:, 4 * c:4 * c + 4, :].rearrange("p k t -> p (k t)"), M.h[:, c, :], ACT.Square,
                             accum_out=M.stat[:, c:c + 1]).then_inc(s.sq, 1)
    act.wait_ge(s.ms, 1)
    nc.scalar.activation(M.stat[:, 4:6], M.stat[:, 2:4], ACT.Sqrt).then_inc(s.sd, 1)


def norm_dve(nc, dve, M, s):
    dve.wait_ge(s.sq, TC)
    nc.vector.tensor_scalar(M.stat[:, 2:4], M.stat[:, 0:2], 1.0 / D, EPS, ALU.mult, ALU.add).then_inc(s.ms, 1)
    dve.wait_ge(s.sd, 1)
    nc.vector.reciprocal(M.stat[:, 6:8], M.stat[:, 4:6]).then_inc(s.rs, 1)
    dve.wait_ge(s.rs, 1)
    dve.wait_ge(s.gain, 16)
    for c in range(TC):
        nc.vector.scalar_tensor_tensor(M.hn[:, c, :], M.h[:, c, :], M.stat[:, 6 + c:7 + c], M.gain[:, :],
                                       ALU.mult, ALU.mult).then_inc(s.hn, 1)


def turn_pe(pe, M, b, src):
    for kk in range(2):
        for c in range(TC):
            k = 2 * (b % 4) + kk
            mm = pe.transpose(M.ps[:, b % 8, kk * SEQ + c * P:kk * SEQ + (c + 1) * P],
                              src[:, c, k * P:(k + 1) * P], M.ident[:, :])
    return mm


def norm_pe(pe, M, s):
    pe.wait_ge(s.hn, TC)
    for b in range(4):
        turn_pe(pe, M, b, M.hn).then_inc(s.tp, 1)


def bank_pair(M, b):
    return M.ps[:, b, :].rearrange("p (k t) -> p k t", k=2)


def norm_evac(nc, eng, M, s, which):
    for b in range(which, 4, 2):
        eng.wait_ge(s.tp, b + 1)
        dst = M.hnT[:, 2 * b:2 * b + 2, :]
        if which == 0:
            nc.scalar.copy(dst, bank_pair(M, b)).then_inc(s.ev[0], 1)
        else:
            nc.vector.tensor_copy(dst, bank_pair(M, b)).then_inc(s.ev[1], 1)


def wait_hnT(eng, s):
    eng.wait_ge(s.ev[0], 2)
    eng.wait_ge(s.ev[1], 2)



def conv_phase(nc, M, T, sem, moe, pre, gains):
    U = M.at(PRE, KC, TAPS - 1 + SEQ)
    ACC = M.at(PRE + 2288, KC, SEQ)
    SIG = M.at(PRE + 4336, 2, SEQ)
    SQ = M.at(PRE + 4848, KC, SEQ)
    RSTD = M.at(PRE + 6896, 2, SEQ)
    ROWS = M.at(PRE + 7408, 1024)
    ROWS2 = M.at(PRE + 8432, P)
    WIN = M.ring[:, 0:4, :].rearrange("p u (k n) -> p (u k) n", k=2)
    WOUT = M.ring[:, 4:6, :].rearrange("p u (k n) -> p (u k) n", k=4)
    n = NormSems(sem, gains[0], "n0")
    s_x, s_rows, s_wout, s_small = sem("x_in"), sem("rows_in"), sem("wout_in"), sem("small_in")
    s_win = [sem(f"win_in{q}") for q in range(4)]
    s_const, s_pool = sem("constants"), sem("pool_chain")
    s_cols, s_colsT = sem("cols"), sem("colsT")
    s_mm, s_sig, s_glu = sem("glu_mm"), sem("glu_sig"), sem("glu_done")
    s_tap, s_sq, s_ssum = sem("taps"), sem("conv_sq"), sem("conv_ssum")
    s_ms, s_sd, s_rs, s_z, s_y = (sem(f"conv_{k}") for k in ("ms", "sd", "rs", "z", "y"))
    s_out, s_res = sem("conv_out"), sem("conv_res")

    with nc.Block() as block:
        @block.sync
        def _(sp):
            sp.dma_start(M.h[:], T["x"][0].rearrange("(c p) d -> p c d", p=P)).then_inc(s_x, 16)
            sp.dma_start(ROWS[0:TAPS, :], T["a_dw"][0]).then_inc(s_rows, 16)
            sp.dma_start(ROWS[TAPS:TAPS + 1, :], T["a_dw_bias"]).then_inc(s_rows, 16)
            sp.dma_start(ROWS[TAPS + 1:TAPS + 2, :], T["a_conv_norm"]).then_inc(s_rows, 16)
            sp.dma_start(M.gain[:], T["a_norm"][0].partition_broadcast(P)).then_inc(n.gain, 16)
            sp.dma_start(ROWS2[0:32, :], T["cmp_pe"].rearrange("i (j l) d -> (i j) (l d)", l=2)).then_inc(s_rows, 16)
            for half in range(2):
                cs = slice(half * DH, (half + 1) * DH)
                sp.dma_start(ROWS2[32:35, cs], T["k_norm"]).then_inc(s_rows, 16)
                sp.dma_start(ROWS2[35:36, cs], T["b_q_norm"]).then_inc(s_rows, 16)
            sp.dma_start(ROWS2[36:38, :], T["phi_b1"]).then_inc(s_rows, 16)
            wi = T["a_w_in"][0].rearrange("(k p) n -> p k n", p=P)
            for q in range(4):
                for ab in range(2):
                    c0 = ab * D + 256 * q
                    sp.dma_start(WIN[:, :, c0:c0 + 256], wi[:, :, c0:c0 + 256]).then_inc(s_win[q], 16)
            sp.dma_start(WOUT, T["a_w_out"][0].rearrange("(k p) n -> p k n", p=P)).then_inc(s_wout, 16)
            sp.dma_start(M.rw[:], T["router_w"].rearrange("(k p) e -> p k e", p=P)).then_inc(s_small, 16)
            sp.dma_start(M.rb[:], T["router_bias"].partition_broadcast(P)).then_inc(s_small, 16)
            sp.dma_start(M.wg[:], T["b_w_in"][0].rearrange("(k p) n -> p k n", p=P)[:, :, D:]).then_inc(s_small, 16)
            sp.dma_start(M.phi2[:], T["phi_w2"].rearrange("i h d -> h i d")).then_inc(s_small, 16)
            wkv = T["w_kv"].rearrange("(k p) n -> p k n", p=P)
            for b in range(2):
                sp.dma_start(M.at(b * UNIT, KC, 512), wkv[:, :, b * 512:(b + 1) * 512]).then_inc(pre[b], 16)
            sp.wait_ge(n.hn, TC)
            sp.dma_start(M.gain[:], T["ffn_norm"][0].partition_broadcast(P)).then_inc(gains[1], 16)
            sp.wait_ge(s_mm, KC)
            for slot in range(2):
                load_w1(sp, M, T, 0, slot, slot, moe)
                load_w3(sp, M, T, 0, slot, slot, moe)
            sp.wait_ge(s_out, 1)
            for slot in range(2):
                load_w2(sp, M, T, 0, slot, slot, moe)
            sp.wait_ge(s_small, 64)

        @block.gpsimd
        def _(pool):
            chain = Link(pool, s_pool)
            g = nc.gpsimd
            chain(g.memset(M.ones[:], 1.0))
            chain(g.affine_select(out=M.ident[:], in_=M.ones[:], pattern=[[-1, P]], compare_op=ALU.is_equal,
                                  fill=0.0, base=0, channel_multiplier=1))
            g.memset(U[:, :, 0:TAPS - 1], 0.0).then_inc(s_const, 1)
            chain(g.affine_select(out=M.before[:], in_=M.ones[:], pattern=[[1, P]], compare_op=ALU.is_ge,
                                  fill=0.0, base=-1, channel_multiplier=-1))
            chain(g.iota(M.iota[:], pattern=[[1, P]], base=0, channel_multiplier=0,
                         allow_small_or_imprecise_dtypes=True))
            chain(g.tensor_copy(M.identb[:], M.ident[:]))
            chain(g.memset(M.causal[:], 0.0))
            chain(g.memset(M.cmask[:], 0.0))
            chain(g.memset(M.cvalid[:], 1.0))
            chain(g.affine_select(out=M.causal[:], in_=M.causal[:], pattern=[[-1, P]], compare_op=ALU.is_ge,
                                  fill=NEG, base=0, channel_multiplier=1))
            for c in range(TC):
                end = c * P - (CMP_LEN - 1)
                chain(g.affine_select(out=M.cmask[:, c], in_=M.cmask[:, c], pattern=[[-CMP_STRIDE, CPAD]],
                                      compare_op=ALU.is_ge, fill=NEG, base=end, channel_multiplier=1))
                chain(g.affine_select(out=M.cvalid[:, c:c + 1], in_=M.cvalid[:, c:c + 1], pattern=[[0, 1]],
                                      compare_op=ALU.is_ge, fill=0.0, base=end, channel_multiplier=1))

        @block.scalar
        def _(act):
            act.wait_ge(s_x, 16)
            norm_act(nc, act, M, n)
            act.wait_ge(s_colsT, 1)
            nc.scalar.copy(M.cols[:], M.ps[:, 7, 0:KC * (TAPS + 2)].rearrange("p (k r) -> p k r", k=KC)
                           ).then_inc(s_cols, 1)
            nc.scalar.copy(M.cols2[:], M.ps[:, 6, 0:38]).then_inc(s_cols, 1)
            norm_evac(nc, act, M, n, 0)

            def square(c):
                act.wait_ge(s_tap, 2 * TAPS * (c // 2 + 1))
                nc.scalar.activation(SQ[:, c], ACC[:, c], ACT.Square).then_inc(s_sq, 1)

            for c in range(KC):
                act.wait_ge(s_mm, c + 1)
                if c >= 2:
                    act.wait_ge(s_glu, c - 1)
                nc.scalar.activation(SIG[:, c % 2], M.ps[:, 4 + c % 2, SEQ:], ACT.Sigmoid).then_inc(s_sig, 1)
                if c >= 4 and c % 2 == 1:
                    square(c - 5)
                    square(c - 4)
            for c in range(KC - 4, KC):
                square(c)
            act.wait_ge(s_ms, 1)
            nc.scalar.activation(RSTD[:, 1], RSTD[:, 0], ACT.Sqrt).then_inc(s_sd, 1)
            for c in range(KC):
                act.wait_ge(s_z, c // 4 + 1)
                nc.scalar.activation(SQ[:, c], SQ[:, c], ACT.Silu,
                                     scale=M.cols[:, c, TAPS + 1:TAPS + 2]).then_inc(s_y, 1)

        @block.vector
        def _(dve):
            norm_dve(nc, dve, M, n)
            norm_evac(nc, dve, M, n, 1)
            dve.wait_ge(s_cols, 1)
            dve.wait_ge(s_const, 1)
            done = 0
            for pair in range(KC // 2):
                for c in (2 * pair, 2 * pair + 1):
                    dve.wait_ge(s_sig, c + 1)
                    nc.vector.tensor_tensor(U[:, c, TAPS - 1:], M.ps[:, 4 + c % 2, 0:SEQ], SIG[:, c % 2],
                                            ALU.mult).then_inc(s_glu, 1)
                for tap in range(TAPS):
                    for c in (2 * pair, 2 * pair + 1):
                        w = M.cols[:, c, tap:tap + 1]
                        u = U[:, c, tap:tap + SEQ]
                        if tap == 0:
                            dve.wait_ge(s_glu, c + 1)
                            nc.vector.tensor_scalar(ACC[:, c], u, w, M.cols[:, c, TAPS:TAPS + 1], ALU.mult,
                                                    ALU.add).then_inc(s_tap, 1)
                        else:
                            dve.wait_ge(s_tap, done - 1)
                            nc.vector.scalar_tensor_tensor(ACC[:, c], u, w, ACC[:, c], ALU.mult,
                                                           ALU.add).then_inc(s_tap, 1)
                        done += 1
            dve.wait_ge(s_ssum, 1)
            nc.vector.tensor_scalar(RSTD[:, 0], M.ps[:, 6, 0:SEQ], 1.0 / D, EPS, ALU.mult, ALU.add).then_inc(s_ms, 1)
            dve.wait_ge(s_sd, 1)
            nc.vector.reciprocal(RSTD[:, 0], RSTD[:, 1]).then_inc(s_rs, 1)
            dve.wait_ge(s_rs, 1)
            dve.wait_ge(s_tap, TAPS * KC)
            for half in range(2):
                cs = slice(4 * half, 4 * half + 4)
                nc.vector.tensor_tensor(SQ[:, cs], ACC[:, cs], RSTD[:, 0].unsqueeze(1).to_broadcast([P, 4, SEQ]),
                                        ALU.mult).then_inc(s_z, 1)
            dve.wait_ge(s_out, 1)
            for i in range(4):
                hs = M.h[:, i // 2, (i % 2) * 512:(i % 2 + 1) * 512]
                nc.vector.tensor_tensor(hs, hs, M.ps[:, i, :], ALU.add).then_inc(s_res, 1)

        @block.tensor
        def _(pe):
            pe.wait_ge(s_pool, 2)
            pe.wait_ge(s_rows, 16 * 9)
            for k in range(KC):
                pe.transpose(M.ps[:, 7, k * (TAPS + 2):(k + 1) * (TAPS + 2)], ROWS[0:TAPS + 2, k * P:(k + 1) * P],
                             M.ident[0:TAPS + 2, 0:TAPS + 2])
            pe.transpose(M.ps[:, 6, 0:38], ROWS2[0:38, :], M.ident[0:38, 0:38]).then_inc(s_colsT, 1)
            norm_pe(pe, M, n)
            wait_hnT(pe, n)
            for c in range(KC):
                if c % 2 == 0:
                    pe.wait_ge(s_win[c // 2], 32)
                if c >= 2:
                    pe.wait_ge(s_glu, c - 1)
                for ab in range(2):
                    for k in range(KC):
                        mm = pe.matmul(M.ps[:, 4 + c % 2, ab * SEQ:(ab + 1) * SEQ],
                                       WIN[:, k, ab * D + c * P:ab * D + (c + 1) * P], M.hnT[:, k, :],
                                       start=(k == 0), stop=(k == KC - 1))
                mm.then_inc(s_mm, 1)
            pe.wait_ge(s_cols, 2)
            for c in range(KC):
                pe.wait_ge(s_sq, c + 1)
                mm = pe.matmul(M.ps[:, 6, 0:SEQ], M.ones[:], SQ[:, c], start=(c == 0), stop=(c == KC - 1))
            mm.then_inc(s_ssum, 1)
            pe.wait_ge(s_wout, 16)
            for k in range(KC):
                pe.wait_ge(s_y, k + 1)
                for i in range(4):
                    mm = pe.matmul(M.ps[:, i, :], SQ[:, k, (i // 2) * P:(i // 2 + 1) * P],
                                   WOUT[:, k, (i % 2) * 512:(i % 2 + 1) * 512], start=(k == 0), stop=(k == KC - 1))
            mm.then_inc(s_out, 1)



class Landed:

    def __init__(self, sem, tag):
        self.w1 = [sem(f"{tag}_w1_in{i}") for i in range(2)]
        self.w3 = [sem(f"{tag}_w3_in{i}") for i in range(2)]
        self.w2 = [sem(f"{tag}_w2_in{i}") for i in range(2)]


class MoeSems:

    def __init__(self, sem, landed, tag):
        self.w1, self.w3, self.w2 = landed.w1, landed.w3, landed.w2
        self.g_done, self.u_done = sem(f"{tag}_g_done"), sem(f"{tag}_u_done")
        self.silu = sem(f"{tag}_silu")
        self.gu = sem(f"{tag}_gu_free")
        self.turned = sem(f"{tag}_turned_free")
        self.guT = sem(f"{tag}_guT_free")
        self.y_mm = sem(f"{tag}_y_free")
        self.y_out = sem(f"{tag}_yout_free")
        self.gather = sem(f"{tag}_gather")
        self.xg = sem(f"{tag}_xg")
        self.scat, self.res = sem(f"{tag}_scatter"), sem(f"{tag}_residual")


def moe_views(M):
    class V:
        XG = M.at(PRE, KC, P)
        Y = M.at(PRE + 1024, EGROUPS, D)
        S = M.at(PRE + 5120, EGROUPS, TC, P)
        ST = M.at(PRE + 6144, EGROUPS, SEQ)
        SIL = M.at(PRE + 7168, 2, DE)
        GU = M.at(PRE + 8192, 2, DE)
        GUT = M.at(PRE + 9216, 2, FC, P)
    return V


def route_phase(nc, M, T, sem, layer, gain, next_gain, next_landed):
    n = NormSems(sem, gain, f"n{layer}")
    V = moe_views(M)
    t = f"r{layer}"
    s_lg, s_sc, s_ch, s_gm, s_rk, s_S, s_St, s_Ste, s_jg = (
        sem(f"{t}_{k}") for k in ("logits", "scores", "chain", "gm", "rank", "S", "S_turned", "ST", "jobgate"))
    tmp = V.SIL.rearrange("p a b -> p (a b)")
    names = {}
    off = [0]

    def small(name, *shape):
        k = 1
        for x in shape:
            k *= x
        v = tmp[:, off[0]:off[0] + k]
        off[0] += k
        if len(shape) == 2:
            v = v.rearrange("p (a b) -> p a b", a=shape[0])
        if len(shape) == 3:
            v = v.rearrange("p (a b c) -> p a b c", a=shape[0], b=shape[1])
        names[name] = v
        return v

    CG = TC * EGROUPS
    score, biased, mb, oh1, oh2, cand = (small(x, TC, EXPERTS) for x in ("score", "biased", "mb", "oh1", "oh2", "cand"))
    hi, lo = small("hi", CG, 2), small("lo", CG, 2)
    top, mn, ml, gs, off1 = (small(x, CG) for x in ("top", "mn", "ml", "gs", "off1"))
    gm, gcand, gr = (small(x, TC, EGROUPS) for x in ("gm", "gcand", "gr"))
    m2 = small("m2", 8, TC)
    cnt, cnt2, of = small("cnt", EGROUPS), small("cnt2", EGROUPS), small("of", 2)

    with nc.Block() as block:
        @block.sync
        def _(sp):
            sp.wait_ge(n.hn, TC)
            if next_gain is not None:
                sp.dma_start(M.gain[:], next_gain.partition_broadcast(P)).then_inc(next_landed, 16)

        @block.scalar
        def _(act):
            norm_act(nc, act, M, n)
            norm_evac(nc, act, M, n, 0)
            act.wait_ge(s_lg, 1)
            nc.scalar.activation(score, M.ps[:, 4, 0:TC * EXPERTS].rearrange("p (c e) -> p c e", c=TC),
                                 ACT.Sigmoid).then_inc(s_sc, 1)
            act.wait_ge(s_St, 2)
            nc.scalar.copy(V.ST[:, 0:2], M.ps[:, 0, :].rearrange("p (j t) -> p j t", j=2)).then_inc(s_Ste, 1)
            act.wait_ge(s_jg, 1)
            nc.scalar.copy(M.jgate[:, 0:EGROUPS], M.ps[:, 6, 0:16].rearrange("p (j e) -> p j e", j=EGROUPS)
                           ).then_inc(s_jg, 1)

        @block.vector
        def _(dve):
            norm_dve(nc, dve, M, n)
            norm_evac(nc, dve, M, n, 1)
            v = nc.vector
            ln = Link(dve, s_ch)
            dve.wait_ge(s_sc, 1)
            ln(v.tensor_tensor(biased, score, M.rb[:].unsqueeze(1).to_broadcast([P, TC, EXPERTS]), ALU.add))
            b4 = biased.rearrange("p c (g k) -> p (c g) k", k=EPG)
            v.tensor_tensor(hi, b4[:, :, 0:2], b4[:, :, 2:4], ALU.max).then_inc(s_ch, 1)
            ln.n += 1
            ln(v.tensor_tensor(lo, b4[:, :, 0:2], b4[:, :, 2:4], ALU.min))
            v.tensor_tensor(top, hi[:, :, 0], hi[:, :, 1], ALU.max).then_inc(s_ch, 1)
            v.tensor_tensor(mn, hi[:, :, 0], hi[:, :, 1], ALU.min).then_inc(s_ch, 1)
            ln.n += 2
            ln(v.tensor_tensor(ml, lo[:, :, 0], lo[:, :, 1], ALU.max))
            ln(v.tensor_tensor(mn, mn, ml, ALU.max))
            ln(v.tensor_tensor(gs, top, mn, ALU.add))

            def first_max(values, n_val, m, one_hot, cnd):
                ln(v.tensor_reduce(m[:, 0], values, AX.X, ALU.max))
                ln(v.tensor_tensor(cnd, values, m[:, 0].unsqueeze(2).to_broadcast([P, TC, n_val]), ALU.is_equal))
                ln(v.scalar_tensor_tensor(cnd, cnd, -64.0, M.iota[:, 0:n_val].unsqueeze(1).to_broadcast(
                    [P, TC, n_val]), ALU.mult, ALU.add))
                ln(v.tensor_reduce(m[:, 1], cnd, AX.X, ALU.min))
                ln(v.tensor_tensor(one_hot, cnd, m[:, 1].unsqueeze(2).to_broadcast([P, TC, n_val]), ALU.is_equal))

            first_max(gs.rearrange("p (c g) -> p c g", c=TC), EGROUPS, m2[:, 0:2], gm, gcand)
            dve.sem_inc(s_gm, 1)
            gmf = gm.rearrange("p c g -> p (c g)")
            ln(v.tensor_scalar(off1, gmf, -1.0, -NEG, ALU.add, ALU.mult))
            mb4 = mb.rearrange("p c (g k) -> p (c g) k", k=EPG)
            ln(v.tensor_tensor(mb4, b4, gmf.unsqueeze(2).to_broadcast([P, CG, EPG]), ALU.mult))
            ln(v.tensor_tensor(mb4, mb4, off1.unsqueeze(2).to_broadcast([P, CG, EPG]), ALU.add))
            first_max(mb, EXPERTS, m2[:, 2:4], oh1, cand)
            ln(v.scalar_tensor_tensor(mb, oh1, 2 * NEG, mb, ALU.mult, ALU.add))
            first_max(mb, EXPERTS, m2[:, 4:6], oh2, cand)
            ln(v.tensor_tensor(oh1, oh1, oh2, ALU.add))
            ln(v.tensor_tensor(score, score, oh1, ALU.mult))
            ln(v.tensor_reduce(m2[:, 6], score, AX.X, ALU.add))
            ln(v.reciprocal(m2[:, 7], m2[:, 6]))
            ln(v.tensor_tensor(score, score, m2[:, 7].unsqueeze(2).to_broadcast([P, TC, EXPERTS]), ALU.mult))
            for c in range(TC):
                ln(v.tensor_reduce(M.g4[:, c], score[:, c].rearrange("p (g k) -> p k g", k=EPG), AX.X, ALU.add))
            dve.wait_ge(s_rk, 1)
            rk = M.ps[:, 5, 0:CG].rearrange("p (c g) -> p c g", c=TC)
            ln(v.tensor_tensor(gr, gm, rk, ALU.mult))
            ln(v.tensor_reduce(M.rank[:], gr, AX.X, ALU.add))
            for j in range(EGROUPS):
                for c in range(TC):
                    i = v.tensor_scalar(V.S[:, j, c], M.iota[:], M.rank[:, c:c + 1], gm[:, c, j:j + 1], ALU.is_equal,
                                        ALU.mult)
                i.then_inc(s_S, 1)
            ln(v.tensor_scalar(cnt, M.ps[:, 5, CG:CG + EGROUPS], float(P), None, ALU.is_gt))
            ln(v.tensor_tensor(cnt2, cnt, M.iota[:, 0:EGROUPS], ALU.mult))
            ln(v.tensor_reduce(of[:, 0:1], cnt, AX.X, ALU.add))
            ln(v.tensor_reduce(of[:, 1:2], cnt2, AX.X, ALU.add))
            ln(v.tensor_copy(M.ovf[:], of))
            dve.wait_ge(s_St, 4)
            v.tensor_copy(V.ST[:, 2:4], M.ps[:, 1, :].rearrange("p (j t) -> p j t", j=2)).then_inc(s_Ste, 1)

        @block.tensor
        def _(pe):
            norm_pe(pe, M, n)
            wait_hnT(pe, n)
            for c in range(TC):
                for k in range(KC):
                    mm = pe.matmul(M.ps[:, 4, c * EXPERTS:(c + 1) * EXPERTS], M.hnT[:, k, c * P:(c + 1) * P],
                                   M.rw[:, k, :], start=(k == 0), stop=(k == KC - 1))
            mm.then_inc(s_lg, 1)
            pe.wait_ge(s_gm, 1)
            B = M.ps[:, 5, :]
            pe.matmul(B[:, 0:4], M.before[:], gm[:, 0], start=True, stop=True)
            pe.matmul(B[:, 4:8], M.ones[:], gm[:, 0], start=True, stop=False)
            pe.matmul(B[:, 4:8], M.before[:], gm[:, 1], start=False, stop=True)
            pe.matmul(B[:, 8:12], M.ones[:], gm[:, 0], start=True, stop=False)
            pe.matmul(B[:, 8:12], M.ones[:], gm[:, 1], start=False, stop=True).then_inc(s_rk, 1)
            for j in range(EGROUPS):
                pe.wait_ge(s_S, j + 1)
                for c in range(TC):
                    mm = pe.transpose(M.ps[:, j // 2, (j % 2) * SEQ + c * P:(j % 2) * SEQ + (c + 1) * P],
                                      V.S[:, j, c], M.ident[:])
                mm.then_inc(s_St, 1)
            for j in range(EGROUPS):
                for c in range(TC):
                    mm = pe.matmul(M.ps[:, 6, j * EPG:(j + 1) * EPG], V.S[:, j, c], M.g4[:, c], start=(c == 0),
                                   stop=(c == TC - 1))
            mm.then_inc(s_jg, 1)


G_BANK, U_BANK, Y_BANK, T_BANK = 0, 2, 4, 6


def pe_gather(pe, M, V, j, half, s, src):
    bank = (G_BANK, U_BANK)[half]
    for k in range(4):
        col = (4 * half + k) * P
        for c in range(TC):
            mm = pe.matmul(M.ps[:, bank, k * P:(k + 1) * P], M.hn[:, c, col:col + P], src(j, c),
                           start=(c == 0), stop=(c == TC - 1))
    mm.then_inc(s.gather, 1)


def pe_job(pe, M, V, j, s, src, more):
    def g(e):
        E = 4 * j + e
        pe.wait_ge(s.w1[e % 2], (2 * j + e // 2) * 16 + 16)
        pe.wait_ge(s.gu, E + 1)
        for k in range(KC):
            mm = pe.matmul(M.ps[:, G_BANK + e % 2, :], V.XG[:, k], M.unit(e % 2)[:, k, :], start=(k == 0),
                           stop=(k == KC - 1))
        mm.then_inc(s.g_done, 1)

    def u(e):
        pe.wait_ge(s.w3[e % 2], (2 * j + e // 2) * 16 + 16)
        for k in range(KC):
            mm = pe.matmul(M.ps[:, U_BANK + e % 2, :], V.XG[:, k], M.unit(2 + e % 2)[:, k, :], start=(k == 0),
                           stop=(k == KC - 1))
        mm.then_inc(s.u_done, 1)

    def turn(e):
        E = 4 * j + e
        pe.wait_ge(s.gu, E + 3)
        pe.wait_ge(s.guT, E + 1)
        for k in range(FC):
            mm = pe.transpose(M.ps[:, T_BANK, k * P:(k + 1) * P], V.GU[:, e % 2, k * P:(k + 1) * P], M.ident[:])
        mm.then_inc(s.turned, 1)

    def y(e):
        E = 4 * j + e
        pe.wait_ge(s.guT, E + 2)
        pe.wait_ge(s.w2[e % 2], (2 * j + e // 2) * 16 + 16)
        if e == 0:
            pe.wait_ge(s.y_out, j * 2 + 2)
        w2 = M.ring[:, 4 + e % 2, :].rearrange("p (k n) -> p k n", k=FC)
        for k in range(FC):
            for n in range(2):
                mm = pe.matmul(M.ps[:, Y_BANK + n, :], V.GUT[:, e % 2, k], w2[:, k, n * 512:(n + 1) * 512],
                               start=(e == 0 and k == 0), stop=(e == EPG - 1 and k == FC - 1))
        mm.then_inc(s.y_mm, 1)

    pe.wait_ge(s.xg, j * 2 + 2)
    g(0)
    u(0)
    for e in range(1, EPG):
        g(e)
        turn(e - 1)
        u(e)
        y(e - 1)
    if more:
        pe.wait_ge(s.gu, 4 * j + 5)
        pe_gather(pe, M, V, j + 1, 0, s, src)
    turn(EPG - 1)
    if more:
        pe_gather(pe, M, V, j + 1, 1, s, src)
    y(EPG - 1)


def act_take_gather(nc, act, M, V, j, s):
    act.wait_ge(s.gather, j * 2 + 1)
    nc.scalar.copy(V.XG[:, 0:4], M.ps[:, G_BANK, :].rearrange("p (k t) -> p k t", k=4)).then_inc(s.xg, 1)


def dve_take_gather(nc, dve, M, V, j, s):
    dve.wait_ge(s.gather, j * 2 + 2)
    nc.vector.tensor_copy(V.XG[:, 4:8], M.ps[:, U_BANK, :].rearrange("p (k t) -> p k t", k=4)).then_inc(s.xg, 1)


def act_job(nc, act, M, V, j, s, ydst, more):
    def silu(e):
        act.wait_ge(s.g_done, 4 * j + e + 1)
        act.wait_ge(s.gu, 4 * j + e + 1)
        nc.scalar.activation(V.SIL[:, e % 2], M.ps[:, G_BANK + e % 2, :], ACT.Silu).then_inc(s.silu, 1)

    def take_turned(e):
        act.wait_ge(s.turned, 4 * j + e + 3)
        act.wait_ge(s.y_mm, 4 * j + e + 1)
        nc.scalar.copy(V.GUT[:, e % 2], M.ps[:, T_BANK, :].rearrange("p (k t) -> p k t", k=FC)).then_inc(s.guT, 1)

    silu(0)
    for e in range(1, EPG):
        silu(e)
        take_turned(e - 1)
    if more:
        act.wait_ge(s.u_done, 4 * j + 4)
        act_take_gather(nc, act, M, V, j + 1, s)
    take_turned(EPG - 1)
    act.wait_ge(s.y_mm, 4 * j + 6)
    nc.scalar.copy(ydst(j)[:, 0:512], M.ps[:, Y_BANK, :]).then_inc(s.y_out, 1)


def dve_job(nc, dve, M, V, j, s, gate, ydst, more):
    for e in range(EPG):
        E = 4 * j + e
        dve.wait_ge(s.silu, E + 1)
        dve.wait_ge(s.u_done, E + 1)
        dve.wait_ge(s.turned, E + 1)
        nc.vector.scalar_tensor_tensor(V.GU[:, e % 2], M.ps[:, U_BANK + e % 2, :], gate(j, e), V.SIL[:, e % 2],
                                       ALU.mult, ALU.mult).then_inc(s.gu, 1)
    if more:
        dve_take_gather(nc, dve, M, V, j + 1, s)
    dve.wait_ge(s.y_mm, 4 * j + 6)
    nc.vector.tensor_copy(ydst(j)[:, 512:1024], M.ps[:, Y_BANK + 1, :]).then_inc(s.y_out, 1)


def credits(eng, *pairs):
    for s, n in pairs:
        eng.sem_inc(s, n)


def jobs_phase(nc, M, T, sem, layer, landed, tail_loads):
    s = MoeSems(sem, landed, f"m{layer}")
    V = moe_views(M)
    JL = EGROUPS - 1

    def src(j, c):
        if isinstance(j, int):
            return V.S[:, j, c]
        return V.S[:, bass.ds(j, 1), c].rearrange("p o t -> p (o t)")

    def gate(j, e):
        g = M.jgate[:].rearrange("p j e -> p (j e)")
        return g[:, 4 * j + e:4 * j + e + 1] if isinstance(j, int) else g[:, bass.ds(j * 4 + e, 1)]

    def ydst(j):
        return V.Y[:, j] if isinstance(j, int) else V.Y[:, bass.ds(j, 1)].rearrange("p o d -> p (o d)")

    with nc.Block() as block:
        @block.sync
        def _(sp):
            def load(j, e):
                sp.wait_ge(s.g_done, 4 * j + e + 1)
                load_w1(sp, M, T, layer, e % 2, 4 * j + e + 2, s)
                sp.wait_ge(s.u_done, 4 * j + e + 1)
                load_w3(sp, M, T, layer, e % 2, 4 * j + e + 2, s)
                sp.wait_ge(s.y_mm, 4 * j + e + 3)
                load_w2(sp, M, T, layer, e % 2, 4 * j + e + 2, s)

            with sp.Fori(0, JL) as j:
                for e in range(EPG):
                    load(j, e)
            for e in range(2):
                load(JL, e)
            if tail_loads is not None:
                sp.wait_ge(s.y_mm, EXPERTS + 2)
                tail_loads(sp)

        @block.tensor
        def _(pe):
            credits(pe, (s.turned, 2), (s.y_mm, 2))
            pe_gather(pe, M, V, 0, 0, s, src)
            pe_gather(pe, M, V, 0, 1, s, src)
            with pe.Fori(0, JL) as j:
                pe_job(pe, M, V, j, s, src, True)
            pe_job(pe, M, V, JL, s, src, False)
            pe.wait_ge(s.gu, EXPERTS + 2)
            pe.wait_ge(s.y_out, 2 * EGROUPS + 2)
            for i in range(4):
                for j in range(EGROUPS):
                    mm = pe.matmul(M.ps[:, i, :], V.ST[:, j, (i // 2) * P:(i // 2 + 1) * P],
                                   V.Y[:, j, (i % 2) * 512:(i % 2 + 1) * 512], start=(j == 0),
                                   stop=(j == EGROUPS - 1))
                mm.then_inc(s.scat, 1)

        @block.scalar
        def _(act):
            credits(act, (s.guT, 1))
            act_take_gather(nc, act, M, V, 0, s)
            with act.Fori(0, JL) as j:
                act_job(nc, act, M, V, j, s, ydst, True)
            act_job(nc, act, M, V, JL, s, ydst, False)

        @block.vector
        def _(dve):
            credits(dve, (s.gu, 2), (s.y_out, 2))
            dve_take_gather(nc, dve, M, V, 0, s)
            with dve.Fori(0, JL) as j:
                dve_job(nc, dve, M, V, j, s, gate, ydst, True)
            dve_job(nc, dve, M, V, JL, s, gate, ydst, False)
            for i in range(4):
                dve.wait_ge(s.scat, i + 1)
                hs = M.h[:, i // 2, (i % 2) * 512:(i % 2 + 1) * 512]
                nc.vector.tensor_tensor(hs, hs, M.ps[:, i, :], ALU.add).then_inc(s.res, 1)


def overflow_phase(nc, M, T, sem, layer, landed, after):
    V = moe_views(M)
    t = f"o{layer}"
    s = MoeSems(sem, landed, f"v{layer}")
    s_S, s_St, s_prep, s_ge = sem(f"{t}_S"), sem(f"{t}_ST"), sem(f"{t}_prep"), sem(f"{t}_gate")
    group_max = EGROUPS - 1

    def src(j, c):
        return V.S[:, 0, c]

    def gate(j, e):
        return M.jgate[:, 4, e:e + 1]

    def ydst(j):
        return V.Y[:, 0]

    def when(eng, body):
        n = eng.value_load(M.ovf[0:1, 0:1], min_val=0, max_val=1)
        with eng.If(n > 0):
            body(eng)
        eng.end_ifs()

    with nc.Block() as block:
        @block.sync
        def _(sp):
            g = sp.value_load(M.ovf[0:1, 1:2], min_val=0, max_val=group_max)

            def body(sp):
                if after is not None:
                    after[0](sp)
                for e in range(2):
                    load_w1(sp, M, T, layer, e, g * EPG + e, s)
                    load_w3(sp, M, T, layer, e, g * EPG + e, s)
                    load_w2(sp, M, T, layer, e, g * EPG + e, s)
                for e in range(2):
                    sp.wait_ge(s.g_done, e + 1)
                    load_w1(sp, M, T, layer, e, g * EPG + e + 2, s)
                    sp.wait_ge(s.u_done, e + 1)
                    load_w3(sp, M, T, layer, e, g * EPG + e + 2, s)
                    sp.wait_ge(s.y_mm, e + 3)
                    load_w2(sp, M, T, layer, e, g * EPG + e + 2, s)
                if after is not None:
                    sp.wait_ge(s.y_mm, EPG + 2)
                    after[1](sp)

            when(sp, body)

        @block.tensor
        def _(pe):
            def body(pe):
                credits(pe, (s.turned, 2), (s.y_mm, 2))
                pe.wait_ge(s_S, TC)
                for c in range(TC):
                    pe.transpose(M.ps[:, T_BANK, c * P:(c + 1) * P], V.S[:, 0, c], M.ident[:])
                for c in range(TC):
                    mm = pe.matmul(M.ps[:, 7, 0:EPG], V.S[:, 0, c], M.g4[:, c], start=(c == 0), stop=(c == TC - 1))
                mm.then_inc(s_St, 1)
                pe_gather(pe, M, V, 0, 0, s, src)
                pe_gather(pe, M, V, 0, 1, s, src)
                pe.wait_ge(s_prep, 2)
                pe_job(pe, M, V, 0, s, src, False)
                pe.wait_ge(s.gu, EPG + 2)
                pe.wait_ge(s.y_out, 4)
                for i in range(4):
                    pe.matmul(M.ps[:, i, :], V.ST[:, 0, (i // 2) * P:(i // 2 + 1) * P],
                              V.Y[:, 0, (i % 2) * 512:(i % 2 + 1) * 512], start=True, stop=True).then_inc(s.scat, 1)

            when(pe, body)

        @block.scalar
        def _(act):
            def body(act):
                credits(act, (s.guT, 1))
                act.wait_ge(s_St, 1)
                nc.scalar.copy(V.ST[:, 0], M.ps[:, T_BANK, 0:SEQ]).then_inc(s_prep, 1)
                nc.scalar.copy(M.jgate[:, 4], M.ps[:, 7, 0:EPG]).then_inc(s_prep, 1)
                act_take_gather(nc, act, M, V, 0, s)
                act_job(nc, act, M, V, 0, s, ydst, False)

            when(act, body)

        @block.vector
        def _(dve):
            def body(dve):
                credits(dve, (s.gu, 2), (s.y_out, 2))
                nc.vector.tensor_scalar(M.stat[:, 0:TC], M.rank[:], float(-P), None, ALU.add).then_inc(s_ge, 1)
                dve.wait_ge(s_ge, 1)
                for c in range(TC):
                    nc.vector.tensor_scalar(V.S[:, 0, c], M.iota[:], M.stat[:, c:c + 1], None,
                                            ALU.is_equal).then_inc(s_S, 1)
                dve_take_gather(nc, dve, M, V, 0, s)
                dve.wait_ge(s_prep, 2)
                dve_job(nc, dve, M, V, 0, s, gate, ydst, False)
                for i in range(4):
                    dve.wait_ge(s.scat, i + 1)
                    hs = M.h[:, i // 2, (i % 2) * 512:(i % 2 + 1) * 512]
                    nc.vector.tensor_tensor(hs, hs, M.ps[:, i, :], ALU.add).then_inc(s.res, 1)

            when(dve, body)



KV = PRE
Q = PRE + 3072
HNB = PRE + 5120
HNBT = PRE + 7168
GAIN2 = PRE + 9216


def attention_loads(sp, M, T, into):
    sp.dma_start(M.unit(0), T["w_kv"].rearrange("(k p) n -> p k n", p=P)[:, :, 1024:1536]).then_inc(into[0], 16)
    wi = T["b_w_in"][0].rearrange("(k p) n -> p k n", p=P)
    for b in range(2):
        sp.dma_start(M.unit(1 + b), wi[:, :, b * 512:(b + 1) * 512]).then_inc(into[1 + b], 16)
    sp.dma_start(M.ring[:, 3, :].rearrange("p (i j f) -> p i j f", i=2, j=16),
                 T["phi_w1"].rearrange("i (j p) f -> p i j f", p=P)).then_inc(into[3], 16)
    sp.dma_start(M.ring[:, 4:6, :].rearrange("p u (k n) -> p (u k) n", k=4),
                 T["b_w_out"][0].rearrange("(k p) n -> p k n", p=P)).then_inc(into[4], 16)


def project_phase(nc, M, T, sem, gain, loaded, loaded01):
    n = NormSems(sem, gain, "np")
    s_g2, s_mm = sem("gain2_in"), sem("proj_mm")
    s_ev = [sem("proj_act"), sem("proj_dve")]
    kv = M.at(KV, TC, 3, 512)
    q = M.at(Q, TC, 2, 512)
    hnb, hnbT = M.at(HNB, TC, D), M.at(HNBT, KC, SEQ)
    W = [M.at(b * UNIT, KC, 512) for b in range(2)] + [M.unit(0), M.unit(1), M.unit(2)]
    items = [("turn", b, hnT_part(M.hnT, b)) for b in range(4)] + [("turnb", b, hnT_part(hnbT, b)) for b in range(4)]
    items += [("kv", (b, c), kv[:, c, b]) for b in range(3) for c in range(TC)]
    items += [("q", (b, c), q[:, c, b]) for b in range(2) for c in range(TC)]
    items += [("gates", None, M.gates[:])]

    def source(i):
        kind = items[i][0]
        if kind in ("turn", "turnb"):
            return bank_pair(M, i % 8)
        if kind == "gates":
            return M.ps[:, i % 8, 0:TC * 3 * HEADS].rearrange("p (c n) -> p c n", c=TC)
        return M.ps[:, i % 8, :]

    def wait_item(eng, i):
        eng.wait_ge(s_ev[i % 2], i // 2 + 1)

    with nc.Block() as block:
        @block.sync
        def _(sp):
            sp.dma_start(M.at(GAIN2, D), T["b_norm"][0].partition_broadcast(P)).then_inc(s_g2, 16)

        @block.scalar
        def _(act):
            norm_act(nc, act, M, n)
            for i in range(0, len(items), 2):
                act.wait_ge(s_mm, i + 1)
                if items[i][0] == "gates":
                    nc.scalar.activation(items[i][2], source(i), ACT.Sigmoid).then_inc(s_ev[0], 1)
                else:
                    nc.scalar.copy(items[i][2], source(i)).then_inc(s_ev[0], 1)

        @block.vector
        def _(dve):
            norm_dve(nc, dve, M, n)
            dve.wait_ge(s_g2, 16)
            for c in range(TC):
                nc.vector.scalar_tensor_tensor(hnb[:, c, :], M.h[:, c, :], M.stat[:, 6 + c:7 + c], M.at(GAIN2, D),
                                               ALU.mult, ALU.mult).then_inc(n.hn, 1)
            for i in range(1, len(items), 2):
                dve.wait_ge(s_mm, i + 1)
                nc.vector.tensor_copy(items[i][2], source(i)).then_inc(s_ev[1], 1)

        @block.tensor
        def _(pe):
            pe.wait_ge(n.hn, TC)
            for i, (kind, what, _dst) in enumerate(items):
                if i >= 8:
                    wait_item(pe, i - 8)
                if kind in ("turn", "turnb"):
                    if i == 4:
                        pe.wait_ge(n.hn, 2 * TC)
                    turn_pe(pe, M, i, M.hn if kind == "turn" else hnb).then_inc(s_mm, 1)
                    continue
                if i == 8:
                    wait_item(pe, 2)
                    wait_item(pe, 3)
                if i == 14:
                    wait_item(pe, 6)
                    wait_item(pe, 7)
                if kind == "gates":
                    for c in range(TC):
                        for k in range(KC):
                            mm = pe.matmul(M.ps[:, i % 8, c * 48:(c + 1) * 48], hnbT[:, k, c * P:(c + 1) * P],
                                           M.wg[:, k, :], start=(k == 0), stop=(k == KC - 1))
                else:
                    b, c = what
                    if kind == "kv":
                        x, w = M.hnT, W[b]
                        pe.wait_ge(loaded01[b] if b < 2 else loaded[0], 16)
                    else:
                        x, w = hnbT, W[3 + b]
                        pe.wait_ge(loaded[1 + b], 16)
                    for k in range(KC):
                        mm = pe.matmul(M.ps[:, i % 8, :], x[:, k, c * P:(c + 1) * P], w[:, k, :], start=(k == 0),
                                       stop=(k == KC - 1))
                mm.then_inc(s_mm, 1)


def hnT_part(x, b):
    return x[:, 2 * b:2 * b + 2, :]


KN, QN, SQK, SQQ = 0, 1024, PRE + 5120, PRE + 6144
KCT, X2, BLK = 3072, 4096, 6144
KT, QT = PRE + 8192, 0
HIDK, HIDV, HIDVP, KCN, KCMPT, VCBD = PRE + 9216, PRE + 9280, PRE + 9344, PRE + 9856, PRE + 9984, PRE + 5120


def prep_phase(nc, M, T, sem, loaded, moe1, next_gain):
    kv = M.at(KV, TC, 6, 256)
    q = M.at(Q, TC, D)
    kn, qn = M.at(KN, 2, TC, 256), M.at(QN, TC, 2, 2 * 256)
    hnf = M.hn[:].rearrange("p c d -> p (c d)")
    sqk = M.hnT[:].rearrange("p k t -> p (k t)")[:, 0:1024].rearrange("p (i c n) -> p i c n", i=2, c=TC)
    st = M.hnT[:].rearrange("p k t -> p (k t)")[:, 1024:1024 + 3 * 48].rearrange("p (a n) -> p a n", a=3)
    sqq = hnf.rearrange("p (c n) -> p c n", c=TC)
    kcT = M.at(KCT, 2, 2, SEQ)
    x2 = M.at(X2, 2, GROUPS, SEQ)
    blk = M.at(BLK, 2, 16, GROUPS * NCMP)
    kT = M.at(KT, 2, 2, SEQ)
    qT = M.hnT
    hidk, hidv = M.at(HIDK, 60), M.at(HIDV, GROUPS, NCMP)
    hidvp = M.at(HIDVP, GROUPS, HPG, CPAD)
    kcn, kcmpT = M.at(KCN, 2, DH), M.at(KCMPT, GROUPS, CPAD)
    vcbd = M.at(VCBD, GROUPS, HPG, DH)
    phi1 = M.ring[:, 3, :].rearrange("p (i j f) -> p i j f", i=2, j=16)
    names = ("kcT_mm", "kn_mm", "qn_mm", "kcT_a", "kcT_d", "x2_in", "blk", "hid_mm", "hidk", "hidv", "hidvp",
             "kc_mm", "kc_sq", "kc_ms", "kc_sd", "kcn", "kcT2_mm", "vc_mm", "sq", "ssum", "std", "rstd", "kn", "qn",
             "kT", "qT_a", "qT_d", "pads", "ch", "end", "colq", "st2")
    S = {k: sem("p_" + k) for k in names}

    with nc.Block() as block:
        @block.sync
        def _(sp):
            sp.wait_ge(S["kcT_a"], 1)
            sp.wait_ge(S["kcT_d"], 1)
            for g2 in range(2):
                for l2 in range(2):
                    dst = x2[DH * l2:DH * (l2 + 1)].rearrange("p i (a b) t -> p i a b t", b=2)[:, :, :, g2]
                    for i in range(2):
                        sp.dma_start(dst[:, i, :, 0:SEQ - l2], kcT[DH * g2:DH * (g2 + 1), i, :, l2:SEQ]
                                     ).then_inc(S["x2_in"], 16)
            load_w1(sp, M, T, 1, 0, 0, moe1)
            load_w1(sp, M, T, 1, 1, 1, moe1)
            load_w3(sp, M, T, 1, 0, 0, moe1)
            sp.dma_start(M.gain[:], T["ffn_norm"][1].partition_broadcast(P)).then_inc(next_gain, 16)
            sp.wait_ge(S["hid_mm"], 2)
            load_w3(sp, M, T, 1, 1, 1, moe1)

        @block.gpsimd
        def _(pool):
            nc.gpsimd.memset(M.at(HIDVP, 512), 0.0).then_inc(S["pads"], 1)
            nc.gpsimd.memset(M.at(KCMPT, 128), 0.0).then_inc(S["pads"], 1)
            nc.gpsimd.memset(M.at(VCBD, 1024), 0.0).then_inc(S["pads"], 1)

        @block.tensor
        def _(pe):
            B = M.ps
            for i in range(2):
                for a in range(2):
                    for c in range(TC):
                        mm = pe.transpose(B[:, i, a * SEQ + c * P:a * SEQ + (c + 1) * P],
                                          kv[:, c, i, a * P:(a + 1) * P], M.ident[:])
                mm.then_inc(S["kcT_mm"], 1)
            pe.wait_ge(S["kn"], 2)
            for i in range(2):
                for a in range(2):
                    for c in range(TC):
                        mm = pe.transpose(B[:, 2 + i, a * SEQ + c * P:a * SEQ + (c + 1) * P],
                                          kn[:, i, c, a * P:(a + 1) * P], M.ident[:])
                mm.then_inc(S["kn_mm"], 1)
            pe.wait_ge(S["qn"], 4)
            for b in range(4):
                for kk in range(2):
                    for c in range(TC):
                        a, r = (2 * b + kk) // HPG, (2 * b + kk) % HPG
                        mm = pe.transpose(B[:, 4 + b, kk * SEQ + c * P:kk * SEQ + (c + 1) * P],
                                          qn[:, c, a, r * P:(r + 1) * P], M.ident[:])
                mm.then_inc(S["qn_mm"], 1)
            pe.wait_ge(S["kcT_a"], 1)
            pe.wait_ge(S["kcT_d"], 1)
            pe.wait_ge(loaded[3], 16)
            for i in range(2):
                pe.wait_ge(S["blk"], 2 * (i + 1))
                for j in range(16):
                    mm = pe.matmul(B[:, i, 0:60], phi1[:, i, j], blk[:, i, j], start=(j == 0), stop=(j == 15))
                mm.then_inc(S["hid_mm"], 1)
            pe.wait_ge(S["kT"], 2)
            pe.wait_ge(S["hidk"], 1)
            pe.matmul(B[0:60, 2, 0:DH], hidk, M.phi2[:, 0], start=True, stop=True).then_inc(S["kc_mm"], 1)
            pe.wait_ge(S["hidvp"], HPG)
            for g in range(GROUPS):
                mm = pe.matmul(B[:, 3, g * DH:(g + 1) * DH], hidvp[:, g].rearrange("p r n -> p (r n)"),
                               M.phi2[:, 1], start=True, stop=True)
            mm.then_inc(S["vc_mm"], 1)
            pe.wait_ge(S["kcn"], 2)
            pe.transpose(B[:, 0, 0:60], kcn[0:60].rearrange("p a d -> p (a d)"), M.ident[0:60, 0:60]
                         ).then_inc(S["kcT2_mm"], 1)

        @block.scalar
        def _(act):
            a = nc.scalar
            act.wait_ge(S["kcT_mm"], 1)
            a.copy(kcT[:, 0], bank_pair(M, 0)).then_inc(S["kcT_a"], 1)
            for i in range(2):
                a.activation(sqk[:, i], kv[:, :, 2 + 2 * i], ACT.Square).then_inc(S["sq"], 1)
            a.activation(sqq, q, ACT.Square).then_inc(S["sq"], 1)
            act.wait_ge(S["ssum"], 1)
            a.activation(st[:, 1], st[:, 0], ACT.Sqrt).then_inc(S["std"], 1)
            act.wait_ge(S["kn_mm"], 1)
            a.activation(kT[:, 0], bank_pair(M, 2), ACT.Copy, scale=M.cols2[:, 33:34]).then_inc(S["kT"], 1)
            act.wait_ge(S["colq"], 1)
            act.wait_ge(S["st2"], 1)
            for b in (0, 2):
                act.wait_ge(S["qn_mm"], b + 1)
                a.activation(hnT_part(qT, b), bank_pair(M, 4 + b), ACT.Copy, scale=M.stat[:, 0:1]
                             ).then_inc(S["qT_a"], 1)
            act.wait_ge(S["hid_mm"], 1)
            a.activation(hidk, M.ps[:, 0, 0:60], ACT.Gelu_apprx_tanh, bias=M.cols2[:, 36:37]).then_inc(S["hidk"], 1)
            act.wait_ge(S["hid_mm"], 2)
            a.activation(hidv.rearrange("p g n -> p (g n)"), M.ps[:, 1, 0:60], ACT.Gelu_apprx_tanh,
                         bias=M.cols2[:, 37:38]).then_inc(S["hidv"], 1)
            act.wait_ge(S["kc_mm"], 1)
            act.wait_ge(S["kn_mm"], 2)
            a.activation(kcn[0:60, 0], M.ps[0:60, 2, 0:DH], ACT.Square, accum_out=M.stat[0:60, 1:2]
                         ).then_inc(S["kc_sq"], 1)
            act.wait_ge(S["kc_ms"], 1)
            a.activation(M.stat[0:60, 3:4], M.stat[0:60, 2:3], ACT.Sqrt).then_inc(S["kc_sd"], 1)

        @block.vector
        def _(dve):
            v = nc.vector
            ln = Link(dve, S["ch"])
            dve.wait_ge(S["kcT_mm"], 2)
            v.tensor_copy(kcT[:, 1], bank_pair(M, 1)).then_inc(S["kcT_d"], 1)
            v.tensor_scalar(M.stat[:, 0:1], M.cols2[:, 35:36], DH ** -0.5, None, ALU.mult).then_inc(S["colq"], 1)
            dve.wait_ge(S["sq"], 3)
            ln(v.tensor_reduce(st[:, 0, 0:16], sqk.rearrange("p i c (g d) -> p (i c g) d", d=DH), AX.X, ALU.add))
            ln(v.tensor_reduce(st[:, 0, 16:48], sqq.rearrange("p c (h d) -> p (c h) d", d=DH), AX.X, ALU.add))
            v.tensor_scalar(st[:, 0], st[:, 0], 1.0 / DH, EPS, ALU.mult, ALU.add).then_inc(S["ssum"], 1)
            dve.wait_ge(S["std"], 1)
            ln(v.reciprocal(st[:, 2], st[:, 1]))
            for i in range(2):
                r = st[:, 2, 8 * i:8 * i + 8].rearrange("p (c g) -> p c g", c=TC)
                v.tensor_tensor(kn[:, i].rearrange("p c (g d) -> p c g d", d=DH),
                                kv[:, :, 2 + 2 * i].rearrange("p c (g d) -> p c g d", d=DH),
                                r.unsqueeze(3).to_broadcast([P, TC, GROUPS, DH]), ALU.mult).then_inc(S["kn"], 1)
            for c in range(TC):
                for pr in range(2):
                    r = st[:, 2, 16 + 16 * c + 8 * pr:24 + 16 * c + 8 * pr].rearrange("p (g r) -> p g r", g=2)
                    v.tensor_tensor(qn[:, c, pr].rearrange("p (r g d) -> p g r d", g=2, d=DH),
                                    q[:, c, pr * 512:(pr + 1) * 512].rearrange("p (g r d) -> p g r d", g=2, d=DH),
                                    r.unsqueeze(3).to_broadcast([P, 2, HPG, DH]), ALU.mult).then_inc(S["qn"], 1)
            dve.wait_ge(S["qn"], 4)
            dve.sem_inc(S["st2"], 1)
            dve.wait_ge(S["x2_in"], 16 * 8)
            for i in range(2):
                for hj in range(2):
                    win = x2[:, i, :, 16 * hj:16 * hj + 240].rearrange("p g (n j x) -> p j g n x", j=8, x=2)
                    for g in range(GROUPS):
                        pe_col = M.cols2[:, 16 * i + 8 * hj:16 * i + 8 * hj + 8]
                        o = v.tensor_tensor(blk[:, i, 8 * hj:8 * hj + 8, g * NCMP:(g + 1) * NCMP], win[:, :, g, :, 0],
                                            pe_col.unsqueeze(2).to_broadcast([P, 8, NCMP]), ALU.add)
                    o.then_inc(S["blk"], 1)
            dve.wait_ge(S["kn_mm"], 2)
            v.tensor_scalar(kT[:, 1], bank_pair(M, 3), M.cols2[:, 34:35], None, ALU.mult).then_inc(S["kT"], 1)
            for b in (1, 3):
                dve.wait_ge(S["qn_mm"], b + 1)
                v.tensor_scalar(hnT_part(qT, b), bank_pair(M, 4 + b), M.stat[:, 0:1], None, ALU.mult
                                ).then_inc(S["qT_d"], 1)
            dve.wait_ge(S["pads"], 3)
            dve.wait_ge(S["hidv"], 1)
            for r in range(HPG):
                v.tensor_copy(hidvp[:, :, r, 0:NCMP], hidv).then_inc(S["hidvp"], 1)
            dve.wait_ge(S["kc_sq"], 1)
            v.tensor_scalar(M.stat[0:60, 2:3], M.stat[0:60, 1:2], 1.0 / DH, EPS, ALU.mult, ALU.add
                            ).then_inc(S["kc_ms"], 1)
            dve.wait_ge(S["kc_sd"], 1)
            ln(v.reciprocal(M.stat[0:60, 4:5], M.stat[0:60, 3:4]))
            for x in range(2):
                v.tensor_scalar(kcn[0:60, x], M.ps[0:60, 2, 0:DH], M.stat[0:60, 4:5], None, ALU.mult
                                ).then_inc(S["kcn"], 1)
            dve.wait_ge(S["vc_mm"], 1)
            for r in range(HPG):
                rs = slice(CPAD * r, CPAD * (r + 1))
                v.tensor_copy(vcbd[rs, :, r], M.ps[rs, 3, 0:256].rearrange("p (g d) -> p g d", d=DH)
                              ).then_inc(S["end"], 1)
            dve.wait_ge(S["kcT2_mm"], 1)
            v.tensor_scalar(kcmpT[:, :, 0:NCMP], M.ps[:, 0, 0:60].rearrange("p (g n) -> p g n", g=GROUPS),
                            M.cols2[:, 32:33], None, ALU.mult).then_inc(S["end"], 1)


SC, PTC, PB, PTB, O, OT = 0, 1024, 2048, 2048 + 3 * 512, Q, 5120


def attend_phase(nc, M, T, sem, loaded, moe1):
    kv = M.at(KV, TC, 6, 256)
    qT, kT = M.hnT, M.at(KT, 2, 2, SEQ)
    kcmpT, vcbd = M.at(KCMPT, GROUPS, CPAD), M.at(VCBD, GROUPS, HPG * DH)
    sc = M.at(SC, TC, HEADS, CPAD)
    ptc = M.at(PTC, TC, GROUPS, P)
    pb = M.at(PB, 3, 2, SEQ)
    ptb = M.at(PTB, 2, 4, P)
    o = M.at(O, TC, D)
    oT = M.at(OT, KC, SEQ)
    st = M.at(HIDK, 8, 32)
    nm, sm, gr = (M.hn[:, 0, i * 64:(i + 1) * 64].rearrange("p (n b) -> p n b", b=2) for i in range(3))
    N = TC * HEADS
    names = ("c_mm", "c_ch", "c_exp", "c_p", "c_tp", "c_ev", "s_mm", "max", "exp", "scaled", "t_mm", "pt", "pv",
             "o_ev", "o_tp", "oT_a", "oT_d", "out", "res", "sm_ch", "wl")
    S = {k: sem("a_" + k) for k in names}
    wout = M.ring[:, 4:6, :].rearrange("p u (k n) -> p (u k) n", k=4)

    def where(h):
        g, r = h // HPG, h % HPG
        return g, (g // 2) * HPG + r, slice(DH * (g % 2), DH * (g % 2) + DH), g // 2

    with nc.Block() as block:
        @block.sync
        def _(sp):
            sp.wait_ge(S["out"], 1)
            for slot in range(2):
                load_w2(sp, M, T, 1, slot, slot, moe1)

        @block.tensor
        def _(pe):
            B = M.ps
            for c in range(TC):
                for h in range(HEADS):
                    g, pair, half, a = where(h)
                    col = (a * HPG + h % HPG) * CPAD
                    mm = pe.matmul(B[:, 4 + 2 * c + g % 2, col:col + CPAD], qT[half, pair, c * P:(c + 1) * P],
                                   kcmpT[half, g], start=True, stop=True)
            mm.then_inc(S["c_mm"], 1)

            def scores(n):
                c, h = n // HEADS, n % HEADS
                g, pair, half, a = where(h)
                nk = P * (c + 1)
                if n >= 2:
                    pe.wait_ge(S["exp"], 2 * (n - 1))
                bank = B[:, 4 + n % 2, :]
                for b in range(2):
                    pe.matmul(bank[:, b * SEQ:b * SEQ + nk], qT[half, pair, c * P:(c + 1) * P], kT[half, b, a, 0:nk],
                              start=True, stop=False)
                    mm = pe.matmul(bank[:, b * SEQ + nk - P:b * SEQ + nk], M.identb[:], M.causal[:], start=False,
                                   stop=True)
                mm.then_inc(S["s_mm"], 1)

            def turn(n):
                c = n // HEADS
                pe.wait_ge(S["scaled"], 2 * (n + 1))
                if n >= 2:
                    pe.wait_ge(S["pt"], n - 1)
                for kc in range(c + 1):
                    for b in range(2):
                        x = 2 * kc + b
                        mm = pe.transpose(B[:, 6 + n % 2, x * P:(x + 1) * P], pb[:, n % 3, b, kc * P:(kc + 1) * P],
                                          M.ident[:])
                mm.then_inc(S["t_mm"], 1)

            def values(n):
                c, h = n // HEADS, n % HEADS
                pe.wait_ge(S["pt"], n + 1)
                for kc in range(c + 1):
                    for b in range(2):
                        mm = pe.matmul(B[:, 2 * c + h // 8, (h % 8) * DH:(h % 8 + 1) * DH], ptb[:, n % 2, 2 * kc + b],
                                       kv[:, kc, 3 + 2 * b, (h // HPG) * DH:(h // HPG + 1) * DH], start=False,
                                       stop=(h % 8 == 7 and kc == c and b == 1), skip_group_check=True)
                mm.then_inc(S["pv"], 1)

            pe.wait_ge(S["c_ch"], 4)
            scores(0)
            scores(1)
            for c in range(TC):
                pe.wait_ge(S["c_p"], c + 1)
                for g in range(GROUPS):
                    mm = pe.transpose(B[:, 6 + c, g * P:(g + 1) * P], sc[:, c, g * HPG:(g + 1) * HPG].rearrange(
                        "p r n -> p (r n)"), M.ident[:])
                mm.then_inc(S["c_tp"], 1)
            for c in range(TC):
                pe.wait_ge(S["c_ev"], c + 1)
                for g in range(GROUPS):
                    pe.matmul(B[:, 2 * c + g // 2, (g % 2) * 256:(g % 2 + 1) * 256], ptc[:, c, g], vcbd[:, g],
                              start=(g % 2 == 0), stop=False, skip_group_check=True)
            for n in range(N + 2):
                if 2 <= n < N:
                    scores(n)
                if 1 <= n <= N:
                    turn(n - 1)
                if n >= 2:
                    values(n - 2)
            pe.wait_ge(S["o_ev"], 4)
            for b in range(4):
                turn_pe(pe, M, b, o).then_inc(S["o_tp"], 1)
            pe.wait_ge(S["oT_a"], 2)
            pe.wait_ge(S["oT_d"], 2)
            pe.wait_ge(loaded[4], 16)
            for i in range(4):
                for k in range(KC):
                    mm = pe.matmul(B[:, 4 + i, :], oT[:, k, (i // 2) * P:(i // 2 + 1) * P],
                                   wout[:, k, (i % 2) * 512:(i % 2 + 1) * 512], start=(k == 0), stop=(k == KC - 1))
                mm.then_inc(S["res"], 1)
            mm = pe.matmul(B[:, 0, 0:1], M.ident[:], M.ones[:, 0:1], start=True, stop=True)
            mm.then_inc(S["out"], 1)

        @block.scalar
        def _(act):
            a = nc.scalar
            act.wait_ge(S["c_ch"], 7)
            for c in range(TC):
                a.activation(sc[:, c], sc[:, c], ACT.Exp).then_inc(S["c_exp"], 1)
            for n in range(N + 1):
                if n < N:
                    nk = P * (n // HEADS + 1)
                    act.wait_ge(S["max"], n + 1)
                    if n >= 3:
                        act.wait_ge(S["t_mm"], n - 2)
                    for b in range(2):
                        a.activation(pb[:, n % 3, b, 0:nk], M.ps[:, 4 + n % 2, b * SEQ:b * SEQ + nk], ACT.Exp,
                                     bias=nm[:, n, b:b + 1], accum_out=sm[:, n, b:b + 1]).then_inc(S["exp"], 1)
                if n == 0:
                    for c in range(TC):
                        act.wait_ge(S["c_tp"], c + 1)
                        a.copy(ptc[:, c], M.ps[:, 6 + c, :].rearrange("p (g q) -> p g q", g=GROUPS)
                               ).then_inc(S["c_ev"], 1)
                if n >= 1:
                    m = n - 1
                    blocks = 2 * (m // HEADS + 1)
                    act.wait_ge(S["t_mm"], m + 1)
                    if m >= 2:
                        act.wait_ge(S["pv"], m - 1)
                    a.copy(ptb[:, m % 2, 0:blocks], M.ps[:, 6 + m % 2, 0:blocks * P].rearrange(
                        "p (x q) -> p x q", q=P)).then_inc(S["pt"], 1)
            act.wait_ge(S["pv"], N)
            for c in range(TC):
                a.copy(o[:, c, 0:512], M.ps[:, 2 * c, :]).then_inc(S["o_ev"], 1)
            for b in (0, 2):
                act.wait_ge(S["o_tp"], b + 1)
                a.copy(hnT_part(oT, b), bank_pair(M, b)).then_inc(S["oT_a"], 1)

        @block.vector
        def _(dve):
            v = nc.vector
            ln = Link(dve, S["c_ch"])
            ch2 = Link(dve, S["sm_ch"])
            dve.wait_ge(S["c_mm"], 1)
            scf = sc.rearrange("p c h n -> p (c h) n")
            for c in range(TC):
                for g2 in range(2):
                    ln(v.tensor_tensor(sc[:, c].rearrange("p (a b r) n -> p b a r n", a=2, b=2)[:, g2],
                                       M.ps[:, 4 + 2 * c + g2, 0:256].rearrange("p (a r n) -> p a r n", a=2, r=HPG),
                                       M.cmask[:, c].unsqueeze(1).unsqueeze(1).to_broadcast([P, 2, HPG, CPAD]),
                                       ALU.add))
            ln(v.tensor_reduce(st[:, 0], scf, AX.X, ALU.max, negate=True))
            for c in range(TC):
                ln(v.tensor_tensor(sc[:, c], sc[:, c], st[:, 0, 16 * c:16 * c + 16].unsqueeze(2).to_broadcast(
                    [P, HEADS, CPAD]), ALU.add))

            def highest(n):
                nk = P * (n // HEADS + 1)
                dve.wait_ge(S["s_mm"], n + 1)
                v.tensor_reduce(nm[:, n], M.ps[:, 4 + n % 2, :].rearrange("p (b k) -> p b k", b=2)[:, :, 0:nk], AX.X,
                                ALU.max, negate=True).then_inc(S["max"], 1)

            def scale(n):
                c, h = n // HEADS, n % HEADS
                nk = P * (c + 1)
                dve.wait_ge(S["exp"], 2 * (n + 1))
                ch2(v.reciprocal(gr[:, n], sm[:, n]))
                ch2(v.tensor_tensor(gr[:, n], gr[:, n], M.gates[:, c, 3 * h + 1:3 * h + 3], ALU.mult))
                for b in range(2):
                    v.tensor_scalar(pb[:, n % 3, b, 0:nk], pb[:, n % 3, b, 0:nk], gr[:, n, b:b + 1], None, ALU.mult
                                    ).then_inc(S["scaled"], 1)

            highest(0)
            dve.wait_ge(S["c_exp"], 2)
            ch2(v.tensor_reduce(st[:, 1], scf, AX.X, ALU.add))
            ch2(v.reciprocal(st[:, 2], st[:, 1]))
            for c in range(TC):
                cs = slice(16 * c, 16 * c + 16)
                g0 = M.gates[:, c].rearrange("p (h b) -> p h b", b=3)[:, :, 0]
                ch2(v.scalar_tensor_tensor(st[:, 3, cs], st[:, 2, cs], M.cvalid[:, c:c + 1], g0, ALU.mult, ALU.mult))
                v.tensor_tensor(sc[:, c], sc[:, c], st[:, 3, cs].unsqueeze(2).to_broadcast([P, HEADS, CPAD]),
                                ALU.mult).then_inc(S["c_p"], 1)
            for n in range(1, N):
                highest(n)
                scale(n - 1)
            scale(N - 1)
            dve.wait_ge(S["pv"], N)
            for c in range(TC):
                v.tensor_copy(o[:, c, 512:1024], M.ps[:, 2 * c + 1, :]).then_inc(S["o_ev"], 1)
            for b in (1, 3):
                dve.wait_ge(S["o_tp"], b + 1)
                v.tensor_copy(hnT_part(oT, b), bank_pair(M, b)).then_inc(S["oT_d"], 1)
            for i in range(4):
                dve.wait_ge(S["res"], i + 1)
                hs = M.h[:, i // 2, (i % 2) * 512:(i % 2 + 1) * 512]
                v.tensor_tensor(hs, hs, M.ps[:, 4 + i, :], ALU.add).then_inc(S["wl"], 1)


def build(nc, T, out):
    with ExitStack() as ctx:
        sem = Sems(nc, ctx)
        M = Mem(nc, ctx)
        landed = [Landed(sem, f"m{i}") for i in range(2)]
        landed_ovf = [Landed(sem, f"v{i}") for i in range(2)]
        gains = [sem(f"gain_in{i}") for i in range(4)]
        pre = [sem(f"wkv_in{i}") for i in range(2)]
        loaded, again = [sem(f"att_in{i}") for i in range(5)], [sem(f"att_again{i}") for i in range(5)]
        s_end = sem("h_out")

        def phase(f, *args):
            with ExitStack() as c:
                own = Sems(nc, c)
                f(nc, M, T, own, *args)
                own.clear()

        def wait_loaded(sp):
            for x in loaded:
                sp.wait_ge(x, 16)

        def load_again(sp):
            attention_loads(sp, M, T, again)
            for x in again:
                sp.wait_ge(x, 16)

        phase(conv_phase, landed[0], pre, gains)
        phase(route_phase, 0, gains[1], T["kv_norm"], gains[2])
        phase(jobs_phase, 0, landed[0], lambda sp: attention_loads(sp, M, T, loaded))
        phase(overflow_phase, 0, landed_ovf[0], (wait_loaded, load_again))
        phase(project_phase, gains[2], loaded, pre)
        phase(prep_phase, loaded, landed[1], gains[3])
        phase(attend_phase, loaded, landed[1])
        phase(route_phase, 1, gains[3], None, None)
        phase(jobs_phase, 1, landed[1], None)
        phase(overflow_phase, 1, landed_ovf[1], None)
        with nc.Block() as block:
            @block.sync
            def _(sp):
                sp.dma_start(out[0].rearrange("(c p) d -> p c d", p=P), M.h[:]).then_inc(s_end, 16)
                sp.wait_ge(s_end, 16)


NAMES = ["x", "a_norm", "a_w_in", "a_dw", "a_dw_bias", "a_conv_norm", "a_w_out", "kv_norm", "w_kv", "cmp_pe",
         "phi_w1", "phi_b1", "phi_w2", "k_norm", "b_norm", "b_w_in", "b_q_norm", "b_w_out", "ffn_norm",
         "router_w", "router_bias", "moe_w1", "moe_w3", "moe_w2"]


def kernel(**inputs):
    import numpy as _np
    import concourse.bacc as _bacc
    from concourse import mybir as _mybir
    from concourse.bass_utils import run_bass_kernel_spmd as _run

    nc = _bacc.Bacc("TRN2", target_bir_lowering=False, num_devices=1)
    arrays, aps = {}, {}
    for name in NAMES:
        a = _np.ascontiguousarray(inputs[name])
        arrays[f"in_{name}"] = a
        aps[name] = nc.dram_tensor(f"in_{name}", a.shape, _mybir.dt.from_np(a.dtype), kind="ExternalInput").ap()
    out = nc.dram_tensor("out", inputs["x"].shape, _mybir.dt.float32, kind="ExternalOutput").ap()
    build(nc, aps, out)
    r = _run(nc, [arrays], core_ids=[0])
    return r.results[0]["out"]
```

```python
from contextlib import ExitStack

import concourse.bass as bass
from concourse import mybir

F32 = mybir.dt.float32
F32R = mybir.dt.float32r
BF16 = mybir.dt.bfloat16
I32 = mybir.dt.int32
ALU = mybir.AluOpType
ACT = mybir.ActivationFunctionType
AX = mybir.AxisListType

P = 128
SEQ = 256
TC = SEQ // P
D = 1024
KC = D // P
TAPS = 31
HEADS, GROUPS, HPG, DH = 16, 4, 4, 64
CMP_LEN, CMP_STRIDE = 32, 16
NCMP = (SEQ - CMP_LEN) // CMP_STRIDE + 1
CPAD = 32
HID = 128
EXPERTS, EGROUPS, EPG = 16, 4, 4
DE = 512
FC = DE // P
EPS = 1e-6
NEG = -1e30
BANK = 512
CHUNK = 2048
ARENA = 12352
RAWS, PARTS = 6, 3


CLOCK_UP = 4


class Sems:

    def __init__(self, nc, ctx):
        self.nc, self.ctx, self.taken = nc, ctx, []

    def __call__(self, name):
        s = self.ctx.enter_context(self.nc.semaphore(name))
        self.taken.append(s)
        return s

    def clear(self):
        nums = sorted(s.num for s in self.taken)
        first = [n for n in nums if n - 1 not in nums]
        last = [n for n in nums if n + 1 not in nums]
        with self.nc.Block() as block:
            @block.gpsimd
            def _(pool):
                for a, b in zip(first, last):
                    pool.sem_clear(range(a, b + 1))


class Link:

    def __init__(self, eng, sem):
        self.eng, self.sem, self.n = eng, sem, 0

    def __call__(self, ins):
        self.n += 1
        ins.then_inc(self.sem, 1)
        self.eng.wait_ge(self.sem, self.n)


class Mem:

    def __init__(self, nc, ctx):
        def sb(name, shape, dt=F32):
            return ctx.enter_context(nc.sbuf_tensor(name, shape, dt))

        self.raw = sb("raw", [P, RAWS, CHUNK])
        self.hi = sb("hi", [P, PARTS, CHUNK], F32R)
        self.lo = sb("lo", [P, PARTS, CHUNK], F32R)
        self.arena = sb("arena", [P, ARENA])
        self.xg = [sb("xg_hi", [P, KC, P], F32R), sb("xg_lo", [P, KC, P], F32R)]
        self.gut = [sb("gut_hi", [P, 2, FC, P], F32R), sb("gut_lo", [P, 2, FC, P], F32R)]
        self.h = sb("h", [P, TC, D])
        self.hn = sb("hn", [P, TC, D])
        self.hnT = [sb("hnT_hi", [P, KC, SEQ], F32R), sb("hnT_lo", [P, KC, SEQ], F32R)]
        self.gain = sb("gain", [P, D])
        self.ident = sb("ident", [P, P])
        self.ones = sb("ones", [P, P])
        self.before = sb("before", [P, P])
        self.iota = sb("iota", [P, P])
        self.identb = sb("identb", [P, P], BF16)
        self.causal = sb("causal", [P, P], BF16)
        self.cmask = sb("cmask", [P, TC, CPAD])
        self.cvalid = sb("cvalid", [P, TC])
        self.cols = sb("cols", [P, KC, TAPS + 2])
        self.cols2 = sb("cols2", [P, 38])
        self.stat = sb("stat", [P, 8])
        self.rw = [sb("rw_hi", [P, KC, EXPERTS], F32R), sb("rw_lo", [P, KC, EXPERTS], F32R)]
        self.rb = sb("rb", [P, EXPERTS])
        self.wg = [sb("wg_hi", [P, KC, 3 * HEADS], F32R), sb("wg_lo", [P, KC, 3 * HEADS], F32R)]
        self.phi2 = sb("phi2", [P, 2, DH])
        self.jgate = sb("jgate", [P, 5, EPG])
        self.rank = sb("rank", [P, TC])
        self.g4 = sb("g4", [P, TC, EPG])
        self.gates = sb("gates", [P, TC, 3 * HEADS])
        self.ovf = sb("ovf", [P, 2], I32)
        self.ps = ctx.enter_context(nc.psum_tensor("ps", [P, 8, BANK], F32))

    def at(self, start, *shape):
        n = 1
        for s in shape:
            n *= s
        v = self.arena[:, start:start + n]
        if len(shape) == 1:
            return v
        names = "abcd"[:len(shape)]
        return v.rearrange(f"p ({' '.join(names)}) -> p {' '.join(names)}",
                           **{k: s for k, s in zip(names, shape)})


def mm3(pe, out, x, w, start, stop):
    pe.matmul(out, x[0], w[0], start=start, stop=False)
    pe.matmul(out, x[0], w[1], start=False, stop=False)
    return pe.matmul(out, x[1], w[0], start=False, stop=stop)


def both(parts, *index):
    return [p[index] for p in parts]


class Stream:

    def __init__(self, nc, M, sem, tag, off):
        self.nc, self.M, self.off = nc, M, off
        self.landed = [sem(f"{tag}_landed{i}") for i in range(RAWS)]
        self.hi, self.lo, self.used = sem(f"{tag}_hi"), sem(f"{tag}_lo"), sem(f"{tag}_used")

    def load(self, eng, n, src):
        slot = (self.off + n) % RAWS
        dst = self.M.raw[:, slot, :].rearrange("p (k f) -> p k f", k=src.shape[1])
        eng.dma_start(dst, src).then_inc(self.landed[slot], 16)

    def number(self, j, i):
        return j * JOB_CHUNKS + i

    def filled(self, j, i):
        return j * (16 * JOB_CHUNKS // RAWS) + 16 * (i // RAWS + 1)

    def split_hi(self, act, j, i):
        slot = (self.off + i) % RAWS
        act.wait_ge(self.landed[slot], self.filled(j, i))
        act.wait_ge(self.used, self.number(j, i) + 1)
        self.nc.scalar.copy(self.M.hi[:, (self.off + i) % PARTS], self.M.raw[:, slot]).then_inc(self.hi, 1)

    def split_lo(self, eng, j, i):
        eng.wait_ge(self.hi, self.number(j, i) + 1)
        x = (self.off + i) % PARTS
        eng.tensor_tensor(self.M.lo[:, x], self.M.raw[:, (self.off + i) % RAWS], self.M.hi[:, x], ALU.subtract
                          ).then_inc(self.lo, 1)

    def parts(self, pe, j, i, k):
        pe.wait_ge(self.lo, self.number(j, i) + 1)
        x = (self.off + i) % PARTS
        return [t[:, x].rearrange("p (k f) -> p k f", k=k) for t in (self.M.hi, self.M.lo)]

    def wait_raw_free(self, sp, j, i):
        sp.wait_ge(self.lo, self.number(j, i) + 1)

    def wait_used(self, eng, j, i):
        eng.wait_ge(self.used, self.number(j, i) + 1 + PARTS)


JOB_CHUNKS = 24


def cut_k(w, halves):
    v = w.rearrange("(k p) n -> p k n", p=P)
    return [v[:, 4 * i:4 * i + 4] for i in range(halves)]


def cut_wide(w):
    v = w.rearrange("(k p) n -> p k n", p=P)
    return [v[:, 2 * i:2 * i + 2] for i in range(v.shape[1] // 2)]


def conv_chunks(T):
    v = T["a_w_in"][0].rearrange("(k p) n -> p k n", p=P)
    return [v[:, :, ab * D + 256 * q:ab * D + 256 * (q + 1)] for q in range(4) for ab in range(2)] + \
        cut_wide(T["a_w_out"][0])


def attention_chunks(T):
    out = []
    for b in range(3):
        out += cut_k(T["w_kv"][:, b * 512:(b + 1) * 512], 2)
    for b in range(2):
        out += cut_k(T["b_w_in"][0][:, b * 512:(b + 1) * 512], 2)
    out += [T["phi_w1"][i].rearrange("(j p) f -> p j f", p=P) for i in range(2)]
    return out + cut_wide(T["b_w_out"][0])


JOB_ORDER = [(w, 0, x) for w in ("w1", "w3") for x in range(2)]
for _e in range(1, EPG):
    JOB_ORDER += [(w, e, x) for w, e in (("w1", _e), ("w3", _e), ("w2", _e - 1)) for x in range(2)]
JOB_ORDER += [("w2", EPG - 1, x) for x in range(2)]


def job_chunk(T, layer, first, i):
    w, e, x = JOB_ORDER[i]
    v = T["moe_" + w][layer][bass.ds(first + e, 1)].rearrange("o (k p) f -> p (o k) f", p=P)
    return v[:, 4 * x:4 * x + 4] if w != "w2" else v[:, 2 * x:2 * x + 2]



class NormSems:
    def __init__(self, sem, gain, tag):
        self.sq, self.ms, self.sd, self.rs = (sem(f"{tag}_{n}") for n in ("sumsq", "meansq", "std", "rstd"))
        self.hn, self.tp = sem(f"{tag}_normed"), sem(f"{tag}_turned")
        self.ev = [sem(f"{tag}_hnT_act"), sem(f"{tag}_hnT_dve")]
        self.gain = gain


def norm_act(nc, act, M, s):
    for c in range(TC):
        nc.scalar.activation(M.hn[:, c, :], M.h[:, c, :], ACT.Square, accum_out=M.stat[:, c:c + 1]).then_inc(s.sq, 1)
    act.wait_ge(s.ms, 1)
    nc.scalar.activation(M.stat[:, 4:6], M.stat[:, 2:4], ACT.Sqrt).then_inc(s.sd, 1)


def norm_dve(nc, dve, M, s):
    dve.wait_ge(s.sq, TC)
    nc.vector.tensor_scalar(M.stat[:, 2:4], M.stat[:, 0:2], 1.0 / D, EPS, ALU.mult, ALU.add).then_inc(s.ms, 1)
    dve.wait_ge(s.sd, 1)
    nc.vector.reciprocal(M.stat[:, 6:8], M.stat[:, 4:6]).then_inc(s.rs, 1)
    dve.wait_ge(s.rs, 1)
    dve.wait_ge(s.gain, 16)
    for c in range(TC):
        nc.vector.scalar_tensor_tensor(M.hn[:, c, :], M.h[:, c, :], M.stat[:, 6 + c:7 + c], M.gain[:, :],
                                       ALU.mult, ALU.mult).then_inc(s.hn, 1)


def turn_pe(pe, M, b, src):
    for kk in range(2):
        for c in range(TC):
            k = 2 * (b % 4) + kk
            mm = pe.transpose(M.ps[:, b % 8, kk * SEQ + c * P:kk * SEQ + (c + 1) * P],
                              src[:, c, k * P:(k + 1) * P], M.ident[:, :])
    return mm


def norm_pe(pe, M, s):
    pe.wait_ge(s.hn, TC)
    for b in range(4):
        turn_pe(pe, M, b, M.hn).then_inc(s.tp, 1)


def bank_pair(M, b):
    return M.ps[:, b, :].rearrange("p (k t) -> p k t", k=2)


def part(x, b):
    return x[:, 2 * b:2 * b + 2, :]


def norm_evac_act(nc, act, M, s):
    for b in range(4):
        act.wait_ge(s.tp, b + 1)
        nc.scalar.copy(part(M.hnT[0], b), bank_pair(M, b)).then_inc(s.ev[0], 1)


def norm_evac_dve(nc, dve, M, s):
    for b in range(4):
        dve.wait_ge(s.ev[0], b + 1)
        nc.vector.tensor_tensor(part(M.hnT[1], b), bank_pair(M, b), part(M.hnT[0], b), ALU.subtract
                                ).then_inc(s.ev[1], 1)


def wait_hnT(eng, s):
    eng.wait_ge(s.ev[1], 4)



PE_CONV = (1, 3, 5)
DVE_CONV = (0, 2, 4)
GLU_BANKS, SIGS, DIAGS = 6, 4, 16


def conv_bank(i):
    return 2 + i


def conv_phase(nc, M, T, sem, st, nxt, gains):
    U = M.at(0, KC, TAPS - 1 + SEQ)
    ACC = M.at(2288, KC, SEQ)
    SQ = M.at(4848, KC, SEQ)
    RSTD = M.at(6896, 2, SEQ)
    ROWS = M.at(7408, 1024)
    ROWS2 = M.at(8432, P)
    RW, WG = M.at(8560, KC, EXPERTS), M.at(8688, KC, 3 * HEADS)
    SIG = M.at(9072, SIGS, SEQ)
    DIAG = M.at(9072 + SIGS * SEQ, DIAGS, P)
    chunks, ahead = conv_chunks(T), [job_chunk(T, 0, 0, i) for i in range(RAWS)]
    NC = len(chunks)
    n = NormSems(sem, gains[0], "n0")
    s_x, s_rows, s_small = sem("x_in"), sem("rows_in"), sem("small_in")
    s_smallh, s_smalll, s_yh, s_yl = sem("small_hi"), sem("small_lo"), sem("y_hi"), sem("y_lo")
    s_const, s_pool = sem("constants"), sem("pool_chain")
    s_cols, s_colsT = sem("cols"), sem("colsT")
    s_mm, s_sig, s_glu = sem("glu_mm"), sem("glu_sig"), sem("glu_done")
    s_tap, s_sq, s_ssum = sem("taps"), sem("conv_sq"), sem("conv_ssum")
    s_conv, s_diag, s_dused, s_cmm, s_cev = (sem(x) for x in (
        "conv_chunk_dve", "diag", "diag_used", "conv_chunk_pe", "conv_evac"))
    s_ms, s_sd, s_rs, s_z, s_y = (sem(f"conv_{k}") for k in ("ms", "sd", "rs", "z", "y"))
    s_out, s_res = sem("conv_out"), sem("conv_res")

    with nc.Block() as block:
        @block.sync
        def _(sp):
            sp.dma_start(M.h[:], T["x"][0].rearrange("(c p) d -> p c d", p=P)).then_inc(s_x, 16)
            sp.dma_start(ROWS[0:TAPS, :], T["a_dw"][0]).then_inc(s_rows, 16)
            sp.dma_start(ROWS[TAPS:TAPS + 1, :], T["a_dw_bias"]).then_inc(s_rows, 16)
            sp.dma_start(ROWS[TAPS + 1:TAPS + 2, :], T["a_conv_norm"]).then_inc(s_rows, 16)
            sp.dma_start(M.gain[:], T["a_norm"][0].partition_broadcast(P)).then_inc(n.gain, 16)
            sp.dma_start(ROWS2[0:32, :], T["cmp_pe"].rearrange("i (j l) d -> (i j) (l d)", l=2)).then_inc(s_rows, 16)
            for half in range(2):
                cs = slice(half * DH, (half + 1) * DH)
                sp.dma_start(ROWS2[32:35, cs], T["k_norm"]).then_inc(s_rows, 16)
                sp.dma_start(ROWS2[35:36, cs], T["b_q_norm"]).then_inc(s_rows, 16)
            sp.dma_start(ROWS2[36:38, :], T["phi_b1"]).then_inc(s_rows, 16)
            for i in range(RAWS):
                st.load(sp, i, chunks[i])
            sp.dma_start(RW, T["router_w"].rearrange("(k p) e -> p k e", p=P)).then_inc(s_small, 16)
            sp.dma_start(M.rb[:], T["router_bias"].partition_broadcast(P)).then_inc(s_small, 16)
            sp.dma_start(WG, T["b_w_in"][0].rearrange("(k p) n -> p k n", p=P)[:, :, D:]).then_inc(s_small, 16)
            sp.dma_start(M.phi2[:], T["phi_w2"].rearrange("i h d -> h i d")).then_inc(s_small, 16)
            sp.wait_ge(n.hn, TC)
            sp.dma_start(M.gain[:], T["ffn_norm"][0].partition_broadcast(P)).then_inc(gains[1], 16)
            for i in range(NC):
                st.wait_raw_free(sp, 0, i)
                if i + RAWS < NC:
                    st.load(sp, i + RAWS, chunks[i + RAWS])
                else:
                    nxt.load(sp, i + RAWS - NC, ahead[i + RAWS - NC])

        @block.gpsimd
        def _(pool):
            chain = Link(pool, s_pool)
            g = nc.gpsimd
            chain(g.memset(M.ones[:], 1.0))
            chain(g.affine_select(out=M.ident[:], in_=M.ones[:], pattern=[[-1, P]], compare_op=ALU.is_equal,
                                  fill=0.0, base=0, channel_multiplier=1))
            pool.wait_ge(s_pool, 2)
            g.memset(U[:, :, 0:TAPS - 1], 0.0).then_inc(s_const, 1)
            chain(g.affine_select(out=M.before[:], in_=M.ones[:], pattern=[[1, P]], compare_op=ALU.is_ge,
                                  fill=0.0, base=-1, channel_multiplier=-1))
            chain(g.iota(M.iota[:], pattern=[[1, P]], base=0, channel_multiplier=0,
                         allow_small_or_imprecise_dtypes=True))
            chain(g.tensor_copy(M.identb[:], M.ident[:]))
            chain(g.memset(M.causal[:], 0.0))
            chain(g.memset(M.cmask[:], 0.0))
            chain(g.memset(M.cvalid[:], 1.0))
            chain(g.affine_select(out=M.causal[:], in_=M.causal[:], pattern=[[-1, P]], compare_op=ALU.is_ge,
                                  fill=NEG, base=0, channel_multiplier=1))
            for c in range(TC):
                end = c * P - (CMP_LEN - 1)
                chain(g.affine_select(out=M.cmask[:, c], in_=M.cmask[:, c], pattern=[[-CMP_STRIDE, CPAD]],
                                      compare_op=ALU.is_ge, fill=NEG, base=end, channel_multiplier=1))
                chain(g.affine_select(out=M.cvalid[:, c:c + 1], in_=M.cvalid[:, c:c + 1], pattern=[[0, 1]],
                                      compare_op=ALU.is_ge, fill=0.0, base=end, channel_multiplier=1))
            for i in range(NC):
                st.split_lo(pool, 0, i)

        @block.scalar
        def _(act):
            act.wait_ge(s_x, 16)
            norm_act(nc, act, M, n)
            act.wait_ge(s_colsT, 1)
            nc.scalar.copy(M.cols[:], M.ps[:, 7, 0:KC * (TAPS + 2)].rearrange("p (k r) -> p k r", k=KC)
                           ).then_inc(s_cols, 1)
            nc.scalar.copy(M.cols2[:], M.ps[:, 6, 0:38]).then_inc(s_cols, 1)
            for i in range(2):
                st.split_hi(act, 0, i)
            norm_evac_act(nc, act, M, n)
            st.split_hi(act, 0, 2)

            def diagonals(i, first=0, end=TAPS):
                for tap in range(first, end):
                    k = i * TAPS + tap
                    if k >= DIAGS:
                        act.wait_ge(s_dused, k - DIAGS + 1)
                    nc.scalar.activation(DIAG[:, k % DIAGS], M.ident[:], ACT.Copy,
                                         scale=M.cols[:, PE_CONV[i], tap:tap + 1]).then_inc(s_diag, 1)

            def square(c):
                if c in PE_CONV:
                    i = PE_CONV.index(c)
                    act.wait_ge(s_cmm, i + 1)
                    act.wait_ge(s_conv, i + 1)
                    nc.scalar.activation(ACC[:, c], M.ps[:, conv_bank(i), 0:SEQ], ACT.Identity,
                                         bias=M.cols[:, c, TAPS:TAPS + 1]).then_inc(s_cev, 1)
                    act.wait_ge(s_cev, i + 1)
                else:
                    act.wait_ge(s_conv, DVE_CONV.index(c) + 1 if c in DVE_CONV else c - 2)
                nc.scalar.activation(SQ[:, c], ACC[:, c], ACT.Square).then_inc(s_sq, 1)

            act.wait_ge(s_const, 1)
            for c in range(KC):
                act.wait_ge(s_mm, c + 1)
                if c >= SIGS:
                    act.wait_ge(s_glu, c - SIGS + 1)
                nc.scalar.activation(SIG[:, c % SIGS], M.ps[:, c % GLU_BANKS, SEQ:], ACT.Sigmoid).then_inc(s_sig, 1)
                if c == KC - 2:
                    diagonals(0, 0, DIAGS)
                st.split_hi(act, 0, c + PARTS)
            diagonals(0, DIAGS)
            diagonals(1)
            square(0)
            square(1)
            diagonals(2)
            act.wait_ge(s_small, 64)
            nc.scalar.copy(M.rw[0][:], RW).then_inc(s_smallh, 1)
            nc.scalar.copy(M.wg[0][:], WG).then_inc(s_smallh, 1)
            for c in range(2, KC):
                square(c)
            act.wait_ge(s_ms, 1)
            nc.scalar.activation(RSTD[:, 1], RSTD[:, 0], ACT.Sqrt).then_inc(s_sd, 1)
            for c in range(KC):
                act.wait_ge(s_z, c // 2 + 1)
                nc.scalar.activation(SQ[:, c], SQ[:, c], ACT.Silu,
                                     scale=M.cols[:, c, TAPS + 1:TAPS + 2]).then_inc(s_y, 1)
                if c % 2 == 1:
                    act.wait_ge(s_y, c + 1)
                    nc.scalar.copy(M.hnT[0][:, c - 1:c + 1], SQ[:, c - 1:c + 1]).then_inc(s_yh, 1)
            st.split_hi(act, 0, NC - 1)

        @block.vector
        def _(dve):
            norm_dve(nc, dve, M, n)
            norm_evac_dve(nc, dve, M, n)
            dve.wait_ge(s_cols, 1)
            dve.wait_ge(s_const, 1)
            v = nc.vector
            ntap = [0]

            def glu(c):
                dve.wait_ge(s_sig, c + 1)
                v.tensor_tensor(U[:, c, TAPS - 1:], M.ps[:, c % GLU_BANKS, 0:SEQ], SIG[:, c % SIGS], ALU.mult
                                ).then_inc(s_glu, 1)

            def multiply_add(c, tap, acc):
                w, u = M.cols[:, c, tap:tap + 1], U[:, c, tap:tap + SEQ]
                if tap == 0:
                    ins = v.tensor_scalar(acc, u, w, M.cols[:, c, TAPS:TAPS + 1], ALU.mult, ALU.add)
                elif tap == 1 and c in DVE_CONV:
                    ins = v.tensor_scalar(acc, u, w, None, ALU.mult)
                else:
                    dve.wait_ge(s_tap, ntap[0] - 1)
                    ins = v.scalar_tensor_tensor(acc, u, w, acc, ALU.mult, ALU.add)
                ins.then_inc(s_tap, 1)
                ntap[0] += 1

            glu(0)
            for i, c in enumerate(DVE_CONV):
                dve.wait_ge(s_glu, c + 1)
                for tap in range(TAPS):
                    multiply_add(c, tap, ACC[:, c + tap % 2])
                glu(c + 1)
                glu(c + 2)
                dve.wait_ge(s_tap, ntap[0])
                v.tensor_tensor(ACC[:, c], ACC[:, c], ACC[:, c + 1], ALU.add).then_inc(s_conv, 1)
            glu(7)
            dve.wait_ge(s_glu, KC)
            for tap in range(TAPS):
                for c in (6, 7):
                    multiply_add(c, tap, ACC[:, c])
            dve.wait_ge(s_tap, ntap[0])
            v.sem_inc(s_conv, 2)
            dve.wait_ge(s_ssum, 1)
            nc.vector.tensor_scalar(RSTD[:, 0], M.ps[:, 6, 0:SEQ], 1.0 / D, EPS, ALU.mult, ALU.add).then_inc(s_ms, 1)
            dve.wait_ge(s_sd, 1)
            nc.vector.reciprocal(RSTD[:, 0], RSTD[:, 1]).then_inc(s_rs, 1)
            dve.wait_ge(s_rs, 1)
            dve.wait_ge(s_cev, len(PE_CONV))
            for p in range(KC // 2):
                cs = slice(2 * p, 2 * p + 2)
                nc.vector.tensor_tensor(SQ[:, cs], ACC[:, cs], RSTD[:, 0].unsqueeze(1).to_broadcast([P, 2, SEQ]),
                                        ALU.mult).then_inc(s_z, 1)
            dve.wait_ge(s_smallh, 2)
            nc.vector.tensor_tensor(M.rw[1][:], RW, M.rw[0][:], ALU.subtract).then_inc(s_smalll, 1)
            nc.vector.tensor_tensor(M.wg[1][:], WG, M.wg[0][:], ALU.subtract).then_inc(s_smalll, 1)
            for p in range(KC // 2):
                cs = slice(2 * p, 2 * p + 2)
                dve.wait_ge(s_yh, p + 1)
                nc.vector.tensor_tensor(M.hnT[1][:, cs], SQ[:, cs], M.hnT[0][:, cs], ALU.subtract).then_inc(s_yl, 1)
            dve.wait_ge(s_out, 1)
            for i in range(4):
                hs = M.h[:, i // 2, (i % 2) * 512:(i % 2 + 1) * 512]
                nc.vector.tensor_tensor(hs, hs, M.ps[:, i, :], ALU.add).then_inc(s_res, 1)

        @block.tensor
        def _(pe):
            pe.sem_inc(st.used, PARTS)
            pe.wait_ge(s_pool, 2)
            pe.wait_ge(s_rows, 16 * 9)
            for k in range(KC):
                pe.transpose(M.ps[:, 7, k * (TAPS + 2):(k + 1) * (TAPS + 2)], ROWS[0:TAPS + 2, k * P:(k + 1) * P],
                             M.ident[0:TAPS + 2, 0:TAPS + 2])
            pe.transpose(M.ps[:, 6, 0:38], ROWS2[0:38, :], M.ident[0:38, 0:38]).then_inc(s_colsT, 1)
            norm_pe(pe, M, n)
            wait_hnT(pe, n)
            for c in range(KC):
                if c >= GLU_BANKS:
                    pe.wait_ge(s_glu, c - GLU_BANKS + 1)
                for ab in range(2):
                    w = st.parts(pe, 0, 2 * (c // 2) + ab, KC)
                    cs = slice((c % 2) * P, (c % 2 + 1) * P)
                    for k in range(KC):
                        mm = mm3(pe, M.ps[:, c % GLU_BANKS, ab * SEQ:(ab + 1) * SEQ], [x[:, k, cs] for x in w],
                                 [x[:, k, :] for x in M.hnT], k == 0, k == KC - 1)
                    if ab == 0 and c % 2 == 1:
                        mm.then_inc(st.used, 1)
                mm.then_inc(s_mm, 1)
                if c % 2 == 1:
                    pe.wait_ge(s_mm, c + 1)
                    pe.sem_inc(st.used, 1)

            def sum_squares(c):
                pe.wait_ge(s_sq, c + 1)
                return pe.matmul(M.ps[:, 6, 0:SEQ], M.ones[:], SQ[:, c], start=(c == 0), stop=(c == KC - 1))

            pe.wait_ge(s_cols, 2)
            for i, c in enumerate(PE_CONV):
                pe.wait_ge(s_glu, c + 1)
                for tap in range(TAPS):
                    k = i * TAPS + tap
                    pe.wait_ge(s_diag, k + 1)
                    mm = pe.matmul(M.ps[:, conv_bank(i), 0:SEQ], DIAG[:, k % DIAGS], U[:, c, tap:tap + SEQ],
                                   start=(tap == 0), stop=(tap == TAPS - 1))
                    mm.then_inc(s_dused if tap < TAPS - 1 else s_cmm, 1)
                    if i == 2 and tap == TAPS // 2:
                        sum_squares(0)
                        sum_squares(1)
                pe.wait_ge(s_cmm, i + 1)
                pe.sem_inc(s_dused, 1)
            for c in range(2, KC):
                mm = sum_squares(c)
            mm.then_inc(s_ssum, 1)
            for p in range(KC // 2):
                pe.wait_ge(s_yl, p + 1)
                mm = out_chunk(pe, M, M.hnT, st.parts(pe, 0, KC + p, 2), p, 0)
                if p == KC // 2 - 1:
                    mm.then_inc(s_out, 1)
                else:
                    mm.then_inc(st.used, 1)


def out_chunk(pe, M, x, w, p, bank):
    for k in range(2):
        for i in range(4):
            c, ns = i // 2, slice((i % 2) * 512, (i % 2 + 1) * 512)
            mm = mm3(pe, M.ps[:, bank + i, :], [t[:, 2 * p + k, c * P:(c + 1) * P] for t in x],
                     [t[:, k, ns] for t in w], p == 0 and k == 0, p == KC // 2 - 1 and k == 1)
    return mm



class MoeSems:

    def __init__(self, sem, tag):
        self.silu = sem(f"{tag}_silu")
        self.gu = sem(f"{tag}_gu_free")
        self.turned = sem(f"{tag}_turned_free")
        self.guT = sem(f"{tag}_guT_free")
        self.gut_hi = sem(f"{tag}_gut_hi")
        self.xg_hi = sem(f"{tag}_xg_hi")
        self.y_out = sem(f"{tag}_yout_free")
        self.gather = sem(f"{tag}_gather")
        self.xg = sem(f"{tag}_xg")
        self.scat, self.res = sem(f"{tag}_scatter"), sem(f"{tag}_residual")


def moe_views(M):
    class V:
        Y = M.at(0, EGROUPS, D)
        S = M.at(4096, EGROUPS, TC, P)
        ST = M.at(5120, EGROUPS, SEQ)
        SIL = M.at(6144, 2, DE)
        GU = M.at(7168, 2, DE)
    return V


def route_phase(nc, M, T, sem, layer, gain, next_gain, next_landed):
    n = NormSems(sem, gain, f"n{layer}")
    V = moe_views(M)
    t = f"r{layer}"
    s_lg, s_sc, s_ch, s_gm, s_rk, s_S, s_St, s_Ste, s_jg = (
        sem(f"{t}_{k}") for k in ("logits", "scores", "chain", "gm", "rank", "S", "S_turned", "ST", "jobgate"))
    tmp = V.SIL.rearrange("p a b -> p (a b)")
    names = {}
    off = [0]

    def small(name, *shape):
        k = 1
        for x in shape:
            k *= x
        v = tmp[:, off[0]:off[0] + k]
        off[0] += k
        if len(shape) == 2:
            v = v.rearrange("p (a b) -> p a b", a=shape[0])
        if len(shape) == 3:
            v = v.rearrange("p (a b c) -> p a b c", a=shape[0], b=shape[1])
        names[name] = v
        return v

    CG = TC * EGROUPS
    score, biased, mb, oh1, oh2, cand = (small(x, TC, EXPERTS) for x in ("score", "biased", "mb", "oh1", "oh2", "cand"))
    hi, lo = small("hi", CG, 2), small("lo", CG, 2)
    top, mn, ml, gs, off1 = (small(x, CG) for x in ("top", "mn", "ml", "gs", "off1"))
    gm, gcand, gr = (small(x, TC, EGROUPS) for x in ("gm", "gcand", "gr"))
    m2 = small("m2", 8, TC)
    cnt, cnt2, of = small("cnt", EGROUPS), small("cnt2", EGROUPS), small("of", 2)

    with nc.Block() as block:
        @block.sync
        def _(sp):
            sp.wait_ge(n.hn, TC)
            if next_gain is not None:
                sp.dma_start(M.gain[:], next_gain.partition_broadcast(P)).then_inc(next_landed, 16)

        @block.scalar
        def _(act):
            norm_act(nc, act, M, n)
            norm_evac_act(nc, act, M, n)
            act.wait_ge(s_lg, 1)
            nc.scalar.activation(score, M.ps[:, 4, 0:TC * EXPERTS].rearrange("p (c e) -> p c e", c=TC),
                                 ACT.Sigmoid).then_inc(s_sc, 1)
            act.wait_ge(s_St, 2)
            nc.scalar.copy(V.ST[:, 0:2], M.ps[:, 0, :].rearrange("p (j t) -> p j t", j=2)).then_inc(s_Ste, 1)
            act.wait_ge(s_jg, 1)
            nc.scalar.copy(M.jgate[:, 0:EGROUPS], M.ps[:, 6, 0:16].rearrange("p (j e) -> p j e", j=EGROUPS)
                           ).then_inc(s_jg, 1)

        @block.vector
        def _(dve):
            norm_dve(nc, dve, M, n)
            norm_evac_dve(nc, dve, M, n)
            v = nc.vector
            ln = Link(dve, s_ch)
            dve.wait_ge(s_sc, 1)
            ln(v.tensor_tensor(biased, score, M.rb[:].unsqueeze(1).to_broadcast([P, TC, EXPERTS]), ALU.add))
            b4 = biased.rearrange("p c (g k) -> p (c g) k", k=EPG)
            v.tensor_tensor(hi, b4[:, :, 0:2], b4[:, :, 2:4], ALU.max).then_inc(s_ch, 1)
            ln.n += 1
            ln(v.tensor_tensor(lo, b4[:, :, 0:2], b4[:, :, 2:4], ALU.min))
            v.tensor_tensor(top, hi[:, :, 0], hi[:, :, 1], ALU.max).then_inc(s_ch, 1)
            v.tensor_tensor(mn, hi[:, :, 0], hi[:, :, 1], ALU.min).then_inc(s_ch, 1)
            ln.n += 2
            ln(v.tensor_tensor(ml, lo[:, :, 0], lo[:, :, 1], ALU.max))
            ln(v.tensor_tensor(mn, mn, ml, ALU.max))
            ln(v.tensor_tensor(gs, top, mn, ALU.add))

            def first_max(values, n_val, m, one_hot, cnd):
                ln(v.tensor_reduce(m[:, 0], values, AX.X, ALU.max))
                ln(v.tensor_tensor(cnd, values, m[:, 0].unsqueeze(2).to_broadcast([P, TC, n_val]), ALU.is_equal))
                ln(v.scalar_tensor_tensor(cnd, cnd, -64.0, M.iota[:, 0:n_val].unsqueeze(1).to_broadcast(
                    [P, TC, n_val]), ALU.mult, ALU.add))
                ln(v.tensor_reduce(m[:, 1], cnd, AX.X, ALU.min))
                ln(v.tensor_tensor(one_hot, cnd, m[:, 1].unsqueeze(2).to_broadcast([P, TC, n_val]), ALU.is_equal))

            first_max(gs.rearrange("p (c g) -> p c g", c=TC), EGROUPS, m2[:, 0:2], gm, gcand)
            dve.sem_inc(s_gm, 1)
            gmf = gm.rearrange("p c g -> p (c g)")
            ln(v.tensor_scalar(off1, gmf, -1.0, -NEG, ALU.add, ALU.mult))
            mb4 = mb.rearrange("p c (g k) -> p (c g) k", k=EPG)
            ln(v.tensor_tensor(mb4, b4, gmf.unsqueeze(2).to_broadcast([P, CG, EPG]), ALU.mult))
            ln(v.tensor_tensor(mb4, mb4, off1.unsqueeze(2).to_broadcast([P, CG, EPG]), ALU.add))
            first_max(mb, EXPERTS, m2[:, 2:4], oh1, cand)
            ln(v.scalar_tensor_tensor(mb, oh1, 2 * NEG, mb, ALU.mult, ALU.add))
            first_max(mb, EXPERTS, m2[:, 4:6], oh2, cand)
            ln(v.tensor_tensor(oh1, oh1, oh2, ALU.add))
            ln(v.tensor_tensor(score, score, oh1, ALU.mult))
            ln(v.tensor_reduce(m2[:, 6], score, AX.X, ALU.add))
            ln(v.reciprocal(m2[:, 7], m2[:, 6]))
            ln(v.tensor_tensor(score, score, m2[:, 7].unsqueeze(2).to_broadcast([P, TC, EXPERTS]), ALU.mult))
            for c in range(TC):
                ln(v.tensor_reduce(M.g4[:, c], score[:, c].rearrange("p (g k) -> p k g", k=EPG), AX.X, ALU.add))
            dve.wait_ge(s_rk, 1)
            rk = M.ps[:, 5, 0:CG].rearrange("p (c g) -> p c g", c=TC)
            ln(v.tensor_tensor(gr, gm, rk, ALU.mult))
            ln(v.tensor_reduce(M.rank[:], gr, AX.X, ALU.add))
            for j in range(EGROUPS):
                for c in range(TC):
                    i = v.tensor_scalar(V.S[:, j, c], M.iota[:], M.rank[:, c:c + 1], gm[:, c, j:j + 1], ALU.is_equal,
                                        ALU.mult)
                i.then_inc(s_S, 1)
            ln(v.tensor_scalar(cnt, M.ps[:, 5, CG:CG + EGROUPS], float(P), None, ALU.is_gt))
            ln(v.tensor_tensor(cnt2, cnt, M.iota[:, 0:EGROUPS], ALU.mult))
            ln(v.tensor_reduce(of[:, 0:1], cnt, AX.X, ALU.add))
            ln(v.tensor_reduce(of[:, 1:2], cnt2, AX.X, ALU.add))
            ln(v.tensor_copy(M.ovf[:], of))
            dve.wait_ge(s_St, 4)
            v.tensor_copy(V.ST[:, 2:4], M.ps[:, 1, :].rearrange("p (j t) -> p j t", j=2)).then_inc(s_Ste, 1)

        @block.tensor
        def _(pe):
            norm_pe(pe, M, n)
            wait_hnT(pe, n)
            for c in range(TC):
                for k in range(KC):
                    mm = mm3(pe, M.ps[:, 4, c * EXPERTS:(c + 1) * EXPERTS],
                             [x[:, k, c * P:(c + 1) * P] for x in M.hnT], [x[:, k, :] for x in M.rw],
                             k == 0, k == KC - 1)
            mm.then_inc(s_lg, 1)
            pe.wait_ge(s_gm, 1)
            B = M.ps[:, 5, :]
            pe.matmul(B[:, 0:4], M.before[:], gm[:, 0], start=True, stop=True)
            pe.matmul(B[:, 4:8], M.ones[:], gm[:, 0], start=True, stop=False)
            pe.matmul(B[:, 4:8], M.before[:], gm[:, 1], start=False, stop=True)
            pe.matmul(B[:, 8:12], M.ones[:], gm[:, 0], start=True, stop=False)
            pe.matmul(B[:, 8:12], M.ones[:], gm[:, 1], start=False, stop=True).then_inc(s_rk, 1)
            for j in range(EGROUPS):
                pe.wait_ge(s_S, j + 1)
                for c in range(TC):
                    mm = pe.transpose(M.ps[:, j // 2, (j % 2) * SEQ + c * P:(j % 2) * SEQ + (c + 1) * P],
                                      V.S[:, j, c], M.ident[:])
                mm.then_inc(s_St, 1)
            for j in range(EGROUPS):
                for c in range(TC):
                    mm = pe.matmul(M.ps[:, 6, j * EPG:(j + 1) * EPG], V.S[:, j, c], M.g4[:, c], start=(c == 0),
                                   stop=(c == TC - 1))
            mm.then_inc(s_jg, 1)


G_BANK, U_BANK, Y_BANK, T_BANK = 0, 2, 4, 6


def pe_gather(pe, M, V, j, half, s, src):
    bank = (G_BANK, U_BANK)[half]
    for k in range(4):
        col = (4 * half + k) * P
        for c in range(TC):
            mm = pe.matmul(M.ps[:, bank, k * P:(k + 1) * P], M.hn[:, c, col:col + P], src(j, c),
                           start=(c == 0), stop=(c == TC - 1))
    mm.then_inc(s.gather, 1)


IDX = {key: i for i, key in enumerate(JOB_ORDER)}


def pe_job(pe, M, V, j, s, st, src, more):
    def product(name, bank, e):
        for x in range(2):
            i = IDX[name, e, x]
            w = st.parts(pe, j, i, 4)
            for k in range(4):
                mm = mm3(pe, M.ps[:, bank + e % 2, :], [t[:, 4 * x + k] for t in M.xg], [t[:, k] for t in w],
                         x == 0 and k == 0, x == 1 and k == 3)
            mm.then_inc(st.used, 1)

    def turn(e):
        E = 4 * j + e
        pe.wait_ge(s.gu, E + 3)
        pe.wait_ge(s.guT, E + 1)
        for k in range(FC):
            mm = pe.transpose(M.ps[:, T_BANK, k * P:(k + 1) * P], V.GU[:, e % 2, k * P:(k + 1) * P], M.ident[:])
        mm.then_inc(s.turned, 1)

    def y(e):
        pe.wait_ge(s.guT, 4 * j + e + 2)
        if e == 0:
            pe.wait_ge(s.y_out, j * 2 + 2)
        for x in range(2):
            w = st.parts(pe, j, IDX["w2", e, x], 2)
            for k in range(2):
                for n in range(2):
                    mm = mm3(pe, M.ps[:, Y_BANK + n, :], [t[:, e % 2, 2 * x + k] for t in M.gut],
                             [t[:, k, n * 512:(n + 1) * 512] for t in w], e == 0 and x == 0 and k == 0,
                             e == EPG - 1 and x == 1 and k == 1)
            mm.then_inc(st.used, 1)

    pe.wait_ge(s.xg, j * 2 + 2)
    for e in range(EPG):
        pe.wait_ge(s.gu, 4 * j + e + 1)
        product("w1", G_BANK, e)
        if e > 0:
            turn(e - 1)
        product("w3", U_BANK, e)
        if e > 0:
            y(e - 1)
    if more:
        pe.wait_ge(s.gu, 4 * j + 5)
        pe_gather(pe, M, V, j + 1, 0, s, src)
    turn(EPG - 1)
    if more:
        pe_gather(pe, M, V, j + 1, 1, s, src)
    y(EPG - 1)


def gathered(M, half):
    return M.ps[:, (G_BANK, U_BANK)[half], :].rearrange("p (k t) -> p k t", k=4)


def act_take_gather(nc, act, M, j, half, s):
    act.wait_ge(s.gather, j * 2 + half + 1)
    nc.scalar.copy(M.xg[0][:, 4 * half:4 * half + 4], gathered(M, half)).then_inc(s.xg_hi, 1)


def dve_take_gather(nc, dve, M, j, half, s):
    dve.wait_ge(s.xg_hi, j * 2 + half + 1)
    ks = slice(4 * half, 4 * half + 4)
    nc.vector.tensor_tensor(M.xg[1][:, ks], gathered(M, half), M.xg[0][:, ks], ALU.subtract).then_inc(s.xg, 1)


def turned(M):
    return M.ps[:, T_BANK, :].rearrange("p (k t) -> p k t", k=FC)


def act_job(nc, act, M, V, j, s, st, ydst, more):
    def take_turned(e):
        act.wait_ge(s.turned, 4 * j + e + 3)
        nc.scalar.copy(M.gut[0][:, e % 2], turned(M)).then_inc(s.gut_hi, 1)

    for i, (w, e, x) in enumerate(JOB_ORDER):
        if (w, x) == ("w1", 1):
            st.wait_used(act, j, i)
            act.wait_ge(s.gu, 4 * j + e + 1)
            nc.scalar.activation(V.SIL[:, e % 2], M.ps[:, G_BANK + e % 2, :], ACT.Silu).then_inc(s.silu, 1)
            if e > 0:
                take_turned(e - 1)
        if (w, e, x) == ("w2", EPG - 2, 1):
            if more:
                act_take_gather(nc, act, M, j + 1, 0, s)
            take_turned(EPG - 1)
            if more:
                act_take_gather(nc, act, M, j + 1, 1, s)
        if i == JOB_CHUNKS - 1:
            st.wait_used(act, j, i)
            nc.scalar.copy(ydst(j)[:, 0:512], M.ps[:, Y_BANK, :]).then_inc(s.y_out, 1)
        if more or i + PARTS < JOB_CHUNKS:
            st.split_hi(act, j, i + PARTS)


def dve_job(nc, dve, M, V, j, s, st, gate, ydst, more):
    def take_turned(e):
        dve.wait_ge(s.gut_hi, 4 * j + e + 1)
        nc.vector.tensor_tensor(M.gut[1][:, e % 2], turned(M), M.gut[0][:, e % 2], ALU.subtract).then_inc(s.guT, 1)

    for i, (w, e, x) in enumerate(JOB_ORDER):
        if (w, x) == ("w1", 1) and e > 0:
            take_turned(e - 1)
        if (w, x) == ("w3", 1):
            E = 4 * j + e
            dve.wait_ge(s.silu, E + 1)
            st.wait_used(dve, j, i)
            dve.wait_ge(s.turned, E + 1)
            nc.vector.scalar_tensor_tensor(V.GU[:, e % 2], M.ps[:, U_BANK + e % 2, :], gate(j, e), V.SIL[:, e % 2],
                                           ALU.mult, ALU.mult).then_inc(s.gu, 1)
        if (w, e, x) == ("w2", EPG - 2, 1):
            if more:
                dve_take_gather(nc, dve, M, j + 1, 0, s)
            take_turned(EPG - 1)
            if more:
                dve_take_gather(nc, dve, M, j + 1, 1, s)
        if i == JOB_CHUNKS - 1:
            st.wait_used(dve, j, i)
            nc.vector.tensor_copy(ydst(j)[:, 512:1024], M.ps[:, Y_BANK + 1, :]).then_inc(s.y_out, 1)
        if more or i + PARTS < JOB_CHUNKS:
            st.split_lo(dve, j, i + PARTS)


def credits(eng, *pairs):
    for s, n in pairs:
        eng.sem_inc(s, n)


def jobs_phase(nc, M, T, sem, layer, st, nxt, ahead):
    s = MoeSems(sem, f"m{layer}")
    V = moe_views(M)
    JL = EGROUPS - 1

    def src(j, c):
        if isinstance(j, int):
            return V.S[:, j, c]
        return V.S[:, bass.ds(j, 1), c].rearrange("p o t -> p (o t)")

    def gate(j, e):
        g = M.jgate[:].rearrange("p j e -> p (j e)")
        return g[:, 4 * j + e:4 * j + e + 1] if isinstance(j, int) else g[:, bass.ds(j * 4 + e, 1)]

    def first_act(act):
        for i in range(PARTS):
            st.split_hi(act, 0, i)
        for half in range(2):
            act_take_gather(nc, act, M, 0, half, s)

    def first_dve(dve):
        for i in range(PARTS):
            st.split_lo(dve, 0, i)
        for half in range(2):
            dve_take_gather(nc, dve, M, 0, half, s)

    def ydst(j):
        return V.Y[:, j] if isinstance(j, int) else V.Y[:, bass.ds(j, 1)].rearrange("p o d -> p (o d)")

    with nc.Block() as block:
        @block.sync
        def _(sp):
            def job(j):
                for i in range(JOB_CHUNKS):
                    st.wait_raw_free(sp, j, i)
                    if i + RAWS < JOB_CHUNKS:
                        st.load(sp, i, job_chunk(T, layer, j * EPG, i + RAWS))
                    elif j is not JL:
                        st.load(sp, i, job_chunk(T, layer, (j + 1) * EPG, i + RAWS - JOB_CHUNKS))
                    elif ahead:
                        k = i + RAWS - JOB_CHUNKS
                        nxt.load(sp, k, ahead[k])

            with sp.Fori(0, JL) as j:
                job(j)
            job(JL)

        @block.tensor
        def _(pe):
            credits(pe, (s.turned, 2), (st.used, PARTS))
            pe_gather(pe, M, V, 0, 0, s, src)
            pe_gather(pe, M, V, 0, 1, s, src)
            with pe.Fori(0, JL) as j:
                pe_job(pe, M, V, j, s, st, src, True)
            pe_job(pe, M, V, JL, s, st, src, False)
            pe.wait_ge(s.gu, EXPERTS + 2)
            pe.wait_ge(s.y_out, 2 * EGROUPS + 2)
            for i in range(4):
                for j in range(EGROUPS):
                    mm = pe.matmul(M.ps[:, i, :], V.ST[:, j, (i // 2) * P:(i // 2 + 1) * P],
                                   V.Y[:, j, (i % 2) * 512:(i % 2 + 1) * 512], start=(j == 0),
                                   stop=(j == EGROUPS - 1))
                mm.then_inc(s.scat, 1)

        @block.scalar
        def _(act):
            credits(act, (s.guT, 1))
            first_act(act)
            with act.Fori(0, JL) as j:
                act_job(nc, act, M, V, j, s, st, ydst, True)
            act_job(nc, act, M, V, JL, s, st, ydst, False)

        @block.vector
        def _(dve):
            credits(dve, (s.gu, 2), (s.y_out, 2))
            first_dve(dve)
            with dve.Fori(0, JL) as j:
                dve_job(nc, dve, M, V, j, s, st, gate, ydst, True)
            dve_job(nc, dve, M, V, JL, s, st, gate, ydst, False)
            for i in range(4):
                dve.wait_ge(s.scat, i + 1)
                hs = M.h[:, i // 2, (i % 2) * 512:(i % 2 + 1) * 512]
                nc.vector.tensor_tensor(hs, hs, M.ps[:, i, :], ALU.add).then_inc(s.res, 1)


def overflow_phase(nc, M, T, sem, layer, st, after):
    V = moe_views(M)
    t = f"o{layer}"
    s = MoeSems(sem, f"v{layer}")
    s_S, s_St, s_prep, s_ge = sem(f"{t}_S"), sem(f"{t}_ST"), sem(f"{t}_prep"), sem(f"{t}_gate")
    group_max = EGROUPS - 1

    def src(j, c):
        return V.S[:, 0, c]

    def gate(j, e):
        return M.jgate[:, 4, e:e + 1]

    def ydst(j):
        return V.Y[:, 0]

    def when(eng, body):
        n = eng.value_load(M.ovf[0:1, 0:1], min_val=0, max_val=1)
        with eng.If(n > 0):
            body(eng)
        eng.end_ifs()

    with nc.Block() as block:
        @block.sync
        def _(sp):
            g = sp.value_load(M.ovf[0:1, 1:2], min_val=0, max_val=group_max)

            def body(sp):
                if after is not None:
                    after[0](sp)
                for i in range(RAWS):
                    st.load(sp, i, job_chunk(T, layer, g * EPG, i))
                for i in range(JOB_CHUNKS - RAWS):
                    st.wait_raw_free(sp, 0, i)
                    st.load(sp, i, job_chunk(T, layer, g * EPG, i + RAWS))
                if after is not None:
                    st.wait_raw_free(sp, 0, JOB_CHUNKS - 1)
                    after[1](sp)

            when(sp, body)

        @block.tensor
        def _(pe):
            def body(pe):
                credits(pe, (s.turned, 2), (st.used, PARTS))
                pe.wait_ge(s_S, TC)
                for c in range(TC):
                    pe.transpose(M.ps[:, T_BANK, c * P:(c + 1) * P], V.S[:, 0, c], M.ident[:])
                for c in range(TC):
                    mm = pe.matmul(M.ps[:, 7, 0:EPG], V.S[:, 0, c], M.g4[:, c], start=(c == 0), stop=(c == TC - 1))
                mm.then_inc(s_St, 1)
                pe_gather(pe, M, V, 0, 0, s, src)
                pe_gather(pe, M, V, 0, 1, s, src)
                pe.wait_ge(s_prep, 2)
                pe_job(pe, M, V, 0, s, st, src, False)
                pe.wait_ge(s.gu, EPG + 2)
                pe.wait_ge(s.y_out, 4)
                for i in range(4):
                    pe.matmul(M.ps[:, i, :], V.ST[:, 0, (i // 2) * P:(i // 2 + 1) * P],
                              V.Y[:, 0, (i % 2) * 512:(i % 2 + 1) * 512], start=True, stop=True).then_inc(s.scat, 1)

            when(pe, body)

        @block.scalar
        def _(act):
            def body(act):
                credits(act, (s.guT, 1))
                act.wait_ge(s_St, 1)
                nc.scalar.copy(V.ST[:, 0], M.ps[:, T_BANK, 0:SEQ]).then_inc(s_prep, 1)
                nc.scalar.copy(M.jgate[:, 4], M.ps[:, 7, 0:EPG]).then_inc(s_prep, 1)
                for i in range(PARTS):
                    st.split_hi(act, 0, i)
                for half in range(2):
                    act_take_gather(nc, act, M, 0, half, s)
                act_job(nc, act, M, V, 0, s, st, ydst, False)

            when(act, body)

        @block.vector
        def _(dve):
            def body(dve):
                credits(dve, (s.gu, 2), (s.y_out, 2))
                nc.vector.tensor_scalar(M.stat[:, 0:TC], M.rank[:], float(-P), None, ALU.add).then_inc(s_ge, 1)
                dve.wait_ge(s_ge, 1)
                for c in range(TC):
                    nc.vector.tensor_scalar(V.S[:, 0, c], M.iota[:], M.stat[:, c:c + 1], None,
                                            ALU.is_equal).then_inc(s_S, 1)
                for i in range(PARTS):
                    st.split_lo(dve, 0, i)
                for half in range(2):
                    dve_take_gather(nc, dve, M, 0, half, s)
                dve.wait_ge(s_prep, 2)
                dve_job(nc, dve, M, V, 0, s, st, gate, ydst, False)
                for i in range(4):
                    dve.wait_ge(s.scat, i + 1)
                    hs = M.h[:, i // 2, (i % 2) * 512:(i % 2 + 1) * 512]
                    nc.vector.tensor_tensor(hs, hs, M.ps[:, i, :], ALU.add).then_inc(s.res, 1)

            when(dve, body)



KV = 0
KCT = KT0 = 3072
QT = SQQ = 4096
Q = BLK = SC = 6144
PTC = 7168
X2 = GAIN2 = PTB = 8192
KT1 = 9216
VCBD = SQK = 10240
KCMPT, HIDK, HIDV, HIDVP, KCN, STATS = 11264, 11392, 11456, 11520, 12032, 12160
CST, SMALL = HIDK, STATS

KV_CHUNKS, Q_CHUNKS, PHI_CHUNKS = 6, 4, 2
LAST_SPLIT = KV_CHUNKS + Q_CHUNKS + PARTS


def attention_loads_after(sp, st, nxt, chunks, ahead, first, end):
    for i in range(first, end):
        st.wait_raw_free(sp, 0, i)
        k = i + RAWS
        if k < len(chunks):
            st.load(sp, k, chunks[k])
        else:
            nxt.load(sp, k - len(chunks), ahead[k - len(chunks)])


def project_phase(nc, M, T, sem, st, nxt, chunks, ahead, gain):
    n = NormSems(sem, gain, "np")
    s_g2, s_tp2, s_gates = sem("gain2_in"), sem("turned2"), sem("gates_mm")
    s_ev2 = [sem("hnT2_hi"), sem("hnT2_lo")]
    s_out = [sem("proj_act"), sem("proj_dve")]
    kv = M.at(KV, TC, 3, 512)
    q = M.at(Q, TC, 2, 512)
    dst = [(kv, b) for b in range(3)] + [(q, b) for b in range(2)]
    BANKS = [4, 6, 0, 6, 0]
    TURN2, GATES = 2, 4

    def turn2_bank(b):
        return M.ps[:, TURN2 + b, :].rearrange("p (k t) -> p k t", k=2)

    with nc.Block() as block:
        @block.sync
        def _(sp):
            sp.dma_start(M.at(GAIN2, D), T["b_norm"][0].partition_broadcast(P)).then_inc(s_g2, 16)
            attention_loads_after(sp, st, nxt, chunks, ahead, 0, LAST_SPLIT)

        @block.scalar
        def _(act):
            norm_act(nc, act, M, n)
            for i in range(PARTS):
                st.split_hi(act, 0, i)
            norm_evac_act(nc, act, M, n)
            for i in range(KV_CHUNKS + Q_CHUNKS):
                if i % 2 == 1:
                    st.wait_used(act, 0, i)
                    x, b = dst[i // 2]
                    nc.scalar.copy(x[:, 0, b], M.ps[:, BANKS[i // 2], :]).then_inc(s_out[0], 1)
                if i == KV_CHUNKS - 1:
                    for b in range(4):
                        act.wait_ge(s_tp2, b + 1)
                        nc.scalar.copy(part(M.hnT[0], b), turn2_bank(b)).then_inc(s_ev2[0], 1)
                st.split_hi(act, 0, i + PARTS)
            act.wait_ge(s_gates, 1)
            nc.scalar.activation(M.gates[:], M.ps[:, GATES, 0:TC * 3 * HEADS].rearrange("p (c n) -> p c n", c=TC),
                                 ACT.Sigmoid).then_inc(s_out[0], 1)

        @block.vector
        def _(dve):
            v = nc.vector
            norm_dve(nc, dve, M, n)
            for i in range(PARTS):
                st.split_lo(dve, 0, i)
            norm_evac_dve(nc, dve, M, n)
            dve.wait_ge(s_g2, 16)
            dve.wait_ge(n.tp, 4)
            for c in range(TC):
                v.scalar_tensor_tensor(M.hn[:, c, :], M.h[:, c, :], M.stat[:, 6 + c:7 + c], M.at(GAIN2, D),
                                       ALU.mult, ALU.mult).then_inc(n.hn, 1)
            for i in range(KV_CHUNKS + Q_CHUNKS):
                if i % 2 == 1:
                    st.wait_used(dve, 0, i)
                    x, b = dst[i // 2]
                    v.tensor_copy(x[:, 1, b], M.ps[:, BANKS[i // 2] + 1, :]).then_inc(s_out[1], 1)
                if i == KV_CHUNKS - 1:
                    for b in range(4):
                        dve.wait_ge(s_ev2[0], b + 1)
                        v.tensor_tensor(part(M.hnT[1], b), turn2_bank(b), part(M.hnT[0], b), ALU.subtract
                                        ).then_inc(s_ev2[1], 1)
                st.split_lo(dve, 0, i + PARTS)

        @block.tensor
        def _(pe):
            pe.sem_inc(st.used, PARTS)
            norm_pe(pe, M, n)
            wait_hnT(pe, n)
            for b in range(5):
                if b >= 3:
                    for x in s_out:
                        pe.wait_ge(x, b - 1)
                if b == 3:
                    pe.wait_ge(n.hn, 2 * TC)
                    for x in range(4):
                        for kk in range(2):
                            for c in range(TC):
                                k = 2 * x + kk
                                mm = pe.transpose(M.ps[:, TURN2 + x, kk * SEQ + c * P:kk * SEQ + (c + 1) * P],
                                                  M.hn[:, c, k * P:(k + 1) * P], M.ident[:])
                        mm.then_inc(s_tp2, 1)
                    pe.wait_ge(s_ev2[1], 4)
                for x in range(2):
                    w = st.parts(pe, 0, 2 * b + x, 4)
                    for c in range(TC):
                        for k in range(4):
                            mm = mm3(pe, M.ps[:, BANKS[b] + c, :],
                                     [t[:, 4 * x + k, c * P:(c + 1) * P] for t in M.hnT], [t[:, k] for t in w],
                                     x == 0 and k == 0, x == 1 and k == 3)
                    mm.then_inc(st.used, 1)
            for c in range(TC):
                for k in range(KC):
                    mm = mm3(pe, M.ps[:, GATES, c * 48:(c + 1) * 48], [t[:, k, c * P:(c + 1) * P] for t in M.hnT],
                             [t[:, k, :] for t in M.wg], k == 0, k == KC - 1)
            mm.then_inc(s_gates, 1)


def prep_phase(nc, M, T, sem, st, nxt, chunks, ahead, next_gain):
    kv = M.at(KV, TC, 6, 256)
    q = M.at(Q, TC, D)
    qn = M.hn[:].rearrange("p c (a n) -> p c a n", a=2)
    sqk, sqq = M.at(SQK, 2, TC, 256), M.at(SQQ, TC, D)
    sts = M.at(STATS, 3, 48)
    kcT = M.at(KCT, 2, 2, SEQ)
    x2 = M.at(X2, 2, GROUPS, SEQ)
    blk = M.at(BLK, 2, 16, GROUPS * NCMP)
    B60 = 16 * GROUPS * NCMP
    blk_parts = [[t[:].rearrange("p k t -> p (k t)")[:, 0:B60].rearrange("p (j n) -> p j n", j=16) for t in M.xg],
                 [t[:].rearrange("p a k t -> p (a k t)")[:, 0:B60].rearrange("p (j n) -> p j n", j=16)
                  for t in M.gut]]
    kT = [M.at(KT0, 2, 2, SEQ), M.at(KT1, 2, 2, SEQ)]
    qT = M.at(QT, KC, SEQ)
    hidk, hidv = M.at(HIDK, 60), M.at(HIDV, GROUPS, NCMP)
    hidvp = M.at(HIDVP, GROUPS, HPG, CPAD)
    kcn, kcmpT = M.at(KCN, 2, DH), M.at(KCMPT, GROUPS, CPAD)
    vcbd = M.at(VCBD, GROUPS, HPG, DH)
    first_phi = KV_CHUNKS + Q_CHUNKS
    names = ("kcT_mm", "kn_mm", "qn_mm", "kcT_a", "kcT_d", "x2_in", "blk", "hid_mm", "hidk", "hidv", "hidvp",
             "kc_mm", "kc_sq", "kc_ms", "kc_sd", "kcn", "kcT2_mm", "vc_mm", "sq", "ssum", "std", "rstd", "kn", "qn",
             "kT", "qT_a", "qT_d", "pads", "ch", "end", "colq", "blk_hi", "blk_lo")
    S = {k: sem("p_" + k) for k in names}

    with nc.Block() as block:
        @block.sync
        def _(sp):
            sp.wait_ge(S["kcT_a"], 1)
            sp.wait_ge(S["kcT_d"], 1)
            for g2 in range(2):
                for l2 in range(2):
                    dst = x2[DH * l2:DH * (l2 + 1)].rearrange("p i (a b) t -> p i a b t", b=2)[:, :, :, g2]
                    for i in range(2):
                        sp.dma_start(dst[:, i, :, 0:SEQ - l2], kcT[DH * g2:DH * (g2 + 1), i, :, l2:SEQ]
                                     ).then_inc(S["x2_in"], 16)
            sp.dma_start(M.gain[:], T["ffn_norm"][1].partition_broadcast(P)).then_inc(next_gain, 16)
            attention_loads_after(sp, st, nxt, chunks, ahead, LAST_SPLIT, LAST_SPLIT + PHI_CHUNKS)
            sp.wait_ge(S["x2_in"], 16 * 8)

        @block.gpsimd
        def _(pool):
            fill = Link(pool, S["pads"])
            fill(nc.gpsimd.memset(M.at(HIDVP, 512), 0.0))
            fill(nc.gpsimd.memset(M.at(KCMPT, 128), 0.0))
            pool.wait_ge(S["ssum"], 1)
            fill(nc.gpsimd.memset(M.at(VCBD, 1024), 0.0))
            pool.wait_ge(S["x2_in"], 16 * 8)
            fill(nc.gpsimd.memset(kT[0][DH:P], 0.0))
            pool.wait_ge(S["blk"], 4)
            fill(nc.gpsimd.memset(kT[1][0:DH], 0.0))

        @block.tensor
        def _(pe):
            B = M.ps
            for i in range(2):
                for a in range(2):
                    for c in range(TC):
                        mm = pe.transpose(B[:, i, a * SEQ + c * P:a * SEQ + (c + 1) * P],
                                          kv[:, c, i, a * P:(a + 1) * P], M.ident[:])
                mm.then_inc(S["kcT_mm"], 1)
            pe.wait_ge(S["kn"], 2)
            for i in range(2):
                for a in range(2):
                    for c in range(TC):
                        mm = pe.transpose(B[:, 2 + i, a * SEQ + c * P:a * SEQ + (c + 1) * P],
                                          kv[:, c, 2 + 2 * i, a * P:(a + 1) * P], M.ident[:])
                mm.then_inc(S["kn_mm"], 1)
            pe.wait_ge(S["qn"], 4)
            for b in range(4):
                for kk in range(2):
                    for c in range(TC):
                        a, r = (2 * b + kk) // HPG, (2 * b + kk) % HPG
                        mm = pe.transpose(B[:, 4 + b, kk * SEQ + c * P:kk * SEQ + (c + 1) * P],
                                          qn[:, c, a, r * P:(r + 1) * P], M.ident[:])
                mm.then_inc(S["qn_mm"], 1)
            pe.wait_ge(S["kcT_a"], 1)
            pe.wait_ge(S["kcT_d"], 1)
            for i in range(2):
                pe.wait_ge(S["blk_lo"], i + 1)
                phi = st.parts(pe, 0, first_phi + i, 16)
                for j in range(16):
                    mm = mm3(pe, B[:, i, 0:60], [t[:, j] for t in phi], [t[:, j] for t in blk_parts[i]], j == 0,
                             j == 15)
                mm.then_inc(st.used, 1)
            pe.wait_ge(S["kT"], 4)
            pe.wait_ge(S["hidk"], 1)
            pe.matmul(B[0:60, 2, 0:DH], hidk, M.phi2[:, 0], start=True, stop=True).then_inc(S["kc_mm"], 1)
            pe.wait_ge(S["hidvp"], HPG)
            for g in range(GROUPS):
                mm = pe.matmul(B[:, 3, g * DH:(g + 1) * DH], hidvp[:, g].rearrange("p r n -> p (r n)"),
                               M.phi2[:, 1], start=True, stop=True)
            mm.then_inc(S["vc_mm"], 1)
            pe.wait_ge(S["qT_a"], 2)
            pe.wait_ge(S["qT_d"], 2)
            for i in range(CLOCK_UP):
                pe.matmul(B[:, 5], M.ident[:], qT[:, 0:2].rearrange("p k t -> p (k t)"), start=True, stop=True)
            pe.wait_ge(S["kcn"], 2)
            pe.transpose(B[:, 0, 0:60], kcn[0:60].rearrange("p a d -> p (a d)"), M.ident[0:60, 0:60]
                         ).then_inc(S["kcT2_mm"], 1)

        @block.scalar
        def _(act):
            a = nc.scalar
            act.wait_ge(S["kcT_mm"], 1)
            a.copy(kcT[:, 0], bank_pair(M, 0)).then_inc(S["kcT_a"], 1)
            for i in range(2):
                a.activation(sqk[:, i], kv[:, :, 2 + 2 * i], ACT.Square).then_inc(S["sq"], 1)
            a.activation(sqq, q, ACT.Square).then_inc(S["sq"], 1)
            act.wait_ge(S["ssum"], 1)
            a.activation(sts[:, 1], sts[:, 0], ACT.Sqrt).then_inc(S["std"], 1)
            act.wait_ge(S["kn_mm"], 1)
            act.wait_ge(S["x2_in"], 16 * 8)
            for i in range(2):
                act.wait_ge(S["kn_mm"], i + 1)
                a.activation(kT[0][0:DH, i], bank_pair(M, 2 + i)[0:DH], ACT.Copy, scale=M.cols2[0:DH, 33 + i:34 + i]
                             ).then_inc(S["kT"], 1)
            act.wait_ge(S["colq"], 1)
            for i in range(2):
                act.wait_ge(S["blk"], 2 * (i + 1))
                a.copy(blk_parts[i][0], blk[:, i]).then_inc(S["blk_hi"], 1)
            for b in (0, 2):
                act.wait_ge(S["qn_mm"], b + 1)
                a.activation(part(qT, b), bank_pair(M, 4 + b), ACT.Copy, scale=M.stat[:, 0:1]
                             ).then_inc(S["qT_a"], 1)
            for i in range(LAST_SPLIT, LAST_SPLIT + PHI_CHUNKS):
                st.split_hi(act, 0, i)
            st.wait_used(act, 0, first_phi)
            a.activation(hidk, M.ps[:, 0, 0:60], ACT.Gelu_apprx_tanh, bias=M.cols2[:, 36:37]).then_inc(S["hidk"], 1)
            st.wait_used(act, 0, first_phi + 1)
            a.activation(hidv.rearrange("p g n -> p (g n)"), M.ps[:, 1, 0:60], ACT.Gelu_apprx_tanh,
                         bias=M.cols2[:, 37:38]).then_inc(S["hidv"], 1)
            act.wait_ge(S["kc_mm"], 1)
            act.wait_ge(S["kn_mm"], 2)
            a.activation(kcn[0:60, 0], M.ps[0:60, 2, 0:DH], ACT.Square, accum_out=M.stat[0:60, 1:2]
                         ).then_inc(S["kc_sq"], 1)
            act.wait_ge(S["kc_ms"], 1)
            a.activation(M.stat[0:60, 3:4], M.stat[0:60, 2:3], ACT.Sqrt).then_inc(S["kc_sd"], 1)

        @block.vector
        def _(dve):
            v = nc.vector
            ln = Link(dve, S["ch"])
            dve.wait_ge(S["kcT_mm"], 2)
            v.tensor_copy(kcT[:, 1], bank_pair(M, 1)).then_inc(S["kcT_d"], 1)
            v.tensor_scalar(M.stat[:, 0:1], M.cols2[:, 35:36], DH ** -0.5, None, ALU.mult).then_inc(S["colq"], 1)
            dve.wait_ge(S["sq"], 3)
            ln(v.tensor_reduce(sts[:, 0, 0:16], sqk.rearrange("p i c (g d) -> p (i c g) d", d=DH), AX.X, ALU.add))
            ln(v.tensor_reduce(sts[:, 0, 16:48], sqq.rearrange("p c (h d) -> p (c h) d", d=DH), AX.X, ALU.add))
            v.tensor_scalar(sts[:, 0], sts[:, 0], 1.0 / DH, EPS, ALU.mult, ALU.add).then_inc(S["ssum"], 1)
            dve.wait_ge(S["std"], 1)
            ln(v.reciprocal(sts[:, 2], sts[:, 1]))
            for i in range(2):
                r = sts[:, 2, 8 * i:8 * i + 8].rearrange("p (c g) -> p c g", c=TC)
                k_i = kv[:, :, 2 + 2 * i].rearrange("p c (g d) -> p c g d", d=DH)
                v.tensor_tensor(k_i, k_i,
                                r.unsqueeze(3).to_broadcast([P, TC, GROUPS, DH]), ALU.mult).then_inc(S["kn"], 1)
            for c in range(TC):
                for pr in range(2):
                    r = sts[:, 2, 16 + 16 * c + 8 * pr:24 + 16 * c + 8 * pr].rearrange("p (g r) -> p g r", g=2)
                    v.tensor_tensor(qn[:, c, pr].rearrange("p (r g d) -> p g r d", g=2, d=DH),
                                    q[:, c, pr * 512:(pr + 1) * 512].rearrange("p (g r d) -> p g r d", g=2, d=DH),
                                    r.unsqueeze(3).to_broadcast([P, 2, HPG, DH]), ALU.mult).then_inc(S["qn"], 1)
            dve.wait_ge(S["qn"], 4)
            dve.wait_ge(S["x2_in"], 16 * 8)
            for i in range(2):
                for hj in range(2):
                    win = x2[:, i, :, 16 * hj:16 * hj + 240].rearrange("p g (n j x) -> p j g n x", j=8, x=2)
                    for g in range(GROUPS):
                        pe_col = M.cols2[:, 16 * i + 8 * hj:16 * i + 8 * hj + 8]
                        o = v.tensor_tensor(blk[:, i, 8 * hj:8 * hj + 8, g * NCMP:(g + 1) * NCMP], win[:, :, g, :, 0],
                                            pe_col.unsqueeze(2).to_broadcast([P, 8, NCMP]), ALU.add)
                    o.then_inc(S["blk"], 1)
            for i in range(2):
                dve.wait_ge(S["blk_hi"], i + 1)
                v.tensor_tensor(blk_parts[i][1], blk[:, i], blk_parts[i][0], ALU.subtract).then_inc(S["blk_lo"], 1)
            dve.wait_ge(S["kn_mm"], 2)
            dve.wait_ge(S["blk"], 4)
            for i in range(2):
                v.tensor_scalar(kT[1][DH:P, i], bank_pair(M, 2 + i)[DH:P], M.cols2[DH:P, 33 + i:34 + i], None,
                                ALU.mult).then_inc(S["kT"], 1)
            for b in (1, 3):
                dve.wait_ge(S["qn_mm"], b + 1)
                v.tensor_scalar(part(qT, b), bank_pair(M, 4 + b), M.stat[:, 0:1], None, ALU.mult
                                ).then_inc(S["qT_d"], 1)
            for i in range(LAST_SPLIT, LAST_SPLIT + PHI_CHUNKS):
                st.split_lo(dve, 0, i)
            dve.wait_ge(S["pads"], 5)
            dve.wait_ge(S["hidv"], 1)
            for r in range(HPG):
                v.tensor_copy(hidvp[:, :, r, 0:NCMP], hidv).then_inc(S["hidvp"], 1)
            dve.wait_ge(S["kc_sq"], 1)
            v.tensor_scalar(M.stat[0:60, 2:3], M.stat[0:60, 1:2], 1.0 / DH, EPS, ALU.mult, ALU.add
                            ).then_inc(S["kc_ms"], 1)
            dve.wait_ge(S["kc_sd"], 1)
            ln(v.reciprocal(M.stat[0:60, 4:5], M.stat[0:60, 3:4]))
            for x in range(2):
                v.tensor_scalar(kcn[0:60, x], M.ps[0:60, 2, 0:DH], M.stat[0:60, 4:5], None, ALU.mult
                                ).then_inc(S["kcn"], 1)
            dve.wait_ge(S["vc_mm"], 1)
            for r in range(HPG):
                rs = slice(CPAD * r, CPAD * (r + 1))
                v.tensor_copy(vcbd[rs, :, r], M.ps[rs, 3, 0:256].rearrange("p (g d) -> p g d", d=DH)
                              ).then_inc(S["end"], 1)
            dve.wait_ge(S["kcT2_mm"], 1)
            for g2 in range(2):
                hs = slice(DH * g2, DH * (g2 + 1))
                v.tensor_scalar(kcmpT[hs].rearrange("p (a b) n -> p a b n", b=2)[:, :, g2, 0:NCMP],
                                M.ps[hs, 0, 0:60].rearrange("p (a b n) -> p a b n", a=2, b=2)[:, :, g2],
                                M.cols2[hs, 32:33], None, ALU.mult).then_inc(S["end"], 1)


def attend_phase(nc, M, T, sem, st, nxt, chunks, ahead):
    kv = M.at(KV, TC, 6, 256)
    qT, kT = M.at(QT, KC, SEQ), [M.at(KT0, 2, 2, SEQ), M.at(KT1, 2, 2, SEQ)]
    kcmpT, vcbd = M.at(KCMPT, GROUPS, CPAD), M.at(VCBD, GROUPS, HPG * DH)
    sc = M.at(SC, TC, HEADS, CPAD)
    ptc = M.at(PTC, TC, GROUPS, P)
    hnf = M.hn[:].rearrange("p c d -> p (c d)")
    pb = hnf[:, 0:1536].rearrange("p (n b k) -> p n b k", n=3, b=2)
    ptb = M.at(PTB, 2, 4, P)
    o, oT = M.hn, M.hnT
    cst = M.at(CST, 8, 32)
    nm, sm, gr = (M.at(SMALL + 64 * i, 32, 2) for i in range(3))
    N = TC * HEADS
    names = ("c_mm", "c_ch", "c_exp", "c_p", "c_tp", "c_ev", "s_mm", "max", "exp", "scaled", "t_mm", "pt", "pv",
             "o_ev", "o_tp", "oT_a", "oT_d", "out", "res", "sm_ch", "wl")
    S = {k: sem("a_" + k) for k in names}
    W0 = KV_CHUNKS + Q_CHUNKS + PHI_CHUNKS
    SCORE, TURN = 4, 6
    COMPRESSED = 6

    def where(h):
        g, r = h // HPG, h % HPG
        return g, (g // 2) * HPG + r, g // 2

    with nc.Block() as block:
        @block.sync
        def _(sp):
            attention_loads_after(sp, st, nxt, chunks, ahead, LAST_SPLIT + PHI_CHUNKS, len(chunks))

        @block.tensor
        def _(pe):
            B = M.ps
            for c in range(TC):
                for pair in range(KC):
                    a = pair // HPG
                    mm = pe.matmul(B[:, TURN + c, pair * 2 * CPAD:(pair + 1) * 2 * CPAD],
                                   qT[:, pair, c * P:(c + 1) * P],
                                   kcmpT[:, 2 * a:2 * a + 2].rearrange("p g n -> p (g n)"), start=True, stop=True)
                mm.then_inc(S["c_mm"], 1)

            def scores(n):
                c, h = n // HEADS, n % HEADS
                g, pair, a = where(h)
                nk = P * (c + 1)
                if n >= 2:
                    pe.wait_ge(S["exp"], 2 * (n - 1))
                bank = B[:, SCORE + n % 2, :].rearrange("p (b k) -> p b k", b=2)
                pe.matmul(bank[:, :, 0:nk], qT[:, pair, c * P:(c + 1) * P], kT[g % 2][:, :, a, 0:nk], start=True,
                          stop=False)
                pe.matmul(bank[:, :, nk - P:nk], M.identb[:], M.causal[:].unsqueeze(1).to_broadcast([P, 2, P]),
                          start=False, stop=True).then_inc(S["s_mm"], 1)

            def turn(n):
                c = n // HEADS
                pe.wait_ge(S["scaled"], 2 * (n + 1))
                if n >= 2:
                    pe.wait_ge(S["pt"], n - 1)
                else:
                    pe.wait_ge(S["c_ch"], 4)
                if n > COMPRESSED:
                    pe.wait_ge(S["c_ev"], TC)
                for kc in range(c + 1):
                    for b in range(2):
                        x = 2 * kc + b
                        mm = pe.transpose(B[:, TURN + n % 2, x * P:(x + 1) * P],
                                          pb[:, n % 3, b, kc * P:(kc + 1) * P], M.ident[:])
                mm.then_inc(S["t_mm"], 1)

            def values(n):
                c, h = n // HEADS, n % HEADS
                pe.wait_ge(S["pt"], n + 1)
                for kc in range(c + 1):
                    for b in range(2):
                        mm = pe.matmul(B[:, 2 * c + h // 8, (h % 8) * DH:(h % 8 + 1) * DH], ptb[:, n % 2, 2 * kc + b],
                                       kv[:, kc, 3 + 2 * b, (h // HPG) * DH:(h // HPG + 1) * DH],
                                       start=(h % 8 == 0 and kc == 0 and b == 0), stop=False, skip_group_check=True)
                mm.then_inc(S["pv"], 1)

            for n in range(N + 3):
                if n < N:
                    scores(n)
                if 2 <= n < N + 2:
                    turn(n - 2)
                if n >= 3:
                    values(n - 3)
                if n == COMPRESSED + 2:
                    pe.wait_ge(S["c_p"], TC)
                    pe.wait_ge(S["pt"], COMPRESSED + 1)
                    for c in range(TC):
                        for g in range(GROUPS):
                            mm = pe.transpose(B[:, TURN + c, g * P:(g + 1) * P], sc[:, c, g * HPG:(g + 1) * HPG
                                              ].rearrange("p r n -> p (r n)"), M.ident[:])
                        mm.then_inc(S["c_tp"], 1)
            for c in range(TC):
                for g in range(GROUPS):
                    mm = pe.matmul(B[:, 2 * c + g // 2, (g % 2) * 256:(g % 2 + 1) * 256], ptc[:, c, g], vcbd[:, g],
                                   start=False, stop=(g % 2 == 1), skip_group_check=True)
            mm.then_inc(S["pv"], 1)
            pe.wait_ge(S["o_ev"], 4)
            for b in range(4):
                turn_pe(pe, M, b, o).then_inc(S["o_tp"], 1)
            pe.wait_ge(S["oT_d"], 4)
            for p in range(KC // 2):
                mm = out_chunk(pe, M, oT, st.parts(pe, 0, W0 + p, 2), p, 4)
                mm.then_inc(st.used if p < KC // 2 - 1 else S["out"], 1)

        @block.scalar
        def _(act):
            a = nc.scalar
            for n in range(N + 2):
                if n < N:
                    nk = P * (n // HEADS + 1)
                    act.wait_ge(S["max"], n + 1)
                    if n >= 3:
                        act.wait_ge(S["t_mm"], n - 2)
                    for b in range(2):
                        a.activation(pb[:, n % 3, b, 0:nk], M.ps[:, SCORE + n % 2, b * SEQ:b * SEQ + nk], ACT.Exp,
                                     bias=nm[:, n, b:b + 1], accum_out=sm[:, n, b:b + 1]).then_inc(S["exp"], 1)
                if n == 4:
                    act.wait_ge(S["c_ch"], 7)
                    for c in range(TC):
                        a.activation(sc[:, c], sc[:, c], ACT.Exp).then_inc(S["c_exp"], 1)
                if n >= 2:
                    m = n - 2
                    blocks = 2 * (m // HEADS + 1)
                    act.wait_ge(S["t_mm"], m + 1)
                    if m >= 2:
                        act.wait_ge(S["pv"], m - 1)
                    a.copy(ptb[:, m % 2, 0:blocks], M.ps[:, TURN + m % 2, 0:blocks * P].rearrange(
                        "p (x q) -> p x q", q=P)).then_inc(S["pt"], 1)
                if n == COMPRESSED + 2:
                    for c in range(TC):
                        act.wait_ge(S["c_tp"], c + 1)
                        a.copy(ptc[:, c], M.ps[:, TURN + c, :].rearrange("p (g q) -> p g q", g=GROUPS)
                               ).then_inc(S["c_ev"], 1)
            act.wait_ge(S["pv"], N + 1)
            for c in range(TC):
                a.copy(o[:, c, 0:512], M.ps[:, 2 * c, :]).then_inc(S["o_ev"], 1)
            for b in range(4):
                act.wait_ge(S["o_tp"], b + 1)
                a.copy(part(oT[0], b), bank_pair(M, b)).then_inc(S["oT_a"], 1)
            st.split_hi(act, 0, len(chunks) - 1)

        @block.vector
        def _(dve):
            v = nc.vector
            ln = Link(dve, S["c_ch"])
            ch2 = Link(dve, S["sm_ch"])
            scf = sc.rearrange("p c h n -> p (c h) n")

            def highest(n):
                nk = P * (n // HEADS + 1)
                dve.wait_ge(S["s_mm"], n + 1)
                v.tensor_reduce(nm[:, n], M.ps[:, SCORE + n % 2, :].rearrange("p (b k) -> p b k", b=2)[:, :, 0:nk],
                                AX.X, ALU.max, negate=True).then_inc(S["max"], 1)

            def scale(n):
                c, h = n // HEADS, n % HEADS
                nk = P * (c + 1)
                dve.wait_ge(S["exp"], 2 * (n + 1))
                ch2(v.reciprocal(gr[:, n], sm[:, n]))
                ch2(v.tensor_tensor(gr[:, n], gr[:, n], M.gates[:, c, 3 * h + 1:3 * h + 3], ALU.mult))
                for b in range(2):
                    v.tensor_scalar(pb[:, n % 3, b, 0:nk], pb[:, n % 3, b, 0:nk], gr[:, n, b:b + 1], None, ALU.mult
                                    ).then_inc(S["scaled"], 1)

            def compressed_scores():
                for c in range(TC):
                    dve.wait_ge(S["c_mm"], c + 1)
                    for g2 in range(2):
                        ln(v.tensor_tensor(sc[:, c].rearrange("p (a b r) n -> p b a r n", a=2, b=2)[:, g2],
                                           M.ps[:, TURN + c, :].rearrange("p (a r b n) -> p b a r n", a=2, r=HPG, b=2
                                                                          )[:, g2],
                                           M.cmask[:, c].unsqueeze(1).unsqueeze(1).to_broadcast([P, 2, HPG, CPAD]),
                                           ALU.add))

            def compressed_gates():
                ch2(v.reciprocal(cst[:, 2], cst[:, 1]))
                for c in range(TC):
                    cs = slice(16 * c, 16 * c + 16)
                    g0 = M.gates[:, c].rearrange("p (h b) -> p h b", b=3)[:, :, 0]
                    ch2(v.scalar_tensor_tensor(cst[:, 3, cs], cst[:, 2, cs], M.cvalid[:, c:c + 1], g0, ALU.mult,
                                               ALU.mult))
                    v.tensor_tensor(sc[:, c], sc[:, c], cst[:, 3, cs].unsqueeze(2).to_broadcast([P, HEADS, CPAD]),
                                    ALU.mult).then_inc(S["c_p"], 1)

            compressed_scores()
            for n in range(N):
                highest(n)
                if n >= 1:
                    scale(n - 1)
                if n == 2:
                    ln(v.tensor_reduce(cst[:, 0], scf, AX.X, ALU.max, negate=True))
                if n == 3:
                    for c in range(TC):
                        ln(v.tensor_tensor(sc[:, c], sc[:, c], cst[:, 0, 16 * c:16 * c + 16].unsqueeze(2
                           ).to_broadcast([P, HEADS, CPAD]), ALU.add))
                if n == 5:
                    dve.wait_ge(S["c_exp"], TC)
                    ch2(v.tensor_reduce(cst[:, 1], scf, AX.X, ALU.add))
                if n == 6:
                    compressed_gates()
            scale(N - 1)
            dve.wait_ge(S["pv"], N + 1)
            for c in range(TC):
                v.tensor_copy(o[:, c, 512:1024], M.ps[:, 2 * c + 1, :]).then_inc(S["o_ev"], 1)
            for b in range(4):
                dve.wait_ge(S["oT_a"], b + 1)
                v.tensor_tensor(part(oT[1], b), bank_pair(M, b), part(oT[0], b), ALU.subtract
                                ).then_inc(S["oT_d"], 1)
            st.split_lo(dve, 0, len(chunks) - 1)
            dve.wait_ge(S["out"], 1)
            for i in range(4):
                hs = M.h[:, i // 2, (i % 2) * 512:(i % 2 + 1) * 512]
                v.tensor_tensor(hs, hs, M.ps[:, 4 + i, :], ALU.add).then_inc(S["wl"], 1)


def build(nc, T, out):
    with ExitStack() as ctx:
        sem = Sems(nc, ctx)
        M = Mem(nc, ctx)
        s_conv = Stream(nc, M, sem, "wconv", 0)
        s_moe0, s_ovf0 = Stream(nc, M, sem, "wmoe0", 0), Stream(nc, M, sem, "wovf0", 0)
        s_att = Stream(nc, M, sem, "watt", 0)
        att = attention_chunks(T)
        s_moe1, s_ovf1 = Stream(nc, M, sem, "wmoe1", len(att) % RAWS), Stream(nc, M, sem, "wovf1", 0)
        moe1_first = [job_chunk(T, 1, 0, i) for i in range(RAWS)]
        gains = [sem(f"gain_in{i}") for i in range(4)]
        again = sem("reloaded")
        s_end = sem("h_out")

        def phase(f, *args):
            with ExitStack() as c:
                own = Sems(nc, c)
                f(nc, M, T, own, *args)
                own.clear()

        def wait_loaded(sp):
            for x in s_att.landed:
                sp.wait_ge(x, 16)

        def load_again(sp):
            for i in range(RAWS):
                dst = M.raw[:, i, :].rearrange("p (k f) -> p k f", k=att[i].shape[1])
                sp.dma_start(dst, att[i]).then_inc(again, 16)
            sp.wait_ge(again, 16 * RAWS)

        phase(conv_phase, s_conv, s_moe0, gains)
        phase(route_phase, 0, gains[1], T["kv_norm"], gains[2])
        phase(jobs_phase, 0, s_moe0, s_att, att[:RAWS])
        phase(overflow_phase, 0, s_ovf0, (wait_loaded, load_again))
        phase(project_phase, s_att, s_moe1, att, moe1_first, gains[2])
        phase(prep_phase, s_att, s_moe1, att, moe1_first, gains[3])
        phase(attend_phase, s_att, s_moe1, att, moe1_first)
        phase(route_phase, 1, gains[3], None, None)
        phase(jobs_phase, 1, s_moe1, None, [])
        phase(overflow_phase, 1, s_ovf1, None)
        with nc.Block() as block:
            @block.sync
            def _(sp):
                sp.dma_start(out[0].rearrange("(c p) d -> p c d", p=P), M.h[:]).then_inc(s_end, 16)
                sp.wait_ge(s_end, 16)


NAMES = ["x", "a_norm", "a_w_in", "a_dw", "a_dw_bias", "a_conv_norm", "a_w_out", "kv_norm", "w_kv", "cmp_pe",
         "phi_w1", "phi_b1", "phi_w2", "k_norm", "b_norm", "b_w_in", "b_q_norm", "b_w_out", "ffn_norm",
         "router_w", "router_bias", "moe_w1", "moe_w3", "moe_w2"]


def kernel(**inputs):
    import numpy as _np
    import concourse.bacc as _bacc
    from concourse import mybir as _mybir
    from concourse.bass_utils import run_bass_kernel_spmd as _run

    nc = _bacc.Bacc("TRN2", target_bir_lowering=False, num_devices=1)
    arrays, aps = {}, {}
    for name in NAMES:
        a = _np.ascontiguousarray(inputs[name])
        arrays[f"in_{name}"] = a
        aps[name] = nc.dram_tensor(f"in_{name}", a.shape, _mybir.dt.from_np(a.dtype), kind="ExternalInput").ap()
    out = nc.dram_tensor("out", inputs["x"].shape, _mybir.dt.float32, kind="ExternalOutput").ap()
    build(nc, aps, out)
    r = _run(nc, [arrays], core_ids=[0])
    return r.results[0]["out"]
```

```python
from contextlib import ExitStack

import concourse.bass as bass
from concourse import mybir

F32 = mybir.dt.float32
F32R = mybir.dt.float32r
BF16 = mybir.dt.bfloat16
I32 = mybir.dt.int32
ALU = mybir.AluOpType
ACT = mybir.ActivationFunctionType
AX = mybir.AxisListType

P = 128
SEQ = 256
TC = SEQ // P
D = 1024
KC = D // P
TAPS = 31
HEADS, GROUPS, HPG, DH = 16, 4, 4, 64
CMP_LEN, CMP_STRIDE = 32, 16
NCMP = (SEQ - CMP_LEN) // CMP_STRIDE + 1
CPAD = 32
HID = 128
EXPERTS, EGROUPS, EPG = 16, 4, 4
DE = 512
FC = DE // P
EPS = 1e-6
NEG = -1e30
BANK = 512
CHUNK = 2048
ARENA = 12352
RAWS, PARTS = 6, 3


class Sems:

    def __init__(self, nc, ctx):
        self.nc, self.ctx, self.taken = nc, ctx, []

    def __call__(self, name):
        s = self.ctx.enter_context(self.nc.semaphore(name))
        self.taken.append(s)
        return s

    def clear(self):
        nums = sorted(s.num for s in self.taken)
        first = [n for n in nums if n - 1 not in nums]
        last = [n for n in nums if n + 1 not in nums]
        with self.nc.Block() as block:
            @block.gpsimd
            def _(pool):
                for a, b in zip(first, last):
                    pool.sem_clear(range(a, b + 1))


class Link:

    def __init__(self, eng, sem):
        self.eng, self.sem, self.n = eng, sem, 0

    def __call__(self, ins):
        self.n += 1
        ins.then_inc(self.sem, 1)
        self.eng.wait_ge(self.sem, self.n)


class Mem:

    def __init__(self, nc, ctx):
        def sb(name, shape, dt=F32):
            return ctx.enter_context(nc.sbuf_tensor(name, shape, dt))

        self.raw = sb("raw", [P, RAWS, CHUNK])
        self.hi = sb("hi", [P, PARTS, CHUNK], F32R)
        self.lo = sb("lo", [P, PARTS, CHUNK], F32R)
        self.arena = sb("arena", [P, ARENA])
        self.xg = [sb("xg_hi", [P, KC, P], F32R), sb("xg_lo", [P, KC, P], F32R)]
        self.gut = [sb("gut_hi", [P, 2, FC, P], F32R), sb("gut_lo", [P, 2, FC, P], F32R)]
        self.h = sb("h", [P, TC, D])
        self.hn = sb("hn", [P, TC, D])
        self.hnT = [sb("hnT_hi", [P, KC, SEQ], F32R), sb("hnT_lo", [P, KC, SEQ], F32R)]
        self.pick = sb("pick", [P, TC, P], F32R)
        self.gain = sb("gain", [P, D])
        self.ident = sb("ident", [P, P])
        self.ones = sb("ones", [P, P])
        self.before = sb("before", [P, P])
        self.iota = sb("iota", [P, P])
        self.identb = sb("identb", [P, P], BF16)
        self.causal = sb("causal", [P, P], BF16)
        self.cmask = sb("cmask", [P, TC, CPAD])
        self.cvalid = sb("cvalid", [P, TC])
        self.cols2 = sb("cols2", [P, 38])
        self.stat = sb("stat", [P, 8])
        self.rw = [sb("rw_hi", [P, KC, EXPERTS], F32R), sb("rw_lo", [P, KC, EXPERTS], F32R)]
        self.rb = sb("rb", [P, EXPERTS])
        self.wg = [sb("wg_hi", [P, KC, 3 * HEADS], F32R), sb("wg_lo", [P, KC, 3 * HEADS], F32R)]
        self.phi2 = sb("phi2", [P, 2, DH])
        self.jgate = sb("jgate", [P, 5, EPG])
        self.rank = sb("rank", [P, TC])
        self.gm = sb("gm", [P, TC, EGROUPS])
        self.g4 = sb("g4", [P, TC, EPG])
        self.gates = sb("gates", [P, TC, 3 * HEADS])
        self.ovf = sb("ovf", [P, 2], I32)
        self.ps = ctx.enter_context(nc.psum_tensor("ps", [P, 8, BANK], F32))

    def at(self, start, *shape):
        n = 1
        for s in shape:
            n *= s
        v = self.arena[:, start:start + n]
        if len(shape) == 1:
            return v
        names = "abcd"[:len(shape)]
        return v.rearrange(f"p ({' '.join(names)}) -> p {' '.join(names)}",
                           **{k: s for k, s in zip(names, shape)})


def mm3(pe, out, x, w, start, stop):
    pe.matmul(out, x[0], w[0], start=start, stop=False)
    pe.matmul(out, x[0], w[1], start=False, stop=False)
    return pe.matmul(out, x[1], w[0], start=False, stop=stop)


def both(parts, *index):
    return [p[index] for p in parts]


class Stream:

    def __init__(self, nc, M, sem, tag, off):
        self.nc, self.M, self.off = nc, M, off
        self.landed = [sem(f"{tag}_landed{i}") for i in range(RAWS)]
        self.hi, self.lo, self.used = sem(f"{tag}_hi"), sem(f"{tag}_lo"), sem(f"{tag}_used")

    def load(self, eng, n, src):
        slot = (self.off + n) % RAWS
        dst = self.M.raw[:, slot, :].rearrange("p (k f) -> p k f", k=src.shape[1])
        eng.dma_start(dst, src).then_inc(self.landed[slot], 16)

    def number(self, j, i):
        return j * JOB_CHUNKS + i

    def filled(self, j, i):
        return j * (16 * JOB_CHUNKS // RAWS) + 16 * (i // RAWS + 1)

    def split_hi(self, act, j, i):
        slot = (self.off + i) % RAWS
        act.wait_ge(self.landed[slot], self.filled(j, i))
        act.wait_ge(self.used, self.number(j, i) + 1)
        self.nc.scalar.copy(self.M.hi[:, (self.off + i) % PARTS], self.M.raw[:, slot]).then_inc(self.hi, 1)

    def split_lo(self, eng, j, i):
        eng.wait_ge(self.hi, self.number(j, i) + 1)
        x = (self.off + i) % PARTS
        eng.tensor_tensor(self.M.lo[:, x], self.M.raw[:, (self.off + i) % RAWS], self.M.hi[:, x], ALU.subtract
                          ).then_inc(self.lo, 1)

    def parts(self, pe, j, i, k):
        pe.wait_ge(self.lo, self.number(j, i) + 1)
        x = (self.off + i) % PARTS
        return [t[:, x].rearrange("p (k f) -> p k f", k=k) for t in (self.M.hi, self.M.lo)]

    def wait_raw_free(self, sp, j, i):
        sp.wait_ge(self.lo, self.number(j, i) + 1)

    def wait_used(self, eng, j, i):
        eng.wait_ge(self.used, self.number(j, i) + 1 + PARTS)


JOB_CHUNKS = 24


def cut_k(w, halves):
    v = w.rearrange("(k p) n -> p k n", p=P)
    return [v[:, 4 * i:4 * i + 4] for i in range(halves)]


def cut_wide(w):
    v = w.rearrange("(k p) n -> p k n", p=P)
    return [v[:, 2 * i:2 * i + 2] for i in range(v.shape[1] // 2)]


def conv_chunks(T):
    v = T["a_w_in"][0].rearrange("(k p) n -> p k n", p=P)
    return [v[:, :, ab * D + 256 * q:ab * D + 256 * (q + 1)] for q in range(4) for ab in range(2)] + \
        cut_wide(T["a_w_out"][0])


def attention_chunks(T):
    out = []
    for b in range(3):
        out += cut_k(T["w_kv"][:, b * 512:(b + 1) * 512], 2)
    for b in range(2):
        out += cut_k(T["b_w_in"][0][:, b * 512:(b + 1) * 512], 2)
    out += [T["phi_w1"][i].rearrange("(j p) f -> p j f", p=P) for i in range(2)]
    return out + cut_wide(T["b_w_out"][0])


JOB_ORDER = [(w, 0, x) for w in ("w1", "w3") for x in range(2)]
for _e in range(1, EPG):
    JOB_ORDER += [(w, e, x) for w, e in (("w1", _e), ("w3", _e), ("w2", _e - 1)) for x in range(2)]
JOB_ORDER += [("w2", EPG - 1, x) for x in range(2)]


def job_chunk(T, layer, first, i):
    w, e, x = JOB_ORDER[i]
    v = T["moe_" + w][layer][bass.ds(first + e, 1)].rearrange("o (k p) f -> p (o k) f", p=P)
    return v[:, 4 * x:4 * x + 4] if w != "w2" else v[:, 2 * x:2 * x + 2]



class NormSems:
    def __init__(self, sem, gain, tag):
        self.sq, self.ms, self.sd, self.rs = (sem(f"{tag}_{n}") for n in ("sumsq", "meansq", "std", "rstd"))
        self.hn, self.tp = sem(f"{tag}_normed"), sem(f"{tag}_turned")
        self.ev = [sem(f"{tag}_hnT_act"), sem(f"{tag}_hnT_dve")]
        self.gain = gain


def norm_act(nc, act, M, s):
    for c in range(TC):
        nc.scalar.activation(M.hn[:, c, :], M.h[:, c, :], ACT.Square, accum_out=M.stat[:, c:c + 1]).then_inc(s.sq, 1)
    act.wait_ge(s.ms, 1)
    nc.scalar.activation(M.stat[:, 4:6], M.stat[:, 2:4], ACT.Sqrt).then_inc(s.sd, 1)


def norm_dve(nc, dve, M, s):
    dve.wait_ge(s.sq, TC)
    nc.vector.tensor_scalar(M.stat[:, 2:4], M.stat[:, 0:2], 1.0 / D, EPS, ALU.mult, ALU.add).then_inc(s.ms, 1)
    dve.wait_ge(s.sd, 1)
    nc.vector.reciprocal(M.stat[:, 6:8], M.stat[:, 4:6]).then_inc(s.rs, 1)
    dve.wait_ge(s.rs, 1)
    dve.wait_ge(s.gain, 16)
    for c in range(TC):
        nc.vector.scalar_tensor_tensor(M.hn[:, c, :], M.h[:, c, :], M.stat[:, 6 + c:7 + c], M.gain[:, :],
                                       ALU.mult, ALU.mult).then_inc(s.hn, 1)


def turn_pe(pe, M, b, src):
    for kk in range(2):
        for c in range(TC):
            k = 2 * (b % 4) + kk
            mm = pe.transpose(M.ps[:, b % 8, kk * SEQ + c * P:kk * SEQ + (c + 1) * P],
                              src[:, c, k * P:(k + 1) * P], M.ident[:, :])
    return mm


def keep_clock(pe, M, bank, times):
    for _ in range(times):
        pe.matmul(M.ps[:, bank, 0:P], M.ident[:], M.ident[:], start=True, stop=True)


def norm_pe(pe, M, s, spare=0):
    keep_clock(pe, M, 0, spare)
    pe.wait_ge(s.hn, TC)
    for b in range(4):
        turn_pe(pe, M, b, M.hn).then_inc(s.tp, 1)


def bank_pair(M, b):
    return M.ps[:, b, :].rearrange("p (k t) -> p k t", k=2)


def part(x, b):
    return x[:, 2 * b:2 * b + 2, :]


def norm_evac_act(nc, act, M, s):
    for b in range(4):
        act.wait_ge(s.tp, b + 1)
        nc.scalar.copy(part(M.hnT[0], b), bank_pair(M, b)).then_inc(s.ev[0], 1)


def norm_evac_dve(nc, dve, M, s):
    for b in range(4):
        dve.wait_ge(s.ev[0], b + 1)
        nc.vector.tensor_tensor(part(M.hnT[1], b), bank_pair(M, b), part(M.hnT[0], b), ALU.subtract
                                ).then_inc(s.ev[1], 1)


def wait_hnT(eng, s):
    eng.wait_ge(s.ev[1], 4)



PE_CONV = (1, 3, 5)
DVE_CONV = (0, 2, 4)
GLU_BANKS, SIGS, DIAGS = 6, 4, 14


def conv_bank(i):
    return 2 + i


def conv_phase(nc, M, T, sem, st, nxt, gains):
    U = M.at(0, KC, TAPS - 1 + SEQ)
    ACC = M.at(2288, KC, SEQ)
    SQ = M.at(4848, KC, SEQ)
    RSTD = M.at(6896, 2, SEQ)
    ROWS = M.at(7408, 1024)
    ROWS2 = M.at(8432, P)
    RW, WG = M.at(8560, KC, EXPERTS), M.at(8688, KC, 3 * HEADS)
    SIG = M.at(9072, SIGS, SEQ)
    DIAG = M.at(10096, DIAGS, P)
    COLS = M.at(10096 + DIAGS * P, KC, TAPS + 2)
    chunks, ahead = conv_chunks(T), [job_chunk(T, 0, 0, i) for i in range(RAWS)]
    NC = len(chunks)
    n = NormSems(sem, gains[0], "n0")
    s_x, s_rows, s_small = sem("x_in"), sem("rows_in"), sem("small_in")
    s_smallh, s_smalll, s_yh, s_yl = sem("small_hi"), sem("small_lo"), sem("y_hi"), sem("y_lo")
    s_const, s_pool = sem("constants"), sem("pool_chain")
    s_cols, s_colsT = sem("cols"), sem("colsT")
    s_mm, s_sig, s_glu = sem("glu_mm"), sem("glu_sig"), sem("glu_done")
    s_tap, s_sq, s_ssum = sem("taps"), sem("conv_sq"), sem("conv_ssum")
    s_conv, s_diag, s_dused, s_cmm, s_cev = (sem(x) for x in (
        "conv_chunk_dve", "diag", "diag_used", "conv_chunk_pe", "conv_evac"))
    s_ms, s_sd, s_rs, s_z, s_y = (sem(f"conv_{k}") for k in ("ms", "sd", "rs", "z", "y"))
    s_out, s_res = sem("conv_out"), sem("conv_res")

    with nc.Block() as block:
        @block.sync
        def _(sp):
            sp.dma_start(M.h[:], T["x"][0].rearrange("(c p) d -> p c d", p=P)).then_inc(s_x, 16)
            sp.dma_start(ROWS[0:TAPS, :], T["a_dw"][0]).then_inc(s_rows, 16)
            sp.dma_start(ROWS[TAPS:TAPS + 1, :], T["a_dw_bias"]).then_inc(s_rows, 16)
            sp.dma_start(ROWS[TAPS + 1:TAPS + 2, :], T["a_conv_norm"]).then_inc(s_rows, 16)
            sp.dma_start(M.gain[:], T["a_norm"][0].partition_broadcast(P)).then_inc(n.gain, 16)
            sp.dma_start(ROWS2[0:32, :], T["cmp_pe"].rearrange("i (j l) d -> (i j) (l d)", l=2)).then_inc(s_rows, 16)
            for half in range(2):
                cs = slice(half * DH, (half + 1) * DH)
                sp.dma_start(ROWS2[32:35, cs], T["k_norm"]).then_inc(s_rows, 16)
                sp.dma_start(ROWS2[35:36, cs], T["b_q_norm"]).then_inc(s_rows, 16)
            sp.dma_start(ROWS2[36:38, :], T["phi_b1"]).then_inc(s_rows, 16)
            for i in range(RAWS):
                st.load(sp, i, chunks[i])
            sp.dma_start(RW, T["router_w"].rearrange("(k p) e -> p k e", p=P)).then_inc(s_small, 16)
            sp.dma_start(M.rb[:], T["router_bias"].partition_broadcast(P)).then_inc(s_small, 16)
            sp.dma_start(WG, T["b_w_in"][0].rearrange("(k p) n -> p k n", p=P)[:, :, D:]).then_inc(s_small, 16)
            sp.dma_start(M.phi2[:], T["phi_w2"].rearrange("i h d -> h i d")).then_inc(s_small, 16)
            sp.wait_ge(n.hn, TC)
            sp.dma_start(M.gain[:], T["ffn_norm"][0].partition_broadcast(P)).then_inc(gains[1], 16)
            for i in range(NC):
                st.wait_raw_free(sp, 0, i)
                if i + RAWS < NC:
                    st.load(sp, i + RAWS, chunks[i + RAWS])
                else:
                    nxt.load(sp, i + RAWS - NC, ahead[i + RAWS - NC])

        @block.gpsimd
        def _(pool):
            chain = Link(pool, s_pool)
            g = nc.gpsimd
            chain(g.memset(M.ones[:], 1.0))
            chain(g.affine_select(out=M.ident[:], in_=M.ones[:], pattern=[[-1, P]], compare_op=ALU.is_equal,
                                  fill=0.0, base=0, channel_multiplier=1))
            pool.wait_ge(s_pool, 2)
            g.memset(U[:, :, 0:TAPS - 1], 0.0).then_inc(s_const, 1)
            chain(g.affine_select(out=M.before[:], in_=M.ones[:], pattern=[[1, P]], compare_op=ALU.is_ge,
                                  fill=0.0, base=-1, channel_multiplier=-1))
            chain(g.iota(M.iota[:], pattern=[[1, P]], base=0, channel_multiplier=0,
                         allow_small_or_imprecise_dtypes=True))
            chain(g.tensor_copy(M.identb[:], M.ident[:]))
            chain(g.memset(M.causal[:], 0.0))
            chain(g.memset(M.cmask[:], 0.0))
            chain(g.memset(M.cvalid[:], 1.0))
            chain(g.affine_select(out=M.causal[:], in_=M.causal[:], pattern=[[-1, P]], compare_op=ALU.is_ge,
                                  fill=NEG, base=0, channel_multiplier=1))
            for c in range(TC):
                end = c * P - (CMP_LEN - 1)
                chain(g.affine_select(out=M.cmask[:, c], in_=M.cmask[:, c], pattern=[[-CMP_STRIDE, CPAD]],
                                      compare_op=ALU.is_ge, fill=NEG, base=end, channel_multiplier=1))
                chain(g.affine_select(out=M.cvalid[:, c:c + 1], in_=M.cvalid[:, c:c + 1], pattern=[[0, 1]],
                                      compare_op=ALU.is_ge, fill=0.0, base=end, channel_multiplier=1))
            for i in range(NC):
                st.split_lo(pool, 0, i)

        @block.scalar
        def _(act):
            act.wait_ge(s_x, 16)
            norm_act(nc, act, M, n)
            act.wait_ge(s_colsT, 1)
            nc.scalar.copy(COLS[:], M.ps[:, 7, 0:KC * (TAPS + 2)].rearrange("p (k r) -> p k r", k=KC)
                           ).then_inc(s_cols, 1)
            nc.scalar.copy(M.cols2[:], M.ps[:, 6, 0:38]).then_inc(s_cols, 1)
            for i in range(2):
                st.split_hi(act, 0, i)
            norm_evac_act(nc, act, M, n)
            st.split_hi(act, 0, 2)

            def diagonals(i, first=0, end=TAPS):
                for tap in range(first, end):
                    k = i * TAPS + tap
                    if k >= DIAGS:
                        act.wait_ge(s_dused, k - DIAGS + 1)
                    nc.scalar.activation(DIAG[:, k % DIAGS], M.ident[:], ACT.Copy,
                                         scale=COLS[:, PE_CONV[i], tap:tap + 1]).then_inc(s_diag, 1)

            def square(c):
                if c in PE_CONV:
                    i = PE_CONV.index(c)
                    act.wait_ge(s_cmm, i + 1)
                    act.wait_ge(s_conv, i + 1)
                    nc.scalar.activation(ACC[:, c], M.ps[:, conv_bank(i), 0:SEQ], ACT.Identity,
                                         bias=COLS[:, c, TAPS:TAPS + 1]).then_inc(s_cev, 1)
                    act.wait_ge(s_cev, i + 1)
                else:
                    act.wait_ge(s_conv, DVE_CONV.index(c) + 1 if c in DVE_CONV else c - 2)
                nc.scalar.activation(SQ[:, c], ACC[:, c], ACT.Square).then_inc(s_sq, 1)

            act.wait_ge(s_const, 1)
            for c in range(KC):
                act.wait_ge(s_mm, c + 1)
                if c >= SIGS:
                    act.wait_ge(s_glu, c - SIGS + 1)
                nc.scalar.activation(SIG[:, c % SIGS], M.ps[:, c % GLU_BANKS, SEQ:], ACT.Sigmoid).then_inc(s_sig, 1)
                if c == KC - 2:
                    diagonals(0, 0, DIAGS)
                st.split_hi(act, 0, c + PARTS)
            diagonals(0, DIAGS)
            diagonals(1)
            square(0)
            square(1)
            diagonals(2)
            act.wait_ge(s_small, 64)
            nc.scalar.copy(M.rw[0][:], RW).then_inc(s_smallh, 1)
            nc.scalar.copy(M.wg[0][:], WG).then_inc(s_smallh, 1)
            for c in range(2, KC):
                square(c)
            act.wait_ge(s_ms, 1)
            nc.scalar.activation(RSTD[:, 1], RSTD[:, 0], ACT.Sqrt).then_inc(s_sd, 1)
            for c in range(KC):
                act.wait_ge(s_z, c // 2 + 1)
                nc.scalar.activation(SQ[:, c], SQ[:, c], ACT.Silu,
                                     scale=COLS[:, c, TAPS + 1:TAPS + 2]).then_inc(s_y, 1)
                if c % 2 == 1:
                    act.wait_ge(s_y, c + 1)
                    nc.scalar.copy(M.hnT[0][:, c - 1:c + 1], SQ[:, c - 1:c + 1]).then_inc(s_yh, 1)
            st.split_hi(act, 0, NC - 1)
            load_sqrt_table(nc, M)

        @block.vector
        def _(dve):
            norm_dve(nc, dve, M, n)
            norm_evac_dve(nc, dve, M, n)
            dve.wait_ge(s_cols, 1)
            dve.wait_ge(s_const, 1)
            v = nc.vector
            ntap = [0]

            def glu(c):
                dve.wait_ge(s_sig, c + 1)
                v.tensor_tensor(U[:, c, TAPS - 1:], M.ps[:, c % GLU_BANKS, 0:SEQ], SIG[:, c % SIGS], ALU.mult
                                ).then_inc(s_glu, 1)

            def multiply_add(c, tap, acc):
                w, u = COLS[:, c, tap:tap + 1], U[:, c, tap:tap + SEQ]
                if tap == 0:
                    ins = v.tensor_scalar(acc, u, w, COLS[:, c, TAPS:TAPS + 1], ALU.mult, ALU.add)
                elif tap == 1 and c in DVE_CONV:
                    ins = v.tensor_scalar(acc, u, w, None, ALU.mult)
                else:
                    dve.wait_ge(s_tap, ntap[0] - 1)
                    ins = v.scalar_tensor_tensor(acc, u, w, acc, ALU.mult, ALU.add)
                ins.then_inc(s_tap, 1)
                ntap[0] += 1

            glu(0)
            for i, c in enumerate(DVE_CONV):
                dve.wait_ge(s_glu, c + 1)
                for tap in range(TAPS):
                    multiply_add(c, tap, ACC[:, c + tap % 2])
                glu(c + 1)
                glu(c + 2)
                dve.wait_ge(s_tap, ntap[0])
                v.tensor_tensor(ACC[:, c], ACC[:, c], ACC[:, c + 1], ALU.add).then_inc(s_conv, 1)
            glu(7)
            dve.wait_ge(s_glu, KC)
            for tap in range(TAPS):
                for c in (6, 7):
                    multiply_add(c, tap, ACC[:, c])
            dve.wait_ge(s_tap, ntap[0])
            v.sem_inc(s_conv, 2)
            dve.wait_ge(s_ssum, 1)
            nc.vector.tensor_scalar(RSTD[:, 0], M.ps[:, 6, 0:SEQ], 1.0 / D, EPS, ALU.mult, ALU.add).then_inc(s_ms, 1)
            dve.wait_ge(s_sd, 1)
            nc.vector.reciprocal(RSTD[:, 0], RSTD[:, 1]).then_inc(s_rs, 1)
            dve.wait_ge(s_rs, 1)
            dve.wait_ge(s_cev, len(PE_CONV))
            for p in range(KC // 2):
                cs = slice(2 * p, 2 * p + 2)
                nc.vector.tensor_tensor(SQ[:, cs], ACC[:, cs], RSTD[:, 0].unsqueeze(1).to_broadcast([P, 2, SEQ]),
                                        ALU.mult).then_inc(s_z, 1)
            dve.wait_ge(s_smallh, 2)
            nc.vector.tensor_tensor(M.rw[1][:], RW, M.rw[0][:], ALU.subtract).then_inc(s_smalll, 1)
            nc.vector.tensor_tensor(M.wg[1][:], WG, M.wg[0][:], ALU.subtract).then_inc(s_smalll, 1)
            for p in range(KC // 2):
                cs = slice(2 * p, 2 * p + 2)
                dve.wait_ge(s_yh, p + 1)
                nc.vector.tensor_tensor(M.hnT[1][:, cs], SQ[:, cs], M.hnT[0][:, cs], ALU.subtract).then_inc(s_yl, 1)
            for i in range(4):
                dve.wait_ge(s_out, i + 1)
                hs = M.h[:, i // 2, (i % 2) * 512:(i % 2 + 1) * 512]
                nc.vector.tensor_tensor(hs, hs, M.ps[:, i, :], ALU.add).then_inc(s_res, 1)

        @block.tensor
        def _(pe):
            pe.sem_inc(st.used, PARTS)
            pe.wait_ge(s_pool, 2)
            pe.wait_ge(s_rows, 16 * 9)
            for k in range(KC):
                pe.transpose(M.ps[:, 7, k * (TAPS + 2):(k + 1) * (TAPS + 2)], ROWS[0:TAPS + 2, k * P:(k + 1) * P],
                             M.ident[0:TAPS + 2, 0:TAPS + 2])
            pe.transpose(M.ps[:, 6, 0:38], ROWS2[0:38, :], M.ident[0:38, 0:38]).then_inc(s_colsT, 1)
            norm_pe(pe, M, n, 8)
            keep_clock(pe, M, 5, 12)
            wait_hnT(pe, n)
            for c in range(KC):
                if c >= GLU_BANKS:
                    pe.wait_ge(s_glu, c - GLU_BANKS + 1)
                for ab in range(2):
                    w = st.parts(pe, 0, 2 * (c // 2) + ab, KC)
                    cs = slice((c % 2) * P, (c % 2 + 1) * P)
                    for k in range(KC):
                        mm = mm3(pe, M.ps[:, c % GLU_BANKS, ab * SEQ:(ab + 1) * SEQ], [x[:, k, cs] for x in w],
                                 [x[:, k, :] for x in M.hnT], k == 0, k == KC - 1)
                    if ab == 0 and c % 2 == 1:
                        mm.then_inc(st.used, 1)
                mm.then_inc(s_mm, 1)
                if c % 2 == 1:
                    pe.wait_ge(s_mm, c + 1)
                    pe.sem_inc(st.used, 1)

            def sum_squares(c):
                pe.wait_ge(s_sq, c + 1)
                return pe.matmul(M.ps[:, 6, 0:SEQ], M.ones[:], SQ[:, c], start=(c == 0), stop=(c == KC - 1))

            pe.wait_ge(s_cols, 2)
            for i, c in enumerate(PE_CONV):
                pe.wait_ge(s_glu, c + 1)
                for tap in range(TAPS):
                    k = i * TAPS + tap
                    pe.wait_ge(s_diag, k + 1)
                    mm = pe.matmul(M.ps[:, conv_bank(i), 0:SEQ], DIAG[:, k % DIAGS], U[:, c, tap:tap + SEQ],
                                   start=(tap == 0), stop=(tap == TAPS - 1))
                    mm.then_inc(s_dused if tap < TAPS - 1 else s_cmm, 1)
                    if i == 2 and tap == TAPS // 2:
                        sum_squares(0)
                        sum_squares(1)
                pe.wait_ge(s_cmm, i + 1)
                pe.sem_inc(s_dused, 1)
            for c in range(2, KC):
                mm = sum_squares(c)
            mm.then_inc(s_ssum, 1)
            keep_clock(pe, M, 7, 30)
            for p in range(KC // 2):
                pe.wait_ge(s_yl, p + 1)
                w = st.parts(pe, 0, KC + p, 2)
                if p == KC // 2 - 1:
                    out_chunk(pe, M, M.hnT, w, p, 0, s_out)
                else:
                    out_chunk(pe, M, M.hnT, w, p, 0).then_inc(st.used, 1)


def out_chunk(pe, M, x, w, p, bank, done=None):
    for i in range(4):
        c, ns = i // 2, slice((i % 2) * 512, (i % 2 + 1) * 512)
        for k in range(2):
            mm = mm3(pe, M.ps[:, bank + i, :], [t[:, 2 * p + k, c * P:(c + 1) * P] for t in x],
                     [t[:, k, ns] for t in w], p == 0 and k == 0, p == KC // 2 - 1 and k == 1)
        if done is not None:
            mm.then_inc(done, 1)
    return mm


def load_sqrt_table(nc, M):
    nc.scalar.activation(M.stat[:, 4:6], M.stat[:, 6:8], ACT.Sqrt)



class MoeSems:

    def __init__(self, sem, tag):
        self.silu = sem(f"{tag}_silu")
        self.gu = sem(f"{tag}_gu_free")
        self.turned = sem(f"{tag}_turned_free")
        self.guT = sem(f"{tag}_guT_free")
        self.gut_hi = sem(f"{tag}_gut_hi")
        self.xg_hi = sem(f"{tag}_xg_hi")
        self.y_out = sem(f"{tag}_yout_free")
        self.pick = sem(f"{tag}_pick")
        self.gather = sem(f"{tag}_gather")
        self.xg = sem(f"{tag}_xg")
        self.scat, self.res = sem(f"{tag}_scatter"), sem(f"{tag}_residual")


def moe_views(M):
    class V:
        Y = M.at(0, EGROUPS, D)
        S = M.at(4096, EGROUPS, TC, P)
        ST = M.at(5120, EGROUPS, SEQ)
        SIL = M.at(6144, 2, DE)
        GU = M.at(7168, 2, DE)
    return V


def one_hot_rows(v, M, dst, j):
    for c in range(TC):
        ins = v.tensor_scalar(dst[:, c], M.iota[:], M.rank[:, c:c + 1], M.gm[:, c, j:j + 1], ALU.is_equal, ALU.mult)
    return ins


def route_phase(nc, M, T, sem, layer, st, gain, next_gain, next_landed):
    n = NormSems(sem, gain, f"n{layer}")
    V = moe_views(M)
    t = f"r{layer}"
    s_lg, s_sc, s_ch, s_gm, s_rk, s_S, s_lgT, s_hnp = (
        sem(f"{t}_{k}") for k in ("logits", "scores", "chain", "gm", "rank", "S", "logitsT", "hn_parts"))
    tmp = V.SIL.rearrange("p a b -> p (a b)")
    logitsT = V.GU[0:EXPERTS, 0, 0:SEQ]
    names = {}
    off = [0]

    def small(name, *shape):
        k = 1
        for x in shape:
            k *= x
        v = tmp[:, off[0]:off[0] + k]
        off[0] += k
        if len(shape) == 2:
            v = v.rearrange("p (a b) -> p a b", a=shape[0])
        if len(shape) == 3:
            v = v.rearrange("p (a b c) -> p a b c", a=shape[0], b=shape[1])
        names[name] = v
        return v

    CG = TC * EGROUPS
    score, biased, mb, oh1, oh2, cand = (small(x, TC, EXPERTS) for x in ("score", "biased", "mb", "oh1", "oh2", "cand"))
    hi, lo = small("hi", CG, 2), small("lo", CG, 2)
    top, mn, ml, gs, off1 = (small(x, CG) for x in ("top", "mn", "ml", "gs", "off1"))
    gcand, gr = (small(x, TC, EGROUPS) for x in ("gcand", "gr"))
    gm = M.gm[:]
    m2 = small("m2", 8, TC)

    with nc.Block() as block:
        @block.sync
        def _(sp):
            sp.wait_ge(n.hn, TC)
            if next_gain is not None:
                sp.dma_start(M.gain[:], next_gain.partition_broadcast(P)).then_inc(next_landed, 16)
            for i in range(PARTS):
                st.wait_raw_free(sp, 0, i)
                st.load(sp, i, job_chunk(T, layer, 0, i + RAWS))

        @block.scalar
        def _(act):
            norm_act(nc, act, M, n)
            norm_evac_act(nc, act, M, n)
            st.split_hi(act, 0, 0)
            act.wait_ge(s_lg, 1)
            nc.scalar.copy(logitsT, M.ps[0:EXPERTS, 4, 0:SEQ]).then_inc(s_lgT, 1)
            for i in range(1, PARTS):
                st.split_hi(act, 0, i)
            act.wait_ge(s_lg, 2)
            nc.scalar.activation(score, M.ps[:, 4, SEQ:SEQ + TC * EXPERTS].rearrange("p (c e) -> p c e", c=TC),
                                 ACT.Sigmoid).then_inc(s_sc, 1)
            nc.scalar.copy(hn_parts(M)[0], M.hn[:]).then_inc(s_hnp, 1)

        @block.gpsimd
        def _(pool):
            pool.wait_ge(s_hnp, 1)
            hi, lo = hn_parts(M)
            nc.gpsimd.tensor_tensor(lo, M.hn[:], hi, ALU.subtract).then_inc(s_hnp, 1)

        @block.vector
        def _(dve):
            norm_dve(nc, dve, M, n)
            norm_evac_dve(nc, dve, M, n)
            for i in range(PARTS):
                st.split_lo(dve, 0, i)
            v = nc.vector
            ln = Link(dve, s_ch)
            dve.wait_ge(s_sc, 1)
            ln(v.tensor_tensor(biased, score, M.rb[:].unsqueeze(1).to_broadcast([P, TC, EXPERTS]), ALU.add))
            b4 = biased.rearrange("p c (g k) -> p (c g) k", k=EPG)
            v.tensor_tensor(hi, b4[:, :, 0:2], b4[:, :, 2:4], ALU.max).then_inc(s_ch, 1)
            ln.n += 1
            ln(v.tensor_tensor(lo, b4[:, :, 0:2], b4[:, :, 2:4], ALU.min))
            v.tensor_tensor(top, hi[:, :, 0], hi[:, :, 1], ALU.max).then_inc(s_ch, 1)
            v.tensor_tensor(mn, hi[:, :, 0], hi[:, :, 1], ALU.min).then_inc(s_ch, 1)
            ln.n += 2
            ln(v.tensor_tensor(ml, lo[:, :, 0], lo[:, :, 1], ALU.max))
            ln(v.tensor_tensor(mn, mn, ml, ALU.max))
            ln(v.tensor_tensor(gs, top, mn, ALU.add))

            def first_max(values, n_val, m, one_hot, cnd):
                ln(v.tensor_reduce(m[:, 0], values, AX.X, ALU.max))
                ln(v.tensor_tensor(cnd, values, m[:, 0].unsqueeze(2).to_broadcast([P, TC, n_val]), ALU.is_equal))
                ln(v.scalar_tensor_tensor(cnd, cnd, -64.0, M.iota[:, 0:n_val].unsqueeze(1).to_broadcast(
                    [P, TC, n_val]), ALU.mult, ALU.add))
                ln(v.tensor_reduce(m[:, 1], cnd, AX.X, ALU.min))
                ln(v.tensor_tensor(one_hot, cnd, m[:, 1].unsqueeze(2).to_broadcast([P, TC, n_val]), ALU.is_equal))

            first_max(gs.rearrange("p (c g) -> p c g", c=TC), EGROUPS, m2[:, 0:2], gm, gcand)
            dve.sem_inc(s_gm, 1)
            gmf = gm.rearrange("p c g -> p (c g)")
            ln(v.tensor_scalar(off1, gmf, -1.0, -NEG, ALU.add, ALU.mult))
            mb4 = mb.rearrange("p c (g k) -> p (c g) k", k=EPG)
            ln(v.tensor_tensor(mb4, b4, gmf.unsqueeze(2).to_broadcast([P, CG, EPG]), ALU.mult))
            ln(v.tensor_tensor(mb4, mb4, off1.unsqueeze(2).to_broadcast([P, CG, EPG]), ALU.add))
            first_max(mb, EXPERTS, m2[:, 2:4], oh1, cand)
            ln(v.scalar_tensor_tensor(mb, oh1, 2 * NEG, mb, ALU.mult, ALU.add))
            first_max(mb, EXPERTS, m2[:, 4:6], oh2, cand)
            ln(v.tensor_tensor(oh1, oh1, oh2, ALU.add))
            ln(v.tensor_tensor(score, score, oh1, ALU.mult))
            ln(v.tensor_reduce(m2[:, 6], score, AX.X, ALU.add))
            ln(v.reciprocal(m2[:, 7], m2[:, 6]))
            ln(v.tensor_tensor(score, score, m2[:, 7].unsqueeze(2).to_broadcast([P, TC, EXPERTS]), ALU.mult))
            for c in range(TC):
                ln(v.tensor_reduce(M.g4[:, c], score[:, c].rearrange("p (g k) -> p k g", k=EPG), AX.X, ALU.add))
            dve.wait_ge(s_rk, 1)
            rk = M.ps[:, 5, 0:CG].rearrange("p (c g) -> p c g", c=TC)
            ln(v.tensor_tensor(gr, gm, rk, ALU.mult))
            ln(v.tensor_reduce(M.rank[:], gr, AX.X, ALU.add))
            one_hot_rows(v, M, M.pick, 0).then_inc(s_S, 1)

        @block.tensor
        def _(pe):
            pe.sem_inc(st.used, PARTS)
            norm_pe(pe, M, n, 16)
            for k in range(KC):
                if k % 2 == 0:
                    pe.wait_ge(n.ev[1], k // 2 + 1)
                mm = mm3(pe, M.ps[0:EXPERTS, 4, 0:SEQ], [x[:, k, :] for x in M.rw], [x[:, k, :] for x in M.hnT],
                         k == 0, k == KC - 1)
            mm.then_inc(s_lg, 1)
            pe.wait_ge(s_lgT, 1)
            for c in range(TC):
                mm = pe.transpose(M.ps[:, 4, SEQ + c * EXPERTS:SEQ + (c + 1) * EXPERTS],
                                  logitsT[:, c * P:(c + 1) * P], M.ident[0:EXPERTS, 0:EXPERTS])
            mm.then_inc(s_lg, 1)
            keep_clock(pe, M, 7, 47)
            pe.wait_ge(s_gm, 1)
            B = M.ps[:, 5, :]
            pe.matmul(B[:, 0:4], M.before[:], gm[:, 0], start=True, stop=True)
            pe.matmul(B[:, 4:8], M.ones[:], gm[:, 0], start=True, stop=False)
            pe.matmul(B[:, 4:8], M.before[:], gm[:, 1], start=False, stop=True)
            pe.matmul(B[:, 8:12], M.ones[:], gm[:, 0], start=True, stop=False)
            pe.matmul(B[:, 8:12], M.ones[:], gm[:, 1], start=False, stop=True).then_inc(s_rk, 1)
            keep_clock(pe, M, 7, 33)


G_BANK, U_BANK, Y_BANK, T_BANK = 0, 2, 4, 6


def hn_parts(M):
    return [t[:].rearrange("p k t -> p (k t)").rearrange("p (c d) -> p c d", c=TC) for t in M.hnT]


def pe_gather(pe, M, j, half, s):
    bank = (G_BANK, U_BANK)[half]
    if half == 0:
        pe.wait_ge(s.pick, j + 1)
    for k in range(4):
        col = (4 * half + k) * P
        for c in range(TC):
            for i, t in enumerate(hn_parts(M)):
                mm = pe.matmul(M.ps[:, bank, k * P:(k + 1) * P], t[:, c, col:col + P], M.pick[:, c],
                               start=(c == 0 and i == 0), stop=(c == TC - 1 and i == 1))
    mm.then_inc(s.gather, 1)


IDX = {key: i for i, key in enumerate(JOB_ORDER)}


SCATTER_BANKS = (0, 2, 1, 3)


def pe_scatter(pe, M, V, i, first, end, last):
    for j in range(first, end):
        mm = pe.matmul(M.ps[:, SCATTER_BANKS[i], :], V.ST[:, j, (i // 2) * P:(i // 2 + 1) * P],
                       V.Y[:, j, (i % 2) * 512:(i % 2 + 1) * 512], start=(j == 0), stop=(j == last))
    return mm


def pe_job(pe, M, V, j, s, st, more, meanwhile=None):
    def product(name, bank, e):
        for x in range(2):
            i = IDX[name, e, x]
            w = st.parts(pe, j, i, 4)
            for k in range(4):
                mm = mm3(pe, M.ps[:, bank + e % 2, :], [t[:, 4 * x + k] for t in M.xg], [t[:, k] for t in w],
                         x == 0 and k == 0, x == 1 and k == 3)
            mm.then_inc(st.used, 1)

    def turn(e):
        E = 4 * j + e
        pe.wait_ge(s.gu, E + 3)
        pe.wait_ge(s.guT, E + 1)
        for k in range(FC):
            mm = pe.transpose(M.ps[:, T_BANK, k * P:(k + 1) * P], V.GU[:, e % 2, k * P:(k + 1) * P], M.ident[:])
        mm.then_inc(s.turned, 1)

    def y(e):
        pe.wait_ge(s.guT, 4 * j + e + 2)
        if e == 0:
            pe.wait_ge(s.y_out, j * 2 + 2)
        for x in range(2):
            w = st.parts(pe, j, IDX["w2", e, x], 2)
            for k in range(2):
                for n in range(2):
                    mm = mm3(pe, M.ps[:, Y_BANK + n, :], [t[:, e % 2, 2 * x + k] for t in M.gut],
                             [t[:, k, n * 512:(n + 1) * 512] for t in w], e == 0 and x == 0 and k == 0,
                             e == EPG - 1 and x == 1 and k == 1)
            mm.then_inc(st.used, 1)

    pe.wait_ge(s.xg, j * 2 + 2)
    for e in range(EPG):
        pe.wait_ge(s.gu, 4 * j + e + 1)
        product("w1", G_BANK, e)
        if e > 0:
            turn(e - 1)
        product("w3", U_BANK, e)
        if e > 0:
            y(e - 1)
    if more:
        pe.wait_ge(s.gu, 4 * j + 5)
        pe_gather(pe, M, j + 1, 0, s)
    turn(EPG - 1)
    if more:
        pe_gather(pe, M, j + 1, 1, s)
    if meanwhile is not None:
        meanwhile()
    y(EPG - 1)


def gathered(M, half):
    return M.ps[:, (G_BANK, U_BANK)[half], :].rearrange("p (k t) -> p k t", k=4)


def act_take_gather(nc, act, M, j, half, s):
    act.wait_ge(s.gather, j * 2 + half + 1)
    nc.scalar.copy(M.xg[0][:, 4 * half:4 * half + 4], gathered(M, half)).then_inc(s.xg_hi, 1)


def dve_take_gather(nc, dve, M, j, half, s):
    dve.wait_ge(s.xg_hi, j * 2 + half + 1)
    ks = slice(4 * half, 4 * half + 4)
    nc.vector.tensor_tensor(M.xg[1][:, ks], gathered(M, half), M.xg[0][:, ks], ALU.subtract).then_inc(s.xg, 1)


def turned(M):
    return M.ps[:, T_BANK, :].rearrange("p (k t) -> p k t", k=FC)


def act_job(nc, act, M, V, j, s, st, ydst, more):
    def take_turned(e):
        act.wait_ge(s.turned, 4 * j + e + 3)
        nc.scalar.copy(M.gut[0][:, e % 2], turned(M)).then_inc(s.gut_hi, 1)

    for i, (w, e, x) in enumerate(JOB_ORDER):
        if (w, x) == ("w1", 1):
            st.wait_used(act, j, i)
            act.wait_ge(s.gu, 4 * j + e + 1)
            nc.scalar.activation(V.SIL[:, e % 2], M.ps[:, G_BANK + e % 2, :], ACT.Silu).then_inc(s.silu, 1)
            if e > 0:
                take_turned(e - 1)
        if (w, e, x) == ("w2", EPG - 2, 1):
            if more:
                act_take_gather(nc, act, M, j + 1, 0, s)
            take_turned(EPG - 1)
            if more:
                act_take_gather(nc, act, M, j + 1, 1, s)
        if i == JOB_CHUNKS - 1:
            st.wait_used(act, j, i)
            nc.scalar.copy(ydst(j)[:, 0:512], M.ps[:, Y_BANK, :]).then_inc(s.y_out, 1)
        if more or i + PARTS < JOB_CHUNKS:
            st.split_hi(act, j, i + PARTS)


def dve_job(nc, dve, M, V, j, s, st, gate, ydst, more):
    def take_turned(e):
        dve.wait_ge(s.gut_hi, 4 * j + e + 1)
        nc.vector.tensor_tensor(M.gut[1][:, e % 2], turned(M), M.gut[0][:, e % 2], ALU.subtract).then_inc(s.guT, 1)

    if more:
        nc.vector.tensor_copy(M.pick[:], V.S[:, bass.ds(j + 1, 1)].rearrange("p o c t -> p (o c) t")
                              ).then_inc(s.pick, 1)
    for i, (w, e, x) in enumerate(JOB_ORDER):
        if (w, x) == ("w1", 1) and e > 0:
            take_turned(e - 1)
        if (w, x) == ("w3", 1):
            E = 4 * j + e
            dve.wait_ge(s.silu, E + 1)
            st.wait_used(dve, j, i)
            dve.wait_ge(s.turned, E + 1)
            nc.vector.scalar_tensor_tensor(V.GU[:, e % 2], M.ps[:, U_BANK + e % 2, :], gate(j, e), V.SIL[:, e % 2],
                                           ALU.mult, ALU.mult).then_inc(s.gu, 1)
        if (w, e, x) == ("w2", EPG - 2, 1):
            if more:
                dve_take_gather(nc, dve, M, j + 1, 0, s)
            take_turned(EPG - 1)
            if more:
                dve_take_gather(nc, dve, M, j + 1, 1, s)
        if i == JOB_CHUNKS - 1:
            st.wait_used(dve, j, i)
            nc.vector.tensor_copy(ydst(j)[:, 512:1024], M.ps[:, Y_BANK + 1, :]).then_inc(s.y_out, 1)
        if more or i + PARTS < JOB_CHUNKS:
            st.split_lo(dve, j, i + PARTS)


def credits(eng, *pairs):
    for s, n in pairs:
        eng.sem_inc(s, n)


def store(sp, M, out, c):
    sp.dma_start(out[0][0, c * P:(c + 1) * P, :], M.h[:, c]).then_inc(out[1], 16)


def jobs_phase(nc, M, T, sem, layer, st, nxt, ahead, out=None):
    s = MoeSems(sem, f"m{layer}")
    V = moe_views(M)
    JL = EGROUPS - 1

    def gate(j, e):
        g = M.jgate[:].rearrange("p j e -> p (j e)")
        return g[:, 4 * j + e:4 * j + e + 1] if isinstance(j, int) else g[:, bass.ds(j * 4 + e, 1)]

    s_St, s_jg, s_rows = sem(f"s{layer}_turned"), sem(f"s{layer}_jobgate"), sem(f"s{layer}_rows")
    s_ST, s_jge, s_ovf = sem(f"s{layer}_ST"), sem(f"s{layer}_jobgate_out"), sem(f"s{layer}_overflow")
    tmp = V.SIL.rearrange("p a b -> p (a b)")
    cnt, cnt2, of = tmp[:, 0:EGROUPS], tmp[:, EGROUPS:2 * EGROUPS], tmp[:, 2 * EGROUPS:2 * EGROUPS + 2]
    TURN_S = (7, T_BANK)
    COUNTS = 8

    def first_pe(pe):
        pe_gather(pe, M, 0, 0, s)
        pe_gather(pe, M, 0, 1, s)
        for j in range(EGROUPS):
            pe.wait_ge(s_rows, j + 1)
            for c in range(TC):
                mm = pe.matmul(M.ps[:, 7, j * EPG:(j + 1) * EPG], V.S[:, j, c], M.g4[:, c], start=(c == 0),
                               stop=(c == TC - 1))
        mm.then_inc(s_jg, 1)

    def turn_S(pe, half):
        for j in (2 * half, 2 * half + 1):
            for c in range(TC):
                mm = pe.transpose(M.ps[:, TURN_S[half], (j % 2) * SEQ + c * P:(j % 2) * SEQ + (c + 1) * P],
                                  V.S[:, j, c], M.ident[:])
        mm.then_inc(s_St, 1)

    def first_act(act):
        for half in range(2):
            act_take_gather(nc, act, M, 0, half, s)
        act.wait_ge(s_jg, 1)
        nc.scalar.copy(M.jgate[:, 0:EGROUPS], M.ps[:, 7, 0:16].rearrange("p (j e) -> p j e", j=EGROUPS)
                       ).then_inc(s_jge, 1)

    def take_turned_S(act, half):
        act.wait_ge(s_St, half + 1)
        nc.scalar.copy(V.ST[:, 2 * half:2 * half + 2], M.ps[:, TURN_S[half], :].rearrange("p (j t) -> p j t", j=2)
                       ).then_inc(s_ST, 1)

    def first_dve(dve):
        v = nc.vector
        for j in range(EGROUPS):
            one_hot_rows(v, M, V.S[:, j], j).then_inc(s_rows, 1)
        ln = Link(dve, s_ovf)
        ln(v.tensor_scalar(cnt, M.ps[:, 5, COUNTS:COUNTS + EGROUPS], float(P), None, ALU.is_gt))
        ln(v.tensor_tensor(cnt2, cnt, M.iota[:, 0:EGROUPS], ALU.mult))
        ln(v.tensor_reduce(of[:, 0:1], cnt, AX.X, ALU.add))
        ln(v.tensor_reduce(of[:, 1:2], cnt2, AX.X, ALU.add))
        ln(v.tensor_copy(M.ovf[:], of))
        for half in range(2):
            dve_take_gather(nc, dve, M, 0, half, s)
        dve.wait_ge(s_jge, 1)

    def ydst(j):
        return V.Y[:, j] if isinstance(j, int) else V.Y[:, bass.ds(j, 1)].rearrange("p o d -> p (o d)")

    with nc.Block() as block:
        @block.sync
        def _(sp):
            def after(j, first, end):
                for i in range(first, end):
                    st.wait_raw_free(sp, j, i)
                    if i + RAWS < JOB_CHUNKS:
                        st.load(sp, i, job_chunk(T, layer, j * EPG, i + RAWS))
                    elif j is not JL:
                        st.load(sp, i, job_chunk(T, layer, (j + 1) * EPG, i + RAWS - JOB_CHUNKS))
                    elif ahead:
                        k = i + RAWS - JOB_CHUNKS
                        nxt.load(sp, k, ahead[k])

            with sp.Fori(0, JL) as j:
                after(j, PARTS, JOB_CHUNKS)
                after(j + 1, 0, PARTS)
            after(JL, PARTS, JOB_CHUNKS)
            if out is not None:
                for c in range(TC):
                    sp.wait_ge(s.res, 2 * (c + 1))
                    store(sp, M, out, c)

        @block.tensor
        def _(pe):
            credits(pe, (s.turned, 2))
            first_pe(pe)
            with pe.Fori(0, JL) as j:
                pe_job(pe, M, V, j, s, st, True)

            def earlier_jobs():
                pe.wait_ge(s.y_out, 2 * JL + 2)
                pe.wait_ge(s_ST, 2)
                for i in range(2):
                    pe_scatter(pe, M, V, i, 0, JL, JL)

            pe.wait_ge(s_jge, 1)
            for half in range(2):
                turn_S(pe, half)
            pe_job(pe, M, V, JL, s, st, False, earlier_jobs)
            pe.wait_ge(s.gu, EXPERTS + 2)
            for i in range(2, 4):
                pe_scatter(pe, M, V, i, 0, JL, JL)
            pe.wait_ge(s.y_out, 2 * EGROUPS + 2)
            for i in range(4):
                pe_scatter(pe, M, V, i, JL, EGROUPS, JL).then_inc(s.scat, 1)

        @block.scalar
        def _(act):
            credits(act, (s.guT, 1))
            first_act(act)
            with act.Fori(0, JL) as j:
                act_job(nc, act, M, V, j, s, st, ydst, True)
            for half in range(2):
                take_turned_S(act, half)
            act_job(nc, act, M, V, JL, s, st, ydst, False)
            load_sqrt_table(nc, M)

        @block.vector
        def _(dve):
            credits(dve, (s.gu, 2), (s.y_out, 2), (s.pick, 1))
            first_dve(dve)
            with dve.Fori(0, JL) as j:
                dve_job(nc, dve, M, V, j, s, st, gate, ydst, True)
            dve_job(nc, dve, M, V, JL, s, st, gate, ydst, False)
            for i in range(4):
                dve.wait_ge(s.scat, i + 1)
                hs = M.h[:, i // 2, (i % 2) * 512:(i % 2 + 1) * 512]
                nc.vector.tensor_tensor(hs, hs, M.ps[:, SCATTER_BANKS[i], :], ALU.add).then_inc(s.res, 1)


def overflow_phase(nc, M, T, sem, layer, st, after, out=None):
    V = moe_views(M)
    t = f"o{layer}"
    s = MoeSems(sem, f"v{layer}")
    s_S, s_St, s_prep, s_ge = sem(f"{t}_S"), sem(f"{t}_ST"), sem(f"{t}_prep"), sem(f"{t}_gate")
    group_max = EGROUPS - 1

    def gate(j, e):
        return M.jgate[:, 4, e:e + 1]

    def ydst(j):
        return V.Y[:, 0]

    def when(eng, body):
        n = eng.value_load(M.ovf[0:1, 0:1], min_val=0, max_val=1)
        with eng.If(n > 0):
            body(eng)
        eng.end_ifs()

    with nc.Block() as block:
        @block.sync
        def _(sp):
            g = sp.value_load(M.ovf[0:1, 1:2], min_val=0, max_val=group_max)

            def body(sp):
                if after is not None:
                    after[0](sp)
                for i in range(RAWS):
                    st.load(sp, i, job_chunk(T, layer, g * EPG, i))
                for i in range(JOB_CHUNKS - RAWS):
                    st.wait_raw_free(sp, 0, i)
                    st.load(sp, i, job_chunk(T, layer, g * EPG, i + RAWS))
                if after is not None:
                    st.wait_raw_free(sp, 0, JOB_CHUNKS - 1)
                    after[1](sp)
                if out is not None:
                    sp.wait_ge(s.res, 4)
                    for c in range(TC):
                        sp.wait_ge(out[1], 16 * (TC + c))
                        store(sp, M, out, c)
                    sp.wait_ge(out[1], 16 * 2 * TC)

            when(sp, body)

        @block.tensor
        def _(pe):
            def body(pe):
                credits(pe, (s.turned, 2), (st.used, PARTS))
                pe.wait_ge(s_S, TC)
                for c in range(TC):
                    pe.transpose(M.ps[:, T_BANK, c * P:(c + 1) * P], V.S[:, 0, c], M.ident[:])
                for c in range(TC):
                    mm = pe.matmul(M.ps[:, 7, 0:EPG], V.S[:, 0, c], M.g4[:, c], start=(c == 0), stop=(c == TC - 1))
                mm.then_inc(s_St, 1)
                pe_gather(pe, M, 0, 0, s)
                pe_gather(pe, M, 0, 1, s)
                pe.wait_ge(s_prep, 2)
                pe_job(pe, M, V, 0, s, st, False)
                pe.wait_ge(s.gu, EPG + 2)
                pe.wait_ge(s.y_out, 4)
                for i in range(4):
                    pe.matmul(M.ps[:, i, :], V.ST[:, 0, (i // 2) * P:(i // 2 + 1) * P],
                              V.Y[:, 0, (i % 2) * 512:(i % 2 + 1) * 512], start=True, stop=True).then_inc(s.scat, 1)

            when(pe, body)

        @block.scalar
        def _(act):
            def body(act):
                credits(act, (s.guT, 1))
                act.wait_ge(s_St, 1)
                nc.scalar.copy(V.ST[:, 0], M.ps[:, T_BANK, 0:SEQ]).then_inc(s_prep, 1)
                nc.scalar.copy(M.jgate[:, 4], M.ps[:, 7, 0:EPG]).then_inc(s_prep, 1)
                for i in range(PARTS):
                    st.split_hi(act, 0, i)
                for half in range(2):
                    act_take_gather(nc, act, M, 0, half, s)
                act_job(nc, act, M, V, 0, s, st, ydst, False)

            when(act, body)

        @block.vector
        def _(dve):
            def body(dve):
                credits(dve, (s.gu, 2), (s.y_out, 2))
                nc.vector.tensor_scalar(M.stat[:, 0:TC], M.rank[:], float(-P), None, ALU.add).then_inc(s_ge, 1)
                dve.wait_ge(s_ge, 1)
                for c in range(TC):
                    nc.vector.tensor_scalar(V.S[:, 0, c], M.iota[:], M.stat[:, c:c + 1], None,
                                            ALU.is_equal).then_inc(s_S, 1)
                dve.wait_ge(s_S, TC)
                nc.vector.tensor_copy(M.pick[:], V.S[:, 0]).then_inc(s.pick, 1)
                for i in range(PARTS):
                    st.split_lo(dve, 0, i)
                for half in range(2):
                    dve_take_gather(nc, dve, M, 0, half, s)
                dve.wait_ge(s_prep, 2)
                dve_job(nc, dve, M, V, 0, s, st, gate, ydst, False)
                for i in range(4):
                    dve.wait_ge(s.scat, i + 1)
                    hs = M.h[:, i // 2, (i % 2) * 512:(i % 2 + 1) * 512]
                    nc.vector.tensor_tensor(hs, hs, M.ps[:, i, :], ALU.add).then_inc(s.res, 1)

            when(dve, body)



KV = 0
KCT = KT0 = 3072
QT = SQQ = BLK = 4096
Q = SC = 6144
PTC = 7168
X2 = GAIN2 = HROW = PTB = 8192
KT1 = 9216
VCBD = SQK = 10240
KCMPT, HIDK, HIDV, HIDVP, KCN, STATS = 11264, 11392, 11456, 11520, 12032, 12160
CST, SMALL = HIDK, STATS

KV_CHUNKS, Q_CHUNKS, PHI_CHUNKS = 6, 4, 2
LAST_SPLIT = KV_CHUNKS + Q_CHUNKS + PARTS


def attention_loads_after(sp, st, nxt, chunks, ahead, first, end):
    for i in range(first, end):
        st.wait_raw_free(sp, 0, i)
        k = i + RAWS
        if k < len(chunks):
            st.load(sp, k, chunks[k])
        else:
            nxt.load(sp, k - len(chunks), ahead[k - len(chunks)])


def head_squares(M):
    sums = M.at(STATS, 3, 48)[:, 0]
    return (M.at(SQK, 2, TC, 256), sums[:, 0:2 * TC * GROUPS], M.at(SQQ, TC, 2, 512),
            sums[:, 2 * TC * GROUPS:].rearrange("p (c a h) -> p c a h", c=TC, a=2))


def project_phase(nc, M, T, sem, st, nxt, chunks, ahead, gain):
    n = NormSems(sem, gain, "np")
    s_g2, s_tp2, s_gates = sem("gain2_in"), sem("turned2"), sem("gates_mm")
    s_ev2 = [sem("hnT2_hi"), sem("hnT2_lo")]
    s_out = [sem("proj_act"), sem("proj_dve")]
    s_sq, s_sum = sem("squares"), sem("head_sums")
    sqk, ksum, sqq, qsum = head_squares(M)
    s_kc, s_kc_ev, s_x2 = sem("kc_vc_turned"), [sem("kc_ev"), sem("vc_ev")], sem("x2_in")
    kcT = M.at(KCT, 2, 2, SEQ)
    x2 = M.at(X2, 2, GROUPS, SEQ)
    kv, kvh = M.at(KV, TC, 3, 512), M.at(KV, TC, 6, 256)
    q = M.at(Q, TC, 2, 512)
    dst = [(kv, b) for b in range(3)] + [(q, b) for b in range(2)]
    BANKS = [4, 6, 0, 6, 0]
    TURN2, GATES = 2, 4

    def turn2_bank(b):
        return M.ps[:, TURN2 + b, :].rearrange("p (k t) -> p k t", k=2)

    with nc.Block() as block:
        @block.sync
        def _(sp):
            sp.dma_start(M.at(GAIN2, D), T["b_norm"][0].partition_broadcast(P)).then_inc(s_g2, 16)
            attention_loads_after(sp, st, nxt, chunks, ahead, 0, KV_CHUNKS + 3)
            for i in range(2):
                sp.wait_ge(s_kc_ev[i], 1)
                for g2 in range(2):
                    for l2 in range(2):
                        dst = x2[DH * l2:DH * (l2 + 1)].rearrange("p i (a b) t -> p i a b t", b=2)[:, :, :, g2]
                        sp.dma_start(dst[:, i, :, 0:SEQ - l2], kcT[DH * g2:DH * (g2 + 1), i, :, l2:SEQ]
                                     ).then_inc(s_x2, 16)
            attention_loads_after(sp, st, nxt, chunks, ahead, KV_CHUNKS + 3, LAST_SPLIT)
            sp.wait_ge(s_x2, 16 * 8)

        @block.scalar
        def _(act):
            norm_act(nc, act, M, n)
            st.split_hi(act, 0, 0)
            norm_evac_act(nc, act, M, n)
            for i in range(1, PARTS):
                st.split_hi(act, 0, i)
            for i in range(KV_CHUNKS + Q_CHUNKS):
                if i % 2 == 1:
                    st.wait_used(act, 0, i)
                    x, b = dst[i // 2]
                    nc.scalar.copy(x[:, 0, b], M.ps[:, BANKS[i // 2], :]).then_inc(s_out[0], 1)
                if i == KV_CHUNKS - 1:
                    for b in range(4):
                        act.wait_ge(s_tp2, b + 1)
                        nc.scalar.copy(part(M.hnT[0], b), turn2_bank(b)).then_inc(s_ev2[0], 1)
                    act.wait_ge(s_kc, 1)
                    nc.scalar.copy(kcT[:, 0], bank_pair(M, 0)).then_inc(s_kc_ev[0], 1)
                st.split_hi(act, 0, i + PARTS)
                if i == KV_CHUNKS:
                    act.wait_ge(s_out[0], 3)
                    act.wait_ge(s_out[1], 3)
                    for x in range(2):
                        nc.scalar.activation(sqk[:, x], kv[:, :, x + 1, 0:256], ACT.Square).then_inc(s_sq, 1)
                if i == KV_CHUNKS + 1:
                    act.wait_ge(s_out[0], 4)
                    act.wait_ge(s_out[1], 4)
                    nc.scalar.activation(sqq[:, :, 0], q[:, :, 0], ACT.Square).then_inc(s_sq, 1)
            act.wait_ge(s_gates, 1)
            nc.scalar.activation(M.gates[:], M.ps[:, GATES, 0:TC * 3 * HEADS].rearrange("p (c n) -> p c n", c=TC),
                                 ACT.Sigmoid).then_inc(s_out[0], 1)

        @block.vector
        def _(dve):
            v = nc.vector
            norm_dve(nc, dve, M, n)
            st.split_lo(dve, 0, 0)
            norm_evac_dve(nc, dve, M, n)
            for i in range(1, PARTS):
                st.split_lo(dve, 0, i)
            dve.wait_ge(s_g2, 16)
            dve.wait_ge(n.tp, 4)
            for c in range(TC):
                v.scalar_tensor_tensor(M.hn[:, c, :], M.h[:, c, :], M.stat[:, 6 + c:7 + c], M.at(GAIN2, D),
                                       ALU.mult, ALU.mult).then_inc(n.hn, 1)
            for i in range(KV_CHUNKS + Q_CHUNKS):
                if i % 2 == 1:
                    st.wait_used(dve, 0, i)
                    x, b = dst[i // 2]
                    v.tensor_copy(x[:, 1, b], M.ps[:, BANKS[i // 2] + 1, :]).then_inc(s_out[1], 1)
                if i == KV_CHUNKS - 1:
                    for b in range(4):
                        dve.wait_ge(s_ev2[0], b + 1)
                        v.tensor_tensor(part(M.hnT[1], b), turn2_bank(b), part(M.hnT[0], b), ALU.subtract
                                        ).then_inc(s_ev2[1], 1)
                    dve.wait_ge(s_kc, 2)
                    v.tensor_copy(kcT[:, 1], bank_pair(M, 1)).then_inc(s_kc_ev[1], 1)
                st.split_lo(dve, 0, i + PARTS)
                if i == KV_CHUNKS + 1:
                    dve.wait_ge(s_sq, 2)
                    v.tensor_reduce(ksum, sqk.rearrange("p i c (g d) -> p (i c g) d", d=DH), AX.X, ALU.add
                                    ).then_inc(s_sum, 1)
                if i == KV_CHUNKS + 2:
                    dve.wait_ge(s_sq, 3)
                    v.tensor_reduce(qsum[:, :, 0], sqq[:, :, 0].rearrange("p c (h d) -> p c h d", d=DH), AX.X,
                                    ALU.add).then_inc(s_sum, 1)

        @block.tensor
        def _(pe):
            pe.sem_inc(st.used, PARTS)
            norm_pe(pe, M, n, 26)
            wait_hnT(pe, n)
            for b in range(5):
                if b >= 3:
                    for x in s_out:
                        pe.wait_ge(x, b - 1)
                if b == 3:
                    pe.wait_ge(n.hn, 2 * TC)
                    for x in range(4):
                        for kk in range(2):
                            for c in range(TC):
                                k = 2 * x + kk
                                mm = pe.transpose(M.ps[:, TURN2 + x, kk * SEQ + c * P:kk * SEQ + (c + 1) * P],
                                                  M.hn[:, c, k * P:(k + 1) * P], M.ident[:])
                        mm.then_inc(s_tp2, 1)
                    for x in s_out:
                        pe.wait_ge(x, b)
                    for i in range(2):
                        for a in range(2):
                            for c in range(TC):
                                mm = pe.transpose(M.ps[:, i, a * SEQ + c * P:a * SEQ + (c + 1) * P],
                                                  kvh[:, c, i, a * P:(a + 1) * P], M.ident[:])
                        mm.then_inc(s_kc, 1)
                    pe.wait_ge(s_ev2[1], 4)
                if b == 4:
                    for x in s_kc_ev:
                        pe.wait_ge(x, 1)
                for x in range(2):
                    w = st.parts(pe, 0, 2 * b + x, 4)
                    for c in range(TC):
                        for k in range(4):
                            mm = mm3(pe, M.ps[:, BANKS[b] + c, :],
                                     [t[:, 4 * x + k, c * P:(c + 1) * P] for t in M.hnT], [t[:, k] for t in w],
                                     x == 0 and k == 0, x == 1 and k == 3)
                    mm.then_inc(st.used, 1)
            for c in range(TC):
                for k in range(KC):
                    mm = mm3(pe, M.ps[:, GATES, c * 48:(c + 1) * 48], [t[:, k, c * P:(c + 1) * P] for t in M.hnT],
                             [t[:, k, :] for t in M.wg], k == 0, k == KC - 1)
            mm.then_inc(s_gates, 1)


def prep_phase(nc, M, T, sem, st, nxt, chunks, ahead, next_gain):
    kv = M.at(KV, TC, 6, 256)
    q = M.at(Q, TC, D)
    qn = M.hn[:].rearrange("p c (a n) -> p c a n", a=2)
    _, _, sqq, qsum = head_squares(M)
    sts = M.at(STATS, 3, 48)
    x2 = M.at(X2, 2, GROUPS, SEQ)
    blk = M.at(BLK, 2, 16, GROUPS * NCMP)
    B60 = 16 * GROUPS * NCMP
    blk_parts = [[t[:].rearrange("p k t -> p (k t)")[:, 0:B60].rearrange("p (j n) -> p j n", j=16) for t in M.xg],
                 [t[:].rearrange("p a k t -> p (a k t)")[:, 0:B60].rearrange("p (j n) -> p j n", j=16)
                  for t in M.gut]]
    kT = [M.at(KT0, 2, 2, SEQ), M.at(KT1, 2, 2, SEQ)]
    qT = M.at(QT, KC, SEQ)
    hidk, hidv = M.at(HIDK, 60), M.at(HIDV, GROUPS, NCMP)
    hidvp = M.at(HIDVP, GROUPS, HPG, CPAD)
    kcn, kcmpT = M.at(KCN, 2, DH), M.at(KCMPT, GROUPS, CPAD)
    vcbd = M.at(VCBD, GROUPS, HPG, DH)
    hrow = M.at(HROW, 2, HID)
    first_phi = KV_CHUNKS + Q_CHUNKS
    names = ("kn_mm", "qn_mm", "blk", "hid_mm", "hidk", "hidv", "hidvp",
             "kc_mm", "kc_sq", "kc_ms", "kc_sd", "kcn", "kcT2_mm", "vc_mm", "sq", "ssum", "std", "kn", "qn",
             "kT", "qT_a", "qT_d", "pads", "ch", "end", "colq", "blk_hi", "blk_lo", "hrow")
    S = {k: sem("p_" + k) for k in names}

    with nc.Block() as block:
        @block.sync
        def _(sp):
            sp.dma_start(M.gain[:], T["ffn_norm"][1].partition_broadcast(P)).then_inc(next_gain, 16)
            attention_loads_after(sp, st, nxt, chunks, ahead, LAST_SPLIT, LAST_SPLIT + PHI_CHUNKS)

        @block.gpsimd
        def _(pool):
            fill = Link(pool, S["pads"])
            fill(nc.gpsimd.memset(M.at(HIDVP, 512), 0.0))
            fill(nc.gpsimd.memset(M.at(KCMPT, 128), 0.0))
            fill(nc.gpsimd.memset(M.at(VCBD, 1024), 0.0))
            fill(nc.gpsimd.memset(kT[0][DH:P], 0.0))
            pool.wait_ge(S["blk"], 4)
            fill(nc.gpsimd.memset(kT[1][0:DH], 0.0))

        @block.tensor
        def _(pe):
            B = M.ps

            keep_clock(pe, M, 5, 17)
            for i in range(2):
                pe.wait_ge(S["blk_lo"], i + 1)
                phi = st.parts(pe, 0, first_phi + i, 16)
                for j in range(16):
                    mm = mm3(pe, B[0:60, i, 0:HID], [t[:, j] for t in blk_parts[i]], [t[:, j] for t in phi], j == 0,
                             j == 15)
                mm.then_inc(st.used, 1)
            pe.wait_ge(S["kn"], 2)
            for i in range(2):
                for a in range(2):
                    for c in range(TC):
                        mm = pe.transpose(B[:, 2 + i, a * SEQ + c * P:a * SEQ + (c + 1) * P],
                                          kv[:, c, 2 + 2 * i, a * P:(a + 1) * P], M.ident[:])
                mm.then_inc(S["kn_mm"], 1)
            for i in range(2):
                pe.wait_ge(S["hrow"], i + 1)
                pe.transpose(B[:, i, HID:HID + 60], hrow[0:60, i], M.ident[0:60, 0:60]).then_inc(S["hid_mm"], 1)
            pe.wait_ge(S["qn"], 4)
            for b in range(4):
                for kk in range(2):
                    for c in range(TC):
                        a, r = (2 * b + kk) // HPG, (2 * b + kk) % HPG
                        mm = pe.transpose(B[:, 4 + b, kk * SEQ + c * P:kk * SEQ + (c + 1) * P],
                                          qn[:, c, a, r * P:(r + 1) * P], M.ident[:])
                mm.then_inc(S["qn_mm"], 1)
            pe.wait_ge(S["kT"], 4)
            pe.wait_ge(S["hidk"], 1)
            pe.matmul(B[0:60, 2, 0:DH], hidk, M.phi2[:, 0], start=True, stop=True).then_inc(S["kc_mm"], 1)
            pe.wait_ge(S["hidvp"], HPG)
            for g in range(GROUPS):
                mm = pe.matmul(B[:, 3, g * DH:(g + 1) * DH], hidvp[:, g].rearrange("p r n -> p (r n)"),
                               M.phi2[:, 1], start=True, stop=True)
            mm.then_inc(S["vc_mm"], 1)
            pe.wait_ge(S["qT_a"], 2)
            pe.wait_ge(S["qT_d"], 2)
            keep_clock(pe, M, 5, 6)
            pe.wait_ge(S["kcn"], 2)
            pe.transpose(B[:, 0, 0:60], kcn[0:60].rearrange("p a d -> p (a d)"), M.ident[0:60, 0:60]
                         ).then_inc(S["kcT2_mm"], 1)
            keep_clock(pe, M, 5, 12)

        @block.scalar
        def _(act):
            a = nc.scalar
            a.activation(sqq[:, :, 1], q[:, :, 512:D], ACT.Square).then_inc(S["sq"], 1)
            act.wait_ge(S["ssum"], 1)
            a.activation(sts[:, 1], sts[:, 0], ACT.Sqrt).then_inc(S["std"], 1)
            for i in range(2):
                act.wait_ge(S["blk"], 2 * (i + 1))
                a.copy(blk_parts[i][0], blk[:, i]).then_inc(S["blk_hi"], 1)
            st.split_hi(act, 0, LAST_SPLIT)
            for i in range(2):
                st.wait_used(act, 0, first_phi + i)
                a.copy(hrow[0:60, i], M.ps[0:60, i, 0:HID]).then_inc(S["hrow"], 1)
            for i in range(2):
                act.wait_ge(S["kn_mm"], i + 1)
                a.activation(kT[0][0:DH, i], bank_pair(M, 2 + i)[0:DH], ACT.Copy, scale=M.cols2[0:DH, 33 + i:34 + i]
                             ).then_inc(S["kT"], 1)
            act.wait_ge(S["hid_mm"], 1)
            a.activation(hidk, M.ps[:, 0, HID:HID + 60], ACT.Gelu_apprx_tanh, bias=M.cols2[:, 36:37]).then_inc(S["hidk"], 1)
            act.wait_ge(S["hid_mm"], 2)
            a.activation(hidv.rearrange("p g n -> p (g n)"), M.ps[:, 1, HID:HID + 60], ACT.Gelu_apprx_tanh,
                         bias=M.cols2[:, 37:38]).then_inc(S["hidv"], 1)
            act.wait_ge(S["colq"], 1)
            act.wait_ge(S["blk_lo"], 2)
            for b in (0, 2):
                act.wait_ge(S["qn_mm"], b + 1)
                a.activation(part(qT, b), bank_pair(M, 4 + b), ACT.Copy, scale=M.stat[:, 0:1]
                             ).then_inc(S["qT_a"], 1)
            act.wait_ge(S["kc_mm"], 1)
            act.wait_ge(S["kn_mm"], 2)
            a.activation(kcn[0:60, 0], M.ps[0:60, 2, 0:DH], ACT.Square, accum_out=M.stat[0:60, 1:2]
                         ).then_inc(S["kc_sq"], 1)
            act.wait_ge(S["kc_ms"], 1)
            a.activation(M.stat[0:60, 3:4], M.stat[0:60, 2:3], ACT.Sqrt).then_inc(S["kc_sd"], 1)
            st.split_hi(act, 0, LAST_SPLIT + 1)

        @block.vector
        def _(dve):
            v = nc.vector
            ln = Link(dve, S["ch"])
            v.tensor_scalar(M.stat[:, 0:1], M.cols2[:, 35:36], DH ** -0.5, None, ALU.mult).then_inc(S["colq"], 1)
            dve.wait_ge(S["sq"], 1)
            ln(v.tensor_reduce(qsum[:, :, 1], sqq[:, :, 1].rearrange("p c (h d) -> p c h d", d=DH), AX.X, ALU.add))
            v.tensor_scalar(sts[:, 0], sts[:, 0], 1.0 / DH, EPS, ALU.mult, ALU.add).then_inc(S["ssum"], 1)
            for i in range(2):
                for hj in range(2):
                    win = x2[:, i, :, 16 * hj:16 * hj + 240].rearrange("p g (n j x) -> p j g n x", j=8, x=2)
                    for g in range(GROUPS):
                        pe_col = M.cols2[:, 16 * i + 8 * hj:16 * i + 8 * hj + 8]
                        o = v.tensor_tensor(blk[:, i, 8 * hj:8 * hj + 8, g * NCMP:(g + 1) * NCMP], win[:, :, g, :, 0],
                                            pe_col.unsqueeze(2).to_broadcast([P, 8, NCMP]), ALU.add)
                    o.then_inc(S["blk"], 1)
            for i in range(2):
                dve.wait_ge(S["blk_hi"], i + 1)
                v.tensor_tensor(blk_parts[i][1], blk[:, i], blk_parts[i][0], ALU.subtract).then_inc(S["blk_lo"], 1)
            dve.wait_ge(S["std"], 1)
            ln(v.reciprocal(sts[:, 2], sts[:, 1]))
            for i in range(2):
                r = sts[:, 2, 8 * i:8 * i + 8].rearrange("p (c g) -> p c g", c=TC)
                k_i = kv[:, :, 2 + 2 * i].rearrange("p c (g d) -> p c g d", d=DH)
                v.tensor_tensor(k_i, k_i,
                                r.unsqueeze(3).to_broadcast([P, TC, GROUPS, DH]), ALU.mult).then_inc(S["kn"], 1)
            for c in range(TC):
                for pr in range(2):
                    r = sts[:, 2, 16 + 16 * c + 8 * pr:24 + 16 * c + 8 * pr].rearrange("p (g r) -> p g r", g=2)
                    v.tensor_tensor(qn[:, c, pr].rearrange("p (r g d) -> p g r d", g=2, d=DH),
                                    q[:, c, pr * 512:(pr + 1) * 512].rearrange("p (g r d) -> p g r d", g=2, d=DH),
                                    r.unsqueeze(3).to_broadcast([P, 2, HPG, DH]), ALU.mult).then_inc(S["qn"], 1)
            st.split_lo(dve, 0, LAST_SPLIT)
            dve.wait_ge(S["kn_mm"], 2)
            dve.wait_ge(S["blk"], 4)
            for i in range(2):
                v.tensor_scalar(kT[1][DH:P, i], bank_pair(M, 2 + i)[DH:P], M.cols2[DH:P, 33 + i:34 + i], None,
                                ALU.mult).then_inc(S["kT"], 1)
            dve.wait_ge(S["pads"], 5)
            dve.wait_ge(S["hidv"], 1)
            for r in range(HPG):
                v.tensor_copy(hidvp[:, :, r, 0:NCMP], hidv).then_inc(S["hidvp"], 1)
            for b in (1, 3):
                dve.wait_ge(S["qn_mm"], b + 1)
                v.tensor_scalar(part(qT, b), bank_pair(M, 4 + b), M.stat[:, 0:1], None, ALU.mult
                                ).then_inc(S["qT_d"], 1)
            dve.wait_ge(S["kc_sq"], 1)
            v.tensor_scalar(M.stat[0:60, 2:3], M.stat[0:60, 1:2], 1.0 / DH, EPS, ALU.mult, ALU.add
                            ).then_inc(S["kc_ms"], 1)
            dve.wait_ge(S["vc_mm"], 1)
            for r in range(HPG):
                rs = slice(CPAD * r, CPAD * (r + 1))
                v.tensor_copy(vcbd[rs, :, r], M.ps[rs, 3, 0:256].rearrange("p (g d) -> p g d", d=DH)
                              ).then_inc(S["end"], 1)
            dve.wait_ge(S["kc_sd"], 1)
            ln(v.reciprocal(M.stat[0:60, 4:5], M.stat[0:60, 3:4]))
            for x in range(2):
                v.tensor_scalar(kcn[0:60, x], M.ps[0:60, 2, 0:DH], M.stat[0:60, 4:5], None, ALU.mult
                                ).then_inc(S["kcn"], 1)
            dve.wait_ge(S["kcT2_mm"], 1)
            for g2 in range(2):
                hs = slice(DH * g2, DH * (g2 + 1))
                v.tensor_scalar(kcmpT[hs].rearrange("p (a b) n -> p a b n", b=2)[:, :, g2, 0:NCMP],
                                M.ps[hs, 0, 0:60].rearrange("p (a b n) -> p a b n", a=2, b=2)[:, :, g2],
                                M.cols2[hs, 32:33], None, ALU.mult).then_inc(S["end"], 1)
            st.split_lo(dve, 0, LAST_SPLIT + 1)


def attend_phase(nc, M, T, sem, st, nxt, chunks, ahead):
    kv = M.at(KV, TC, 6, 256)
    qT, kT = M.at(QT, KC, SEQ), [M.at(KT0, 2, 2, SEQ), M.at(KT1, 2, 2, SEQ)]
    kcmpT, vcbd = M.at(KCMPT, GROUPS, CPAD), M.at(VCBD, GROUPS, HPG * DH)
    sc = M.at(SC, TC, HEADS, CPAD)
    ptc = M.at(PTC, TC, GROUPS, P)
    hnf = M.hn[:].rearrange("p c d -> p (c d)")
    pb = hnf[:, 0:1536].rearrange("p (n b k) -> p n b k", n=3, b=2)
    ptb = M.at(PTB, 2, 4, P)
    o, oT = M.hn, M.hnT
    cst = M.at(CST, 8, 32)
    nm, sm, gr = (M.at(SMALL + 64 * i, 32, 2) for i in range(3))
    N = TC * HEADS
    names = ("c_mm", "c_ch", "c_exp", "c_p", "c_tp", "c_ev", "s_mm", "max", "exp", "scaled", "t_mm", "pt", "pv",
             "o_ev", "o_tp", "oT_a", "oT_d", "out", "sm_ch", "wl")
    S = {k: sem("a_" + k) for k in names}
    W0 = KV_CHUNKS + Q_CHUNKS + PHI_CHUNKS
    SCORE, TURN = 4, 6
    COMPRESSED = 6

    def chunk_of(n):
        return TC - 1 - n // HEADS

    def where(h):
        g, r = h // HPG, h % HPG
        return g, (g // 2) * HPG + r, g // 2

    with nc.Block() as block:
        @block.sync
        def _(sp):
            attention_loads_after(sp, st, nxt, chunks, ahead, LAST_SPLIT + PHI_CHUNKS, len(chunks))

        @block.tensor
        def _(pe):
            B = M.ps
            for c in range(TC):
                for pair in range(KC):
                    a = pair // HPG
                    mm = pe.matmul(B[:, TURN + c, pair * 2 * CPAD:(pair + 1) * 2 * CPAD],
                                   qT[:, pair, c * P:(c + 1) * P],
                                   kcmpT[:, 2 * a:2 * a + 2].rearrange("p g n -> p (g n)"), start=True, stop=True)
                mm.then_inc(S["c_mm"], 1)

            def scores(n):
                c, h = chunk_of(n), n % HEADS
                g, pair, a = where(h)
                nk = P * (c + 1)
                if n >= 2:
                    pe.wait_ge(S["exp"], 2 * (n - 1))
                bank = B[:, SCORE + n % 2, :].rearrange("p (b k) -> p b k", b=2)
                pe.matmul(bank[:, :, 0:nk], qT[:, pair, c * P:(c + 1) * P], kT[g % 2][:, :, a, 0:nk], start=True,
                          stop=False)
                pe.matmul(bank[:, :, nk - P:nk], M.identb[:], M.causal[:].unsqueeze(1).to_broadcast([P, 2, P]),
                          start=False, stop=True).then_inc(S["s_mm"], 1)

            def turn(n):
                c = chunk_of(n)
                pe.wait_ge(S["scaled"], 2 * (n + 1))
                if n >= 2:
                    pe.wait_ge(S["pt"], n - 1)
                else:
                    pe.wait_ge(S["c_ch"], 4)
                if n > COMPRESSED:
                    pe.wait_ge(S["c_ev"], TC)
                for kc in range(c + 1):
                    for b in range(2):
                        x = 2 * kc + b
                        mm = pe.transpose(B[:, TURN + n % 2, x * P:(x + 1) * P],
                                          pb[:, n % 3, b, kc * P:(kc + 1) * P], M.ident[:])
                mm.then_inc(S["t_mm"], 1)

            def values(n):
                c, h = chunk_of(n), n % HEADS
                pe.wait_ge(S["pt"], n + 1)
                for kc in range(c + 1):
                    for b in range(2):
                        mm = pe.matmul(B[:, 2 * c + h // 8, (h % 8) * DH:(h % 8 + 1) * DH], ptb[:, n % 2, 2 * kc + b],
                                       kv[:, kc, 3 + 2 * b, (h // HPG) * DH:(h // HPG + 1) * DH],
                                       start=(h % 8 == 0 and kc == 0 and b == 0), stop=False, skip_group_check=True)
                mm.then_inc(S["pv"], 1)

            for n in range(N + 3):
                if n < N:
                    scores(n)
                if 2 <= n < N + 2:
                    turn(n - 2)
                if n >= 3:
                    values(n - 3)
                if n == COMPRESSED + 2:
                    pe.wait_ge(S["c_p"], TC)
                    pe.wait_ge(S["pt"], COMPRESSED + 1)
                    for c in range(TC):
                        for g in range(GROUPS):
                            mm = pe.transpose(B[:, TURN + c, g * P:(g + 1) * P], sc[:, c, g * HPG:(g + 1) * HPG
                                              ].rearrange("p r n -> p (r n)"), M.ident[:])
                        mm.then_inc(S["c_tp"], 1)
            for c in range(TC):
                for g in range(GROUPS):
                    mm = pe.matmul(B[:, 2 * c + g // 2, (g % 2) * 256:(g % 2 + 1) * 256], ptc[:, c, g], vcbd[:, g],
                                   start=False, stop=(g % 2 == 1), skip_group_check=True)
            mm.then_inc(S["pv"], 1)
            pe.wait_ge(S["o_ev"], 4)
            for b in range(4):
                turn_pe(pe, M, b, o).then_inc(S["o_tp"], 1)
            pe.wait_ge(S["oT_d"], 4)
            for p in range(KC // 2):
                w = st.parts(pe, 0, W0 + p, 2)
                if p == KC // 2 - 1:
                    out_chunk(pe, M, oT, w, p, 4, S["out"])
                else:
                    out_chunk(pe, M, oT, w, p, 4).then_inc(st.used, 1)

        @block.scalar
        def _(act):
            a = nc.scalar
            for n in range(N + 2):
                if n < N:
                    nk = P * (chunk_of(n) + 1)
                    act.wait_ge(S["max"], n + 1)
                    if n >= 3:
                        act.wait_ge(S["t_mm"], n - 2)
                    for b in range(2):
                        a.activation(pb[:, n % 3, b, 0:nk], M.ps[:, SCORE + n % 2, b * SEQ:b * SEQ + nk], ACT.Exp,
                                     bias=nm[:, n, b:b + 1], accum_out=sm[:, n, b:b + 1]).then_inc(S["exp"], 1)
                if n == 4:
                    act.wait_ge(S["c_ch"], 7)
                    for c in range(TC):
                        a.activation(sc[:, c], sc[:, c], ACT.Exp).then_inc(S["c_exp"], 1)
                if n >= 2:
                    m = n - 2
                    blocks = 2 * (chunk_of(m) + 1)
                    act.wait_ge(S["t_mm"], m + 1)
                    if m >= 2:
                        act.wait_ge(S["pv"], m - 1)
                    a.copy(ptb[:, m % 2, 0:blocks], M.ps[:, TURN + m % 2, 0:blocks * P].rearrange(
                        "p (x q) -> p x q", q=P)).then_inc(S["pt"], 1)
                if n == COMPRESSED + 2:
                    for c in range(TC):
                        act.wait_ge(S["c_tp"], c + 1)
                        a.copy(ptc[:, c], M.ps[:, TURN + c, :].rearrange("p (g q) -> p g q", g=GROUPS)
                               ).then_inc(S["c_ev"], 1)
            act.wait_ge(S["pv"], N + 1)
            for c in range(TC):
                a.copy(o[:, c, 0:512], M.ps[:, 2 * c, :]).then_inc(S["o_ev"], 1)
            for b in range(4):
                act.wait_ge(S["o_tp"], b + 1)
                a.copy(part(oT[0], b), bank_pair(M, b)).then_inc(S["oT_a"], 1)
            st.split_hi(act, 0, len(chunks) - 1)
            load_sqrt_table(nc, M)

        @block.vector
        def _(dve):
            v = nc.vector
            ln = Link(dve, S["c_ch"])
            ch2 = Link(dve, S["sm_ch"])
            scf = sc.rearrange("p c h n -> p (c h) n")

            def highest(n):
                nk = P * (chunk_of(n) + 1)
                dve.wait_ge(S["s_mm"], n + 1)
                v.tensor_reduce(nm[:, n], M.ps[:, SCORE + n % 2, :].rearrange("p (b k) -> p b k", b=2)[:, :, 0:nk],
                                AX.X, ALU.max, negate=True).then_inc(S["max"], 1)

            def scale(n):
                c, h = chunk_of(n), n % HEADS
                nk = P * (c + 1)
                dve.wait_ge(S["exp"], 2 * (n + 1))
                ch2(v.reciprocal(gr[:, n], sm[:, n]))
                ch2(v.tensor_tensor(gr[:, n], gr[:, n], M.gates[:, c, 3 * h + 1:3 * h + 3], ALU.mult))
                for b in range(2):
                    v.tensor_scalar(pb[:, n % 3, b, 0:nk], pb[:, n % 3, b, 0:nk], gr[:, n, b:b + 1], None, ALU.mult
                                    ).then_inc(S["scaled"], 1)

            def compressed_scores():
                for c in range(TC):
                    dve.wait_ge(S["c_mm"], c + 1)
                    for g2 in range(2):
                        ln(v.tensor_tensor(sc[:, c].rearrange("p (a b r) n -> p b a r n", a=2, b=2)[:, g2],
                                           M.ps[:, TURN + c, :].rearrange("p (a r b n) -> p b a r n", a=2, r=HPG, b=2
                                                                          )[:, g2],
                                           M.cmask[:, c].unsqueeze(1).unsqueeze(1).to_broadcast([P, 2, HPG, CPAD]),
                                           ALU.add))

            def compressed_gates():
                ch2(v.reciprocal(cst[:, 2], cst[:, 1]))
                for c in range(TC):
                    cs = slice(16 * c, 16 * c + 16)
                    g0 = M.gates[:, c].rearrange("p (h b) -> p h b", b=3)[:, :, 0]
                    ch2(v.scalar_tensor_tensor(cst[:, 3, cs], cst[:, 2, cs], M.cvalid[:, c:c + 1], g0, ALU.mult,
                                               ALU.mult))
                    v.tensor_tensor(sc[:, c], sc[:, c], cst[:, 3, cs].unsqueeze(2).to_broadcast([P, HEADS, CPAD]),
                                    ALU.mult).then_inc(S["c_p"], 1)

            compressed_scores()
            for n in range(N):
                highest(n)
                if n >= 1:
                    scale(n - 1)
                if n == 2:
                    ln(v.tensor_reduce(cst[:, 0], scf, AX.X, ALU.max, negate=True))
                if n == 3:
                    for c in range(TC):
                        ln(v.tensor_tensor(sc[:, c], sc[:, c], cst[:, 0, 16 * c:16 * c + 16].unsqueeze(2
                           ).to_broadcast([P, HEADS, CPAD]), ALU.add))
                if n == 5:
                    dve.wait_ge(S["c_exp"], TC)
                    ch2(v.tensor_reduce(cst[:, 1], scf, AX.X, ALU.add))
                if n == 6:
                    compressed_gates()
            scale(N - 1)
            dve.wait_ge(S["pv"], N + 1)
            for c in range(TC):
                v.tensor_copy(o[:, c, 512:1024], M.ps[:, 2 * c + 1, :]).then_inc(S["o_ev"], 1)
            for b in range(4):
                dve.wait_ge(S["oT_a"], b + 1)
                v.tensor_tensor(part(oT[1], b), bank_pair(M, b), part(oT[0], b), ALU.subtract
                                ).then_inc(S["oT_d"], 1)
            st.split_lo(dve, 0, len(chunks) - 1)
            for i in range(4):
                dve.wait_ge(S["out"], i + 1)
                hs = M.h[:, i // 2, (i % 2) * 512:(i % 2 + 1) * 512]
                v.tensor_tensor(hs, hs, M.ps[:, 4 + i, :], ALU.add).then_inc(S["wl"], 1)


def build(nc, T, out):
    with ExitStack() as ctx:
        sem = Sems(nc, ctx)
        M = Mem(nc, ctx)
        s_conv = Stream(nc, M, sem, "wconv", 0)
        s_moe0, s_ovf0 = Stream(nc, M, sem, "wmoe0", 0), Stream(nc, M, sem, "wovf0", 0)
        s_att = Stream(nc, M, sem, "watt", 0)
        att = attention_chunks(T)
        s_moe1, s_ovf1 = Stream(nc, M, sem, "wmoe1", len(att) % RAWS), Stream(nc, M, sem, "wovf1", 0)
        moe1_first = [job_chunk(T, 1, 0, i) for i in range(RAWS)]
        gains = [sem(f"gain_in{i}") for i in range(4)]
        again = sem("reloaded")
        s_end = sem("h_out")

        def phase(f, *args):
            with ExitStack() as c:
                own = Sems(nc, c)
                f(nc, M, T, own, *args)
                own.clear()

        def wait_loaded(sp):
            for x in s_att.landed:
                sp.wait_ge(x, 16)

        def load_again(sp):
            for i in range(RAWS):
                dst = M.raw[:, i, :].rearrange("p (k f) -> p k f", k=att[i].shape[1])
                sp.dma_start(dst, att[i]).then_inc(again, 16)
            sp.wait_ge(again, 16 * RAWS)

        phase(conv_phase, s_conv, s_moe0, gains)
        phase(route_phase, 0, s_moe0, gains[1], T["kv_norm"], gains[2])
        phase(jobs_phase, 0, s_moe0, s_att, att[:RAWS])
        phase(overflow_phase, 0, s_ovf0, (wait_loaded, load_again))
        phase(project_phase, s_att, s_moe1, att, moe1_first, gains[2])
        phase(prep_phase, s_att, s_moe1, att, moe1_first, gains[3])
        phase(attend_phase, s_att, s_moe1, att, moe1_first)
        phase(route_phase, 1, s_moe1, gains[3], None, None)
        phase(jobs_phase, 1, s_moe1, None, [], (out, s_end))
        phase(overflow_phase, 1, s_ovf1, None, (out, s_end))
        with nc.Block() as block:
            @block.sync
            def _(sp):
                sp.wait_ge(s_end, 16 * TC)


NAMES = ["x", "a_norm", "a_w_in", "a_dw", "a_dw_bias", "a_conv_norm", "a_w_out", "kv_norm", "w_kv", "cmp_pe",
         "phi_w1", "phi_b1", "phi_w2", "k_norm", "b_norm", "b_w_in", "b_q_norm", "b_w_out", "ffn_norm",
         "router_w", "router_bias", "moe_w1", "moe_w3", "moe_w2"]


def kernel(**inputs):
    import numpy as _np
    import concourse.bacc as _bacc
    from concourse import mybir as _mybir
    from concourse.bass_utils import run_bass_kernel_spmd as _run

    nc = _bacc.Bacc("TRN2", target_bir_lowering=False, num_devices=1)
    arrays, aps = {}, {}
    for name in NAMES:
        a = _np.ascontiguousarray(inputs[name])
        arrays[f"in_{name}"] = a
        aps[name] = nc.dram_tensor(f"in_{name}", a.shape, _mybir.dt.from_np(a.dtype), kind="ExternalInput").ap()
    out = nc.dram_tensor("out", inputs["x"].shape, _mybir.dt.float32, kind="ExternalOutput").ap()
    build(nc, aps, out)
    r = _run(nc, [arrays], core_ids=[0])
    return r.results[0]["out"]
```
